# Optimizing a Trainium2 kernel written in Bass

```python
import math
import jax, jax.numpy as jnp
from jax import lax
import numpy as np

D_MODEL = 1024
BATCH = 1
SEQ = 512
DEPTH = 1

GLA_HEADS = 4
GLA_DK = D_MODEL // 2
GLA_DV = D_MODEL
GLA_GATE_RANK = 16
GLA_TAU = 16.0
GLA_CHUNK = 64
DSA_HEADS = 8
DSA_HEAD_DIM = 128
DSA_LATENT = 256
IDX_HEADS = 8
IDX_DIM = 64
DSA_TOPK = 256
Q_BLOCK = 128
PEER_HEADS = 8
PEER_NKEYS = 128
PEER_NEXPERTS = PEER_NKEYS * PEER_NKEYS
PEER_DKEY = 256
PEER_TOPK = 16
PEER_TOKEN_BLOCK = 128
NORM_EPS = 1e-6

IN_SIZES = (GLA_DK, GLA_DK, GLA_DV, GLA_DV, GLA_GATE_RANK,
            DSA_HEADS * DSA_HEAD_DIM, DSA_LATENT, IDX_HEADS * IDX_DIM, IDX_DIM, IDX_HEADS,
            D_MODEL, D_MODEL)
IN_TOTAL = sum(IN_SIZES)


def _rmsnorm(x, g):
    x32 = x.astype(jnp.float32)
    y = x32 * lax.rsqrt(jnp.mean(x32 * x32, axis=-1, keepdims=True) + NORM_EPS)
    return (y * g.astype(jnp.float32)).astype(x.dtype)

def _alibi_slopes(n_heads):
    return jnp.exp2(-8.0 * jnp.arange(1, n_heads + 1, dtype=jnp.float32) / n_heads)

def _gla_chunked(q, k, v, log_alpha):
    B, H, S, dk = q.shape
    dv = v.shape[-1]
    C = GLA_CHUNK
    n = S // C
    q, k, v, la = [t.astype(jnp.float32).reshape(B, H, n, C, t.shape[-1]) for t in (q, k, v, log_alpha)]
    b = jnp.cumsum(la, axis=3)
    b_last = b[:, :, :, -1:, :]
    q_dec = q * jnp.exp(b)
    k_inv = k * jnp.exp(-b)
    k_end = k * jnp.exp(b_last - b)
    causal = jnp.tril(jnp.ones((C, C), dtype=bool))
    attn = jnp.where(causal, jnp.einsum('bhnid,bhnjd->bhnij', q_dec, k_inv), 0.0)
    o_intra = jnp.einsum('bhnij,bhnjv->bhniv', attn, v)

    def step(state, inp):
        q_c, k_c, v_c, decay_c = inp
        o_c = jnp.einsum('bhid,bhdv->bhiv', q_c, state)
        state = decay_c[..., None] * state + jnp.einsum('bhjd,bhjv->bhdv', k_c, v_c)
        return state, o_c

    xs = (jnp.moveaxis(q_dec, 2, 0), jnp.moveaxis(k_end, 2, 0), jnp.moveaxis(v, 2, 0),
          jnp.moveaxis(jnp.exp(b_last[:, :, :, 0, :]), 2, 0))
    state0 = jnp.zeros((B, H, dk, dv), jnp.float32)
    _, o_inter = lax.scan(step, state0, xs)
    o = o_intra + jnp.moveaxis(o_inter, 0, 2)
    return o.reshape(B, H, S, dv)

def _gla_branch(q, k, v, r, g_low, w_gate_up, b_gate, norm_g):
    B, S, _ = q.shape
    dkh = GLA_DK // GLA_HEADS
    dvh = GLA_DV // GLA_HEADS
    gate_logit = (g_low @ w_gate_up + b_gate).astype(jnp.float32)
    log_alpha = jax.nn.log_sigmoid(gate_logit) / GLA_TAU

    def heads(t, d):
        return t.reshape(B, S, GLA_HEADS, d).transpose(0, 2, 1, 3)

    o = _gla_chunked(heads(q, dkh) * (dkh ** -0.5), heads(k, dkh), heads(v, dvh), heads(log_alpha, dkh))
    o = o.transpose(0, 2, 1, 3)
    o = _rmsnorm(o, norm_g.reshape(GLA_HEADS, dvh)).reshape(B, S, GLA_DV)
    return o.astype(r.dtype) * jax.nn.silu(r)

def _dsa_branch(q, kv_raw, iq, ik, iw, kv_norm_g, w_uk, w_uv):
    B, S, _ = q.shape
    n_blocks = S // Q_BLOCK
    k_sel = min(DSA_TOPK, S // 4)
    c_kv = _rmsnorm(kv_raw, kv_norm_g)
    slopes = _alibi_slopes(DSA_HEADS)
    key_pos = jnp.arange(S, dtype=jnp.int32)

    def to_blocks(t):
        return t.reshape((B, n_blocks, Q_BLOCK) + t.shape[2:]).swapaxes(0, 1)

    q_b = to_blocks(q.reshape(B, S, DSA_HEADS, DSA_HEAD_DIM))
    iq_b = to_blocks(iq.reshape(B, S, IDX_HEADS, IDX_DIM))
    iw_b = to_blocks(iw)

    def block(inp):
        qb, iqb, iwb, blk = inp
        t = blk * Q_BLOCK + jnp.arange(Q_BLOCK, dtype=jnp.int32)
        rel = jax.nn.relu(jnp.einsum('bqhd,bsd->bqhs', iqb, ik).astype(jnp.float32) * (IDX_DIM ** -0.5))
        score = jnp.einsum('bqh,bqhs->bqs', iwb.astype(jnp.float32) * (IDX_HEADS ** -0.5), rel)
        score = jnp.where(key_pos[None, None, :] <= t[None, :, None], score, -jnp.inf)
        _, idx = lax.top_k(score, k_sel)
        kv_sel = jax.vmap(lambda cb, ib: cb[ib])(c_kv, idx)
        q_lat = jnp.einsum('bqhd,hdc->bqhc', qb, w_uk)
        logits = jnp.einsum('bqhc,bqkc->bqhk', q_lat, kv_sel).astype(jnp.float32) * (DSA_HEAD_DIM ** -0.5)
        dist = t[None, :, None] - idx
        logits = logits - slopes[None, None, :, None] * dist[:, :, None, :].astype(jnp.float32)
        logits = jnp.where((dist >= 0)[:, :, None, :], logits, -jnp.inf)
        p = jax.nn.softmax(logits, axis=-1).astype(kv_sel.dtype)
        o_lat = jnp.einsum('bqhk,bqkc->bqhc', p, kv_sel)
        o = jnp.einsum('bqhc,hcd->bqhd', o_lat, w_uv)
        return o.reshape(B, Q_BLOCK, DSA_HEADS * DSA_HEAD_DIM)

    out = lax.map(block, (q_b, iq_b, iw_b, jnp.arange(n_blocks, dtype=jnp.int32)))
    return out.swapaxes(0, 1).reshape(B, S, DSA_HEADS * DSA_HEAD_DIM)

def _peer(h, w_q, sub_keys_1, sub_keys_2, expert_u, expert_v):
    B, S, D = h.shape
    half = PEER_DKEY // 2
    q = (h @ w_q).reshape(B, S, PEER_HEADS, PEER_DKEY)
    s1 = jnp.einsum('bshd,nd->bshn', q[..., :half], sub_keys_1).astype(jnp.float32)
    s2 = jnp.einsum('bshd,nd->bshn', q[..., half:], sub_keys_2).astype(jnp.float32)
    v1, i1 = lax.top_k(s1, PEER_TOPK)
    v2, i2 = lax.top_k(s2, PEER_TOPK)
    cand = (v1[..., :, None] + v2[..., None, :]).reshape(B, S, PEER_HEADS, PEER_TOPK * PEER_TOPK)
    best, ci = lax.top_k(cand, PEER_TOPK)
    ia = jnp.take_along_axis(i1, ci // PEER_TOPK, axis=-1)
    ib = jnp.take_along_axis(i2, ci % PEER_TOPK, axis=-1)
    expert_idx = ia * PEER_NKEYS + ib
    gates = jax.nn.softmax(best, axis=-1)
    n_blocks = (B * S) // PEER_TOKEN_BLOCK
    h_b = h.reshape(n_blocks, PEER_TOKEN_BLOCK, D)
    i_b = expert_idx.reshape(n_blocks, PEER_TOKEN_BLOCK, PEER_HEADS, PEER_TOPK)
    g_b = gates.reshape(n_blocks, PEER_TOKEN_BLOCK, PEER_HEADS, PEER_TOPK)

    def block(inp):
        hx, ix, gx = inp
        u = expert_u[ix]
        v = expert_v[ix]
        a = jax.nn.gelu(jnp.einsum('td,thkd->thk', hx, u).astype(jnp.float32), approximate=False) * gx
        return jnp.einsum('thk,thkd->td', a.astype(hx.dtype), v)

    return lax.map(block, (h_b, i_b, g_b)).reshape(B, S, D)

def first_inputs(seed: int = 0) -> dict:
    key = jax.random.key(seed)
    ks = jax.random.split(key, 24)
    D = D_MODEL

    def nrm(k, shape, scale):
        return jax.random.normal(k, shape, jnp.float32) * scale

    def gain(k, shape):
        return 1.0 + 0.1 * jax.random.normal(k, shape, jnp.float32)

    return {
        "x": nrm(ks[0], (BATCH, SEQ, D), 1.0),
        "c": nrm(ks[1], (BATCH, D), 1.0),
        "w_ada": nrm(ks[2], (DEPTH, D, 6 * D), 0.5 * D ** -0.5),
        "b_ada": nrm(ks[3], (DEPTH, 6 * D), 0.02),
        "norm1_g": gain(ks[4], (DEPTH, D)),
        "w_in": nrm(ks[5], (DEPTH, D, IN_TOTAL), D ** -0.5),
        "gla_w_gate_up": nrm(ks[6], (DEPTH, GLA_GATE_RANK, GLA_DK), GLA_GATE_RANK ** -0.5),
        "gla_b_gate": nrm(ks[7], (DEPTH, GLA_DK), 0.1),
        "gla_norm_g": gain(ks[8], (DEPTH, GLA_DV)),
        "dsa_kv_norm_g": gain(ks[9], (DEPTH, DSA_LATENT)),
        "dsa_w_uk": nrm(ks[10], (DEPTH, DSA_HEADS, DSA_HEAD_DIM, DSA_LATENT), DSA_HEAD_DIM ** -0.5),
        "dsa_w_uv": nrm(ks[11], (DEPTH, DSA_HEADS, DSA_LATENT, DSA_HEAD_DIM), DSA_LATENT ** -0.5),
        "w_branch_a": nrm(ks[12], (DEPTH, GLA_DV, D), GLA_DV ** -0.5),
        "w_branch_b": nrm(ks[13], (DEPTH, DSA_HEADS * DSA_HEAD_DIM, D), (DSA_HEADS * DSA_HEAD_DIM) ** -0.5),
        "w_out": nrm(ks[14], (DEPTH, D, D), D ** -0.5),
        "norm2_g": gain(ks[15], (DEPTH, D)),
        "peer_w_q": nrm(ks[16], (DEPTH, D, PEER_HEADS * PEER_DKEY), D ** -0.5),
        "peer_sub_keys_1": nrm(ks[17], (DEPTH, PEER_NKEYS, PEER_DKEY // 2), (PEER_DKEY // 2) ** -0.5),
        "peer_sub_keys_2": nrm(ks[18], (DEPTH, PEER_NKEYS, PEER_DKEY // 2), (PEER_DKEY // 2) ** -0.5),
        "peer_u": nrm(ks[19], (DEPTH, PEER_NEXPERTS, D), D ** -0.5),
        "peer_v": nrm(ks[20], (DEPTH, PEER_NEXPERTS, D), PEER_HEADS ** -0.5),
        "final_norm_g": gain(ks[21], (D,)),
    }

def first_block(x, c, w_ada, b_ada, norm1_g, w_in, gla_w_gate_up, gla_b_gate, gla_norm_g,
              dsa_kv_norm_g, dsa_w_uk, dsa_w_uv, w_branch_a, w_branch_b, w_out, norm2_g,
              peer_w_q, peer_sub_keys_1, peer_sub_keys_2, peer_u, peer_v, final_norm_g):
    split_points = np.cumsum(IN_SIZES)[:-1].tolist()
    for l in range(DEPTH):
        ada = jax.nn.silu(c) @ w_ada[l] + b_ada[l]
        shift1, scale1, gate1, shift2, scale2, gate2 = jnp.split(ada[:, None, :], 6, axis=-1)

        h = _rmsnorm(x, norm1_g[l]) * (1.0 + scale1) + shift1
        proj = h @ w_in[l]
        (gq, gk, gv, gr, glow, dq, dkv, iq, ik, iw, za, zb) = jnp.split(proj, split_points, axis=-1)
        ya = _gla_branch(gq, gk, gv, gr, glow, gla_w_gate_up[l], gla_b_gate[l], gla_norm_g[l]) @ w_branch_a[l]
        yb = _dsa_branch(dq, dkv, iq, ik, iw, dsa_kv_norm_g[l], dsa_w_uk[l], dsa_w_uv[l]) @ w_branch_b[l]
        y = (jax.nn.sigmoid(za) * ya + jax.nn.sigmoid(zb) * yb) @ w_out[l]
        x = x + gate1 * y

        h2 = _rmsnorm(x, norm2_g[l]) * (1.0 + scale2) + shift2
        x = x + gate2 * _peer(h2, peer_w_q[l], peer_sub_keys_1[l], peer_sub_keys_2[l], peer_u[l], peer_v[l])
    return _rmsnorm(x, final_norm_g)


DEPTH_2 = 2

N_MIXERS = 2
EXPAND = 2
D_INNER = EXPAND * D_MODEL
POOL_WINDOWS = (2, 4, 8, 16)
N_POOL_GROUPS = len(POOL_WINDOWS)
POOL_GROUP_DIM = D_INNER // N_POOL_GROUPS
SB_HEADS = 16
SB_QK_DIM = 64
SB_V_DIM = D_INNER // SB_HEADS
SB_QK_WIDTH = SB_HEADS * SB_QK_DIM
RMS_EPS = 1e-6
N_POOL_LAYERS = (DEPTH_2 + 1) // 2
N_SB_LAYERS = DEPTH_2 // 2


def rms_norm(x, g):
    x32 = x.astype(jnp.float32)
    inv = lax.rsqrt(jnp.mean(x32 * x32, axis=-1, keepdims=True) + RMS_EPS)
    return (x32 * inv * g.astype(jnp.float32)).astype(x.dtype)

def causal_pool_minus_self(u, window):
    S = u.shape[1]
    u32 = u.astype(jnp.float32)
    c = jnp.cumsum(u32, axis=1)
    c_shift = jnp.pad(c, ((0, 0), (window, 0), (0, 0)))[:, :S]
    count = jnp.minimum(jnp.arange(S) + 1, window).astype(jnp.float32)
    mean = (c - c_shift) / count[None, :, None]
    return (mean - u32).astype(u.dtype)

def pooling_mixer(u, w_in, w_group, scale, w_out):
    B, S, _ = u.shape
    proj = u @ w_in
    xb, z = jnp.split(proj, 2, axis=-1)
    xg = xb.reshape(B, S, N_POOL_GROUPS, POOL_GROUP_DIM)
    pooled = jnp.stack(
        [causal_pool_minus_self(xg[:, :, gi], w) for gi, w in enumerate(POOL_WINDOWS)],
        axis=2)
    mixed = jnp.einsum('bsgi,gio->bsgo', pooled, w_group).reshape(B, S, D_INNER)
    y = mixed * scale * jax.nn.silu(z)
    return y @ w_out

def stick_breaking_attention(q, k, v):
    S = q.shape[2]
    scale = 1.0 / math.sqrt(q.shape[-1])
    n_blocks = S // Q_BLOCK
    outs = []
    for bi in range(n_blocks):
        q_lo = bi * Q_BLOCK
        k_len = q_lo + Q_BLOCK
        qb = q[:, :, q_lo:q_lo + Q_BLOCK].astype(jnp.float32)
        kb = k[:, :, :k_len].astype(jnp.float32)
        vb = v[:, :, :k_len].astype(jnp.float32)
        z = jnp.einsum('bhqd,bhkd->bhqk', qb, kb) * scale
        q_pos = q_lo + jnp.arange(Q_BLOCK)
        k_pos = jnp.arange(k_len)
        mask = k_pos[None, :] < q_pos[:, None]
        log_beta = jax.nn.log_sigmoid(z)
        log_om = jnp.where(mask, jax.nn.log_sigmoid(-z), 0.0)
        later = lax.cumsum(log_om, axis=3, reverse=True) - log_om
        a = jnp.where(mask, jnp.exp(log_beta + later), 0.0)
        outs.append(jnp.einsum('bhqk,bhkd->bhqd', a, vb))
    return jnp.concatenate(outs, axis=2).astype(v.dtype)

def stick_breaking_mixer(u, w_in, w_out):
    B, S, _ = u.shape
    proj = u @ w_in
    q, k, v, z = jnp.split(
        proj, [SB_QK_WIDTH, 2 * SB_QK_WIDTH, 2 * SB_QK_WIDTH + D_INNER], axis=-1)
    q = q.reshape(B, S, SB_HEADS, SB_QK_DIM).transpose(0, 2, 1, 3)
    k = k.reshape(B, S, SB_HEADS, SB_QK_DIM).transpose(0, 2, 1, 3)
    v = v.reshape(B, S, SB_HEADS, SB_V_DIM).transpose(0, 2, 1, 3)
    o = stick_breaking_attention(q, k, v)
    o = o.transpose(0, 2, 1, 3).reshape(B, S, D_INNER)
    y = o * jax.nn.silu(z)
    return y @ w_out

def second_inputs(seed: int = 0) -> dict:
    key = jax.random.key(seed)
    ks = jax.random.split(key, 10)
    f32 = jnp.float32
    x = jax.random.normal(ks[0], (BATCH, SEQ, D_MODEL), f32)
    norm_g = 1.0 + 0.02 * jax.random.normal(ks[1], (DEPTH_2, D_MODEL), f32)
    pool_w_in = jax.random.normal(ks[2], (N_POOL_LAYERS, D_MODEL, 2 * D_INNER), f32) * D_MODEL ** -0.5
    pool_w = jax.random.normal(ks[3], (N_POOL_LAYERS, N_POOL_GROUPS, POOL_GROUP_DIM, POOL_GROUP_DIM), f32) * POOL_GROUP_DIM ** -0.5
    pool_scale = 1.0 + 0.02 * jax.random.normal(ks[4], (N_POOL_LAYERS, D_INNER), f32)
    pool_w_out = jax.random.normal(ks[5], (N_POOL_LAYERS, D_INNER, D_MODEL), f32) * D_INNER ** -0.5
    sb_w_in = jax.random.normal(ks[6], (N_SB_LAYERS, D_MODEL, 2 * SB_QK_WIDTH + 2 * D_INNER), f32) * D_MODEL ** -0.5
    sb_w_out = jax.random.normal(ks[7], (N_SB_LAYERS, D_INNER, D_MODEL), f32) * D_INNER ** -0.5
    norm_f = 1.0 + 0.02 * jax.random.normal(ks[8], (D_MODEL,), f32)
    return {"x": x, "norm_g": norm_g, "pool_w_in": pool_w_in, "pool_w": pool_w,
            "pool_scale": pool_scale, "pool_w_out": pool_w_out, "sb_w_in": sb_w_in,
            "sb_w_out": sb_w_out, "norm_f": norm_f}

def second_block(x, norm_g, pool_w_in, pool_w, pool_scale, pool_w_out, sb_w_in, sb_w_out, norm_f):
    h = x
    for i in range(DEPTH_2):
        u = rms_norm(h, norm_g[i])
        j = i // N_MIXERS
        if i % N_MIXERS == 0:
            h = h + pooling_mixer(u, pool_w_in[j], pool_w[j], pool_scale[j], pool_w_out[j])
        else:
            h = h + stick_breaking_mixer(u, sb_w_in[j], sb_w_out[j])
    return rms_norm(h, norm_f)


def setup_inputs(seed=0):
    out = dict(first_inputs(seed))
    for name, value in second_inputs(seed + 1).items():
        if name != "x":
            out[name + "_2"] = value
    return out


def reference(
    x, c, w_ada, b_ada, norm1_g, w_in, gla_w_gate_up, gla_b_gate, gla_norm_g, dsa_kv_norm_g,
    dsa_w_uk, dsa_w_uv, w_branch_a, w_branch_b, w_out, norm2_g, peer_w_q, peer_sub_keys_1,
    peer_sub_keys_2, peer_u, peer_v, final_norm_g, norm_g_2, pool_w_in_2, pool_w_2,
    pool_scale_2, pool_w_out_2, sb_w_in_2, sb_w_out_2, norm_f_2,
):
    x = first_block(
        x, c, w_ada, b_ada, norm1_g, w_in, gla_w_gate_up, gla_b_gate, gla_norm_g, dsa_kv_norm_g,
        dsa_w_uk, dsa_w_uv, w_branch_a, w_branch_b, w_out, norm2_g, peer_w_q, peer_sub_keys_1,
        peer_sub_keys_2, peer_u, peer_v, final_norm_g,
    )
    return second_block(
        x, norm_g_2, pool_w_in_2, pool_w_2, pool_scale_2, pool_w_out_2, sb_w_in_2, sb_w_out_2,
        norm_f_2,
    )


_drawn_inputs = setup_inputs


def setup_inputs(seed=0):
    import zlib

    import numpy as np

    out = dict(_drawn_inputs(seed))
    spreads = {}
    factors = {'gla_b_gate': 7.435,
     'gla_norm_g': 4.142,
     'dsa_kv_norm_g': 3.523,
     'norm_g_2': 3.241,
     'pool_scale_2': 5.688,
     'norm_f_2': 2.718}
    for name, (base, spread) in spreads.items():
        noise = np.random.default_rng([zlib.crc32(name.encode()), seed]).standard_normal(out[name].shape)
        drawn = base * np.exp(spread * noise) if base else spread * noise
        out[name] = __import__('jax').numpy.asarray(drawn.astype(out[name].dtype))
    for name, factor in factors.items():
        out[name] = (out[name] * factor).astype(out[name].dtype)
    return out
```

```python
import concourse.bass as bass
from concourse import mybir

P = 128
F32 = mybir.dt.float32
F32R = mybir.dt.float32r
BF16 = mybir.dt.bfloat16
U32 = mybir.dt.uint32
I32 = mybir.dt.int32
ACT = mybir.ActivationFunctionType
ALU = mybir.AluOpType
AX = mybir.AxisListType

S = 512
TT = S // P
D = 1024
KT = D // P
EPS = 1e-6

GH, GDK, GDV, CH = 4, 128, 256, 64
TAU = 16.0
DH, LAT, IH, IDD, TOPK = 8, 256, 8, 64, 128
PH, NK, PK = 8, 128, 16
ET = 8
NCHUNK = NK // ET
VEC_PARTS = (("b_ada", 48), ("norm1_g", 8), ("norm2_g", 8), ("final_norm_g", 8), ("gla_b_gate", 4),
             ("gla_norm_g", 8), ("dsa_kv_norm_g", 2), ("norm_g0", 8), ("norm_g1", 8), ("norm_f", 8),
             ("pool_scale", 16))
TG = 64
WINDOWS = (2, 4, 8, 16)
SBH = 16
NEG = -1e30
TAKEN = -3e38

NADA = 6 * KT
W_L1, W_G, W_ZA, W_A, W_ZB, W_B, W_O = 0, 24, 40, 48, 56, 64, 72
W_Q, W_UV = 80, 96
W_POOL = W_UV + 2 * NK
W_SB = W_POOL + 64
W_END = W_SB + 64
RAW, SPLIT = 4, 2


NCONST = 20
NSMALL = 16 * 4
NSEL = 75
SEL_SHIFTED = 63
SB_REGIONS = [[(0, 0, 128), (512, 128, 384)], [(128, 128, 128), (1024, 256, 256)],
              [(256, 256, 128), (896, 384, 128)], [(384, 384, 128)]]


class Steps:

    def __init__(self, sem, *names):
        self.sem, self.names = sem, names

    def at(self, turn, name):
        return len(self.names) * turn + self.names.index(name) + 1


def schedule_gla():
    main = []
    for h in range(GH):
        w = W_G + 4 * h
        main += [("prep", h), ("lin", w), ("attn", h), ("lin", w + 1), ("kv", h, 0), ("kv", h, 1), ("lin", w + 2),
                 ("kv", h, 2), ("kv", h, 3), ("lin", w + 3), ("o", h)]
    side = [("mask", 0)]
    for tt in range(1, TT):
        side += [("idx", tt, h) for h in range(IH)] + [("fill", tt)]
        side += [("top", tt, r) for r in range(TOPK // 8)] + [("mask", tt)]
    out, done = [("ckv",)], 0
    for n, item in enumerate(main):
        out.append(item)
        upto = len(side) * (n + 1) // len(main)
        out += side[done:upto]
        done = upto
    return out


def schedule_dsa():
    steps = [("qlat", 0)]
    for i in range(DH * TT + 1):
        if i < DH * TT:
            steps.append(("score", i))
        if i >= 1:
            steps.append(("pt", i - 1))
            if i % TT == 0:
                steps.append(("out", i // TT - 1))
        if i % TT == TT - 1 and i // TT + 1 < DH:
            steps.append(("qlat", i // TT + 1))
    lin = [("lin", w) for w in range(W_ZA, W_A + KT)]
    out, done = [("ga", n) for n in range(KT)], 0
    for n, item in enumerate(steps):
        out.append(item)
        upto = len(lin) * (n + 1) // len(steps)
        out += lin[done:upto]
        done = upto
    return out


def build(nc, io):
    base = 16512

    def sb(name, shape, dt, kb):
        return nc.alloc_sbuf_tensor_at(name, shape, dt, offset=base + int(kb * 1024))

    xT = sb("xT", [P, KT, S], F32, 0)
    ah = sb("ah", [P, KT, S], F32R, 16)
    al = sb("al", [P, KT, S], F32R, 32)
    raw = [sb(f"raw{i}", [P, D], F32, 48 + 4 * i) for i in range(RAW)]
    wh = [sb(f"wh{i}", [P, D], F32R, 64 + 4 * i) for i in range(SPLIT)]
    wl = [sb(f"wl{i}", [P, D], F32R, 72 + 4 * i) for i in range(SPLIT)]
    cpos = [80.0]

    def const(name, shape, dt=F32):
        n = 1
        for d in shape[1:]:
            n *= d
        size = n * (2 if dt == BF16 else 4)
        t = sb(name, shape, dt, cpos[0])
        cpos[0] += (size + 31) // 32 * 32 / 1024
        return t

    ident = const("ident", [P, P])
    ones = const("ones", [P, P])
    onesr = const("onesr", [P, P], F32R)
    strict = const("strict", [P, P])
    block_causal = const("block_causal", [P, P])
    trilr = const("trilr", [P, P], F32R)
    neg = const("neg", [P, P])
    chunk_start = const("chunk_start", [P, S])
    iota_row = const("iota_row", [P, P], BF16)
    iota16 = const("iota16", [P, PK])
    zero = const("zero", [P, 8])
    eps = const("eps", [P, 1])
    one = const("one", [P, 1])
    ada = const("ada", [P, NADA])
    vec = const("vec", [P, io["vec"].shape[1]])
    cT = const("c_col", [P, KT])
    csil = const("csil", [P, KT])
    gs = const("gs", [P, 2, KT])
    inv_count = const("inv_count", [P, 4, 16])
    assert cpos[0] <= 89, cpos[0]
    VEC, at = {}, 0
    for name, n in VEC_PARTS:
        VEC[name] = vec[:, at:at + n]
        at += n
    ada_part = [ada[:, KT * i:KT * i + KT] for i in range(6)]
    shift1, scale1, gate1, shift2, scale2, gate2 = ada_part

    nsq = sb("nsq", [P, 2, S], F32, 169)
    nxn = sb("nxn", [P, 2, S], F32, 173)
    nstd = sb("nstd", [P, S], F32, 177)
    nrs = sb("nrs", [P, S], F32, 179)

    qk = sb("qk", [P, 2 * GH, S], F32, 89)
    gr = sb("gr", [P, KT, S], F32, 105)
    maskneg = sb("maskneg", [P, TT, S], F32, 121)
    ckv = sb("ckv", [P, 2, S], F32, 129)
    ckvn = sb("ckvn", [P, TT, LAT], F32, 133)
    gv = sb("gv", [P, TT, D], F32, 137)
    iq = sb("iq", [P, 4, S], F32, 153)
    ik = sb("ik", [P, S], F32, 161)
    misc = sb("misc", [P, S], F32, 163)
    gt1 = sb("gt1", [P, 2, S], F32, 165)
    gb = sb("gb", [P, S], F32, 169)
    geb = sb("geb", [P, S], F32, 171)
    gki = sb("gki", [P, S], F32, 173)
    gke = sb("gke", [P, S], F32, 175)
    gqd = sb("gqd", [P, S], F32, 177)
    gat = sb("gat", [P, TT, P], F32, 179)
    gket = sb("gket", [P, TT, P], F32, 181)
    gst = sb("gst", [P, 7, GDV], F32, 183)
    score = sb("score", [P, S], F32, 190)
    rel = sb("rel", [P, 2, S], F32, 192)
    iwn = sb("iwn", [P, TT, IH], F32, 196)
    m8 = sb("m8", [P, 8], F32, 197)
    relpos = sb("relpos", [P, 896], F32, 198)
    relpos_i = sb("relpos_i", [P, 896], I32, 190)
    gwu = sb("gwu", [16, GH * GDK], F32, 202)
    bh = sb("bh", [P, KT, S], F32R, 137)
    bl = sb("bl", [P, KT, S], F32R, 153)
    qlat = sb("qlat", [P, 2, S], F32, 169)
    uk = sb("uk", [P, 2, LAT], F32, 173)
    uv = sb("uv", [P, 2, 2, P], F32, 175)
    prob = sb("prob", [P, 2, S], F32, 177)
    tneg = sb("tneg", [P, S], F32, 181)
    pT = sb("pT", [P, TT, S], F32, 183)
    olat = sb("olat", [P, 2, S], F32, 191)
    rowstat = sb("rowstat", [P, 3, DH * TT], F32, 196.5)
    zb = sb("zb", [P, KT, S], F32, 169)
    pq = sb("pq", [P, 2, 2, S], F32, 89)
    keys = sb("keys", [P, 2, P], F32, 204)
    topv = sb("topv", [P, 2, TT, PK], F32, 98)
    topi = sb("topi", [P, 2, TT, PK], U32, 98.5)
    topf = sb("topf", [P, 2, TT, PK], F32, 99)
    swork = sb("swork", [P, 2, TT, P], F32, 100)
    cand = sb("cand", [P, TT, PK * PK], F32, 104)
    best = sb("best", [P, TT, PK], F32, 108)
    besti = sb("besti", [P, TT, PK], U32, 108.25)
    bestij = sb("bestij", [P, 2, TT, PK], U32, 108.5)
    bestf = sb("bestf", [P, 2, TT, PK], F32, 109)
    bexp = sb("bexp", [P, TT, PK], F32, 109.5)
    bsum = sb("bsum", [P, TT], F32, 109.75)
    binv = sb("binv", [P, TT], F32, 109.875)
    onehot = sb("onehot", [P, TT * PK, PK], F32, 110)
    slots = sb("slots", [P, 3, TT, PH * PK], F32, 114)
    slotT = sb("slotT", [P, 2, S], F32, 120)
    gp16 = sb("gp16", [P, 3, S], BF16, 124)
    gpart = sb("gpart", [P, 3, S], F32, 127)
    hot = sb("hot", [P, 2, 8, 4, P], BF16, 133)
    stage = sb("stage", [P, NK, TG], F32, 151)
    yT = sb("yT", [P, KT, S], F32, 89)
    eh = sb("eh", [P, ET, S], F32R, 105)
    el = sb("el", [P, ET, S], F32R, 121)
    gt = sb("gt", [P, 2, S // TG, ET * TG], F32, 137)
    act_g = sb("act_g", [P, 2, S], F32, 169)
    act_m = sb("act_m", [P, 2, S], F32, 173)
    ch = sb("ch", [P, KT, S], F32R, 89)
    cl = sb("cl", [P, KT, S], F32R, 105)
    dh = sb("dh", [P, KT, S], F32R, 121)
    dl = sb("dl", [P, KT, S], F32R, 137)
    zs = sb("zs", [P, KT, S], F32, 153)
    ub = sb("ub", [P, 2, 16 + S], F32, 169)
    us = sb("us", [P, 2, 16 + S], F32, 174)
    um = sb("um", [P, 2, S], F32, 179)
    sqk = sb("sqk", [P, KT, S], F32, 121)
    sv = sb("sv", [P, TT, D], F32, 137)
    SW = 1280
    st = sb("st", [P, SW], F32, 169)
    slb = sb("slb", [P, SW], F32, 174)
    slo = sb("slo", [P, SW], F32, 179)
    slh = sb("slh", [P, SW], F32R, 184)
    sll = sb("sll", [P, SW], F32R, 189)
    sy = sb("sy", [P, S], F32, 194)
    outT = sb("outT", [P, KT, S], F32, 121)

    psum = nc.alloc_psum_tensor("psum", [P, 8, S], F32)
    acc = [psum[:, i, :] for i in range(4)]
    aux = [psum[:, 4 + i, :] for i in range(4)]
    aux3 = psum[:, 4:7, :].rearrange("p a n -> p (a n)")[:, 0:SW]
    acc3 = psum[:, 1:4, :].rearrange("p a n -> p (a n)")[:, 0:SW]

    gate_table = nc.dram_tensor("gate_table", (S // TG, P, NK * TG), F32, kind="Internal").ap()

    sem = nc.alloc_semaphore
    raw_here = [sem(f"raw_here{i}") for i in range(RAW)]
    ada_used = sem("ada_used")
    weights_split = sem("weights_split")
    split_step = sem("split_step")
    tile_done = sem("tile_done")
    evacuated = sem("evacuated")
    small_here = sem("small_here")
    xin_here = sem("xin_here")
    const_pool = sem("const_pool")
    const_dve = sem("const_dve")
    const_vec = sem("const_vec")
    csil_done = sem("csil_done")
    ada_done = sem("ada_done")
    x_ready = sem("x_ready")
    nsq_done, nmm_done, nstd_done, ninv_done = sem("nsq_done"), sem("nmm_done"), sem("nstd_done"), sem("ninv_done")
    nxn_done, nhi_done, nlo_done, nout_done = sem("nxn_done"), sem("nhi_done"), sem("nlo_done"), sem("nout_done")
    out_stored = sem("out_stored")

    GP = Steps(sem("gla_pe"), "gate", "attn", "ket", "kv0", "kv1", "kv2", "kv3", "o", "ms")
    GA = Steps(sem("gla_act"), "abs", "exp", "ln", "eb", "enb", "ekd", "ket", "sq0", "sq1", "std")
    GD = Steps(sem("gla_dve"), "min", "logalpha", "cumsum", "dif", "qd", "ki", "ke", "attn",
               *[f"s{c}" for c in range(1, 8)], "rstd", "og0", "og1", "y0", "y1")
    CP = Steps(sem("ckv_pe"), "ms", "iw", "ckvn")
    CA = Steps(sem("ckv_act"), "sq0", "sq1", "std", "n0", "n1")
    CD = Steps(sem("ckv_dve"), "rstd", "c0", "c1", "iw")
    idx_mm, idx_relu, idx_acc = sem("idx_mm"), sem("idx_relu"), sem("idx_acc")
    top_step = sem("top_step")
    ga_hi, ga_lo = sem("ga_hi"), sem("ga_lo")
    uk_here = [sem("uk_here0"), sem("uk_here1")]
    DP_q, DP_s, DP_t, DP_o, DP_v = sem("qlat_mm"), sem("logit_mm"), sem("probT_mm"), sem("olat_mm"), sem("oval_mm")
    DA_q, DA_e, DA_n, DA_o, DA_v = sem("qlat_out"), sem("prob_exp"), sem("prob_norm"), sem("olat_out"), sem("oval_out")
    DD = Steps(sem("dsa_dve"), "bias", "logit", "max", "inv")
    pT_out = sem("probT_out")
    y_step, y_hi, y_lo = sem("y_step"), sem("y_hi"), sem("y_lo")
    db_hi, db_lo = sem("dsaout_hi"), sem("dsaout_lo")
    pq_out, ps_mm = sem("pq_out"), sem("ps_mm")
    sel = sem("sel_step")
    sel_exp = sem("sel_exp")
    sT_mm, sT_step = sem("slotT_mm"), sem("slotT_step")
    hot_done, table_mm, table_out, table_stored = sem("hot_done"), sem("table_mm"), sem("table_out"), sem("table_stored")
    gt_here = [sem("gt_here0"), sem("gt_here1")]
    e_gelu, e_mul, e_hi, e_lo = sem("e_gelu"), sem("e_mul"), sem("e_hi"), sem("e_lo")
    y_zero = sem("y_zero")
    pl_step, pl_hi, pl_lo = sem("pool_step"), sem("pool_hi"), sem("pool_lo")
    pw_y, pw_hi, pw_lo = sem("pooly"), sem("pooly_hi"), sem("pooly_lo")
    SP_ = Steps(sem("sb_pe"), "qk", "cum", "o")
    SA = Steps(sem("sb_act"), "abs", "exp", "ln", "hi", "a", "yhi")
    SD = Steps(sem("sb_dve"), "min", "lb", "lo", "mask", "losplit", "sum", "amask", "y", "ylo")

    def groups(eng, count, body):
        if count == 1:
            body(0)
        else:
            with eng.Fori(0, count) as g:
                body(g)

    def item_of(table, index):
        return table[bass.ds(index, 1), :, :].rearrange("a p n -> p (a n)")


    PL_END, n = [], 0
    for half in range(2):
        for t in range(8):
            n += 2 * half + t // 4 + 1 + 3
            PL_END.append(n)
    SEQ_G, SEQ_D = schedule_gla(), schedule_dsa()
    block_cm = nc.Block()
    block = block_cm.__enter__()
    lin_segments = [("w_in", 0, W_L1, W_A), ("w_branch_a", 0, W_A, W_ZB), ("w_in", W_A, W_ZB, W_B),
                    ("w_branch_b", 0, W_B, W_O), ("w_out", 0, W_O, W_Q), ("peer_w_q", 0, W_Q, W_UV)]

    @block.sync
    def _(sp):
        def load(table, first, count, w, width=D):
            def four(g):
                for j in range(RAW):
                    sp.wait_ge(weights_split, w + 4 * g + j - RAW + 1)
                    sp.dma_start(raw[j][:, 0:width], item_of(table, first + 4 * g + j)).then_inc(raw_here[j], 16)
            groups(sp, count // RAW, four)

        for j in range(RAW):
            sp.dma_start(raw[j][:, :], item_of(io["w_ada"], j)).then_inc(raw_here[j], 16)
        with sp.Fori(0, NADA // RAW - 1) as g:
            for j in range(RAW):
                sp.wait_ge(ada_used, 4 * g + j + 1)
                sp.dma_start(raw[j][:, :], item_of(io["w_ada"], 4 * g + j + RAW)).then_inc(raw_here[j], 16)
        for j in range(RAW):
            sp.wait_ge(ada_used, NADA - RAW + j + 1)
            sp.dma_start(raw[j][:, :], item_of(io["w_in"], j)).then_inc(raw_here[j], 16)
        load(io["w_in"], RAW, W_A - RAW, RAW)
        for name, first, w, end in lin_segments[1:]:
            load(io[name], first, end - w, w)

        sp.wait_ge(table_stored, 16 * S // TG)
        def chunks(g, first):
            for half in range(2):
                w = W_UV + 32 * g + 16 * half
                if not first:
                    sp.wait_ge(e_mul, ET * (2 * g + half - 1))
                sp.dma_start(gt[:, half, :, :],
                             gate_table.rearrange("g p (c n) -> c p g n", c=NCHUNK)[bass.ds(2 * g + half, 1)]
                             .rearrange("a p g n -> p (a g) n")).then_inc(gt_here[half], 16)
                for t in range(16):
                    table, at = ("peer_u", t) if t < 8 else ("peer_v", t - 8)
                    sp.wait_ge(weights_split, w + t - RAW + 1)
                    sp.dma_start(raw[t % RAW][:, :], item_of(io[table], 16 * g + 8 * half + at))\
                        .then_inc(raw_here[t % RAW], 16)
        chunks(0, True)
        with sp.Fori(1, NCHUNK // 2) as g:
            chunks(g, False)

        for half in range(2):
            w = W_POOL + 32 * half
            load(io["pool_w_in"], 16 * half, 16, w)
            load(io["pool_w"], 8 * half, 8, w + 16, width=D // 2)
            load(io["pool_w_out"], 8 * half, 8, w + 24)
        for half in range(2):
            w = W_SB + 32 * half
            load(io["sb_w_in"], 24 * half, 24, w)
            load(io["sb_w_out"], 8 * half, 8, w + 24)

    @block.gpsimd
    def _(pool):
        steps = [
            pool.memset(ident[:, :], 0.0), pool.memset(ones[:, :], 1.0), pool.memset(strict[:, :], 1.0),
            pool.memset(block_causal[:, :], 1.0), pool.memset(neg[:, :], NEG),
            pool.memset(chunk_start[:, :], 1.0), pool.memset(zero[:, :], 0.0), pool.memset(eps[:, :], EPS),
            pool.memset(one[:, :], 1.0),
            pool.iota(iota_row[:, :], pattern=[[1, P]], base=0, channel_multiplier=0,
                      allow_small_or_imprecise_dtypes=True),
            pool.iota(iota16[:, :], pattern=[[1, PK]], base=0, channel_multiplier=0,
                      allow_small_or_imprecise_dtypes=True),
            pool.iota(relpos[:, :], pattern=[[1, 896]], base=-384, channel_multiplier=-1,
                      allow_small_or_imprecise_dtypes=True),
        ]
        for ins in steps:
            ins.then_inc(const_pool, 1)
        n = len(steps)
        pool.wait_ge(const_pool, n)
        for ins in (
            pool.affine_select(out=ident[:, :], in_=ident[:, :], compare_op=ALU.not_equal, fill=1.0, base=0,
                               pattern=[[-1, P]], channel_multiplier=1),
            pool.affine_select(out=strict[:, :], in_=strict[:, :], compare_op=ALU.is_gt, fill=0.0, base=0,
                               pattern=[[1, P]], channel_multiplier=-1),
            pool.affine_select(out=block_causal[:, :], in_=block_causal[:, :], compare_op=ALU.is_ge, fill=0.0,
                               base=0, pattern=[[1, P]], channel_multiplier=-1),
            pool.memset(chunk_start[:, :].rearrange("p (c t) -> p c t", t=CH)[:, :, 0:1], 0.0),
        ):
            ins.then_inc(const_pool, 1)
        pool.wait_ge(const_pool, n + 4)
        pool.memset(block_causal[0:CH, CH:P], 0.0).then_inc(const_pool, 1)
        pool.tensor_tensor(trilr[:, :], ones[:, :], strict[:, :], ALU.subtract).then_inc(const_pool, 1)
        pool.wait_ge(const_pool, n + 6)
        pool.tensor_tensor(trilr[:, :], trilr[:, :].bitcast(F32), ident[:, :], ALU.subtract).then_inc(const_pool, 1)
        pool.tensor_tensor(onesr[:, :], ones[:, :], zero[:, 0:1].broadcast_to([P, P]), ALU.add)\
            .then_inc(const_pool, 1)
        assert n + 8 == NCONST

        def split(w, j, g, width, first=False):
            s = j % SPLIT
            pool.wait_ge(raw_here[j], 16 * (g + 1))
            if not first:
                pool.wait_ge(tile_done, w - SPLIT + 1)
            pool.tensor_tensor(wh[s][:, 0:width], raw[j][:, 0:width], zero[:, 0:1].broadcast_to([P, width]),
                               ALU.add).then_inc(split_step, 1)
            pool.wait_ge(split_step, w + 1)
            pool.tensor_tensor(wl[s][:, 0:width], raw[j][:, 0:width], wh[s][:, 0:width].bitcast(F32),
                               ALU.subtract).then_inc(weights_split, 1)

        G0 = NADA // RAW
        for j in range(RAW):
            split(j, j, G0, D, first=j < SPLIT)
        for w, count, width in [(RAW, W_POOL + 16 - RAW, D), (W_POOL + 16, 8, D // 2), (W_POOL + 24, 24, D),
                                (W_POOL + 48, 8, D // 2), (W_POOL + 56, W_END - W_POOL - 56, D)]:
            with pool.Fori(0, count // RAW) as g:
                for j in range(RAW):
                    split(w + 4 * g + j, j, G0 + w // 4 + g, width)

    @block.tensor
    def _(pe):
        def products(out, whi, wlo, ahi, alo, start, stop):
            pe.matmul(out, whi, ahi, start=start, stop=False, skip_group_check=True)
            pe.matmul(out, whi, alo, start=False, stop=False, skip_group_check=True)
            return pe.matmul(out, wlo, ahi, start=False, stop=stop, skip_group_check=True)

        def lin(w, j, hi, lo, k0=0, kt=KT, bank=None, free=True):
            pe.wait_ge(weights_split, w + 1)
            if free:
                pe.wait_ge(evacuated, w - 3)
            s = j % SPLIT
            out = acc[j if bank is None else bank]
            for k in range(kt):
                cols = slice(P * k, P * k + P)
                mm = products(out, wh[s][:, cols], wl[s][:, cols], hi[:, k0 + k, :], lo[:, k0 + k, :],
                              k == 0, k == kt - 1)
            mm.then_inc(tile_done, 1)

        def lin_loop(w, count, hi, lo):
            def four(g):
                for j in range(4):
                    lin(w + 4 * g + j, j, hi, lo)
            groups(pe, count // 4, four)

        def lin_tokens(w, turns, hi, lo):
            def turn(g):
                for j in range(4):
                    pe.wait_ge(weights_split, w + 4 * g + j + 1)
                    if j == 0:
                        pe.wait_ge(evacuated, w + 4 * g)
                    s = j % SPLIT
                    for kk in range(2):
                        k = 2 * j + kk
                        cols = slice(S * kk, S * kk + S)
                        for t in range(TT):
                            tok = slice(P * t, P * t + P)
                            first, last = k == 0, k == KT - 1
                            pe.matmul(acc[t], hi[:, k, tok], wh[s][:, cols], start=first, stop=False,
                                      skip_group_check=True)
                            pe.matmul(acc[t], lo[:, k, tok], wh[s][:, cols], start=False, stop=False,
                                      skip_group_check=True)
                            mm = pe.matmul(acc[t], hi[:, k, tok], wl[s][:, cols], start=False, stop=last,
                                           skip_group_check=True)
                    mm.then_inc(tile_done, 1)
            groups(pe, turns, turn)

        def norm(o):
            for k in range(KT):
                pe.wait_ge(nsq_done, KT * o + k + 1)
                pe.matmul(aux[0], ones[:, :], nsq[:, k % 2, :], start=k == 0, stop=k == KT - 1)\
                    .then_inc(nmm_done, 1)

        pe.wait_ge(const_pool, NCONST)
        pe.wait_ge(csil_done, 1)
        with pe.Fori(0, NADA // RAW) as g:
            for j in range(RAW):
                pe.wait_ge(raw_here[j], 16 * (g + 1))
                for k in range(KT):
                    mm = pe.matmul(psum[:, 7, bass.ds(4 * g + j, 1)], raw[j][:, P * k:P * k + P],
                                   csil[:, k:k + 1], start=k == 0, stop=k == KT - 1)
                mm.then_inc(ada_used, 1)

        norm(0)
        pe.wait_ge(nlo_done, KT)
        for j in range(4):
            lin(j, j, ah, al, free=False)
        lin_loop(4, 8, ah, al)
        lin_tokens(12, 2, ah, al)
        lin_loop(20, 4, ah, al)

        pe.wait_ge(small_here, NSMALL)
        for item in SEQ_G:
            kind = item[0]
            if kind == "ckv":
                for k in range(2):
                    pe.wait_ge(CA.sem, CA.at(0, f"sq{k}"))
                    mm = pe.matmul(aux[0], ones[:, :], gt1[:, k, :], start=k == 0, stop=k == 1)
                mm.then_inc(CP.sem, 1)
                pe.wait_ge(ada_done, 1)
                for t in range(TT):
                    mm = pe.transpose(aux[3][:, P * t:P * t + P], misc[:, P * t:P * t + P], ident[:, :])
                mm.then_inc(CP.sem, 1)
                pe.wait_ge(CD.sem, CD.at(0, "c1"))
                for t in range(TT):
                    for c in range(2):
                        mm = pe.transpose(psum[:, 5 + t // 2, LAT * (t % 2) + P * c:LAT * (t % 2) + P * c + P],
                                          ckv[:, c, P * t:P * t + P], ident[:, :])
                mm.then_inc(CP.sem, 1)
            elif kind == "lin":
                w = item[1]
                lin(w, w % 4, ah, al)
            elif kind == "prep":
                h = item[1]
                if h:
                    pe.wait_ge(GD.sem, GD.at(h - 1, "og1"))
                else:
                    pe.wait_ge(CA.sem, CA.at(0, "std"))
                pe.matmul(aux[0], gwu[:, GDK * h:GDK * h + GDK], misc[0:16, :], start=True, stop=True)\
                    .then_inc(GP.sem, 1)
            elif kind == "attn":
                h = item[1]
                if h == 0:
                    pe.wait_ge(CA.sem, CA.at(0, "n1"))
                pe.wait_ge(GD.sem, GD.at(h, "ki"))
                for t in range(TT):
                    tok = slice(P * t, P * t + P)
                    mm = pe.matmul(aux[1][:, tok], gki[:, tok], gqd[:, tok], start=True, stop=True)
                mm.then_inc(GP.sem, 1)
                pe.wait_ge(GD.sem, GD.at(h, "ke"))
                for t in range(TT):
                    tok = slice(P * t, P * t + P)
                    mm = pe.transpose(aux[0][:, tok], gke[:, tok], ident[:, :])
                mm.then_inc(GP.sem, 1)
            elif kind == "kv":
                h, t = item[1:]
                if t == 0:
                    pe.wait_ge(GA.sem, GA.at(h, "ket"))
                    pe.wait_ge(GD.sem, GD.at(h, "attn"))
                    if h:
                        pe.wait_ge(GA.sem, GA.at(h - 1, "std"))
                else:
                    pe.wait_ge(GD.sem, GD.at(h, f"s{2 * t}"))
                for c in range(2 if t < 3 else 1):
                    rows = slice(CH * c, CH * c + CH)
                    mm = pe.matmul(aux[2 - c][:, 0:GDV], gket[rows, t, :],
                                   gv[rows, t, GDV * h:GDV * h + GDV], start=True, stop=True)
                mm.then_inc(GP.sem, 1)
            elif kind == "o":
                h = item[1]
                pe.wait_ge(GD.sem, GD.at(h, "s7"))
                for v in range(2):
                    out = aux[1 - v]
                    val = slice(GDV * h + P * v, GDV * h + P * v + P)
                    for t in range(TT):
                        tok = slice(P * t, P * t + P)
                        mm = pe.matmul(out[:, tok], gv[:, t, val], gat[:, t, :], start=t == 0, stop=False,
                                       skip_group_check=True)
                    for c in range(1, 8):
                        tok = slice(CH * c, CH * c + CH)
                        mm = pe.matmul(out[:, tok], gst[:, c - 1, P * v:P * v + P], gqd[:, tok], start=False,
                                       stop=c == 7, skip_group_check=True)
                mm.then_inc(GP.sem, 1)
                for v in range(2):
                    pe.wait_ge(GA.sem, GA.at(h, f"sq{v}"))
                    mm = pe.matmul(aux[2], ones[:, :], gt1[:, v, :], start=v == 0, stop=v == 1)
                mm.then_inc(GP.sem, 1)
            elif kind == "idx":
                tt, h = item[1:]
                i = (tt - 1) * IH + h
                if i:
                    pe.wait_ge(idx_relu, i)
                else:
                    pe.wait_ge(evacuated, W_G)
                    pe.wait_ge(CD.sem, CD.at(0, "iw"))
                rows = slice(IDD * (h % 2), IDD * (h % 2) + IDD)
                pe.matmul(aux[3][:, 0:P * (tt + 1)], iq[rows, h // 2, P * tt:P * tt + P],
                          ik[rows, 0:P * (tt + 1)], start=True, stop=True).then_inc(idx_mm, 1)

        for item in SEQ_D:
            kind = item[0]
            if kind == "lin":
                w = item[1]
                if w == W_A:
                    pe.wait_ge(ga_lo, KT)
                if w < W_A:
                    lin(w, w % 4, ah, al)
                else:
                    lin(w, w % 4, bh, bl)
            elif kind == "qlat":
                h = item[1]
                pe.wait_ge(uk_here[h % 2], 32 * (h // 2 + 1))
                if h >= 2:
                    pe.wait_ge(DA_v, h - 1)
                elif h == 0:
                    pe.wait_ge(GA.sem, GA.at(GH - 1, "std"))
                    pe.wait_ge(idx_relu, 3 * IH)
                    pe.wait_ge(evacuated, W_ZA)
                for c in range(2):
                    mm = pe.matmul(aux[2 + c], uk[:, h % 2, P * c:P * c + P], qk[:, h, :], start=True, stop=True)
                mm.then_inc(DP_q, 1)
            elif kind == "score":
                h, t = divmod(item[1], TT)
                i = item[1]
                n = P * (t + 1)
                pe.wait_ge(DA_q, h + 1)
                if i:
                    pe.wait_ge(DD.sem, DD.at(i - 1, "logit"))
                else:
                    pe.wait_ge(GD.sem, GD.at(GH - 1, "og1"))
                for c in range(2):
                    mm = pe.matmul(aux[0][:, 0:n], qlat[:, c, P * t:P * t + P], ckv[:, c, 0:n],
                                   start=c == 0, stop=c == 1)
                mm.then_inc(DP_s, 1)
            elif kind == "pt":
                i = item[1]
                t = i % TT
                pe.wait_ge(DA_n, i + 1)
                if i:
                    pe.wait_ge(pT_out, i)
                for b in range(t + 1):
                    mm = pe.transpose(aux[1][:, P * b:P * b + P], prob[:, i % 2, P * b:P * b + P], ident[:, :])
                mm.then_inc(DP_t, 1)
            elif kind == "out":
                h = item[1]
                pe.wait_ge(pT_out, TT * (h + 1))
                if h + 1 < DH:
                    pe.wait_ge(DA_q, h + 2)
                for c in range(2):
                    for b in range(TT):
                        mm = pe.matmul(aux[2 + c][:, P * b:S], ckvn[:, b, P * c:P * c + P], pT[:, b, P * b:S],
                                       start=b == 0, stop=b == TT - 1, skip_group_check=True)
                mm.then_inc(DP_o, 1)
                pe.wait_ge(DA_o, h + 1)
                for c in range(2):
                    mm = pe.matmul(aux[2], uv[:, h % 2, c, :], olat[:, c, :], start=c == 0, stop=c == 1)
                mm.then_inc(DP_v, 1)

        lin_loop(W_ZB, 8, ah, al)
        pe.wait_ge(db_lo, KT)
        lin_loop(W_B, 8, bh, bl)
        pe.wait_ge(y_lo, KT)
        lin_loop(W_O, 8, ah, al)
        norm(1)
        pe.wait_ge(nlo_done, 2 * KT)

        for h in range(PH):
            for side in range(2):
                w = W_Q + 2 * h + side
                lin(w, w % 4, ah, al)
            for side in range(2):
                pe.wait_ge(evacuated, W_Q + 2 * h + side + 1)
                if h >= 2:
                    pe.wait_ge(sel, NSEL * (h - 2) + 24)
                for t in range(TT):
                    mm = pe.matmul(aux[2 * (h % 2) + side][:, P * t:P * t + P], pq[:, h % 2, side, P * t:P * t + P],
                                   keys[:, side, :], start=True, stop=True)
                mm.then_inc(ps_mm, 1)
        pe.wait_ge(sel, NSEL * PH)
        for part in range(3):
            for t in range(TT):
                mm = pe.transpose(aux[part][:, P * t:P * t + P], slots[:, part, t, :], ident[:, :])
            mm.then_inc(sT_mm, 1)
        pe.wait_ge(sT_step, 7)
        def table(g, first):
            for q in range(TG // 4):
                if not (first and q < 4):
                    pe.wait_ge(table_out, 16 * g + q - 3)
                if q % 2 == 0:
                    pe.wait_ge(hot_done, 8 * g + q // 2 + 1)
                for t in range(4):
                    u = 4 * (q % 2) + t
                    for part in range(3):
                        mm = pe.matmul(aux[q % 4][:, P * t:P * t + P], hot[:, (q // 2) % 2, u, 0, :],
                                       hot[:, (q // 2) % 2, u, 1 + part, :], start=part == 0, stop=part == 2)
                mm.then_inc(table_mm, 1)
        table(0, True)
        with pe.Fori(1, S // TG) as g:
            table(g, False)

        with pe.Fori(0, NCHUNK // 2) as g:
            for half in range(2):
                w = W_UV + 32 * g + 16 * half
                for e in range(ET):
                    lin(w + e, e % 4, ah, al)
                for hf in range(2):
                    for p in range(ET // 2):
                        v = w + ET + 4 * hf + p
                        pe.wait_ge(weights_split, v + 1)
                        if p == 0:
                            pe.wait_ge(evacuated, v)
                        pe.wait_ge(e_lo, 2 * ET * g + ET * half + 2 * p + 2)
                        for ee in range(2):
                            e = 2 * p + ee
                            for d in range(4):
                                cols = slice(S * ee + P * d, S * ee + P * d + P)
                                mm = products(acc[d], wh[p % 2][:, cols], wl[p % 2][:, cols], eh[:, e, :], el[:, e, :],
                                              e == 0, e == ET - 1)
                        mm.then_inc(tile_done, 1)
        norm(2)
        norm(3)
        pe.wait_ge(nlo_done, 3 * KT)

        for half in range(2):
            w = W_POOL + 32 * half
            lin_loop(w, 16, ah, al)
            for n in range(8):
                if n % 4 == 0:
                    pe.wait_ge(pl_lo, 8 * half + n + 4)
                lin(w + 16 + n, n % 4, ch, cl, k0=n // 4 * 4, kt=4)
            pe.wait_ge(pw_lo, 8 * half + 8)
            lin_loop(w + 24, 8, dh, dl)
        norm(4)
        pe.wait_ge(nlo_done, 4 * KT)

        for half in range(2):
            w = W_SB + 32 * half
            lin_loop(w, 8, ah, al)
            lin_tokens(w + 8, 2, ah, al)
            pe.wait_ge(evacuated, w + 16)
            for hd in range(8):
                i = 8 * half + hd
                rows = slice(64 * (hd % 2), 64 * (hd % 2) + 64)
                q, k = sqk[rows, hd // 2, :], sqk[rows, 4 + hd // 2, :]
                if i:
                    pe.wait_ge(SD.sem, SD.at(i - 1, "lo"))
                for b in range(TT):
                    for at, c0, n in SB_REGIONS[b]:
                        mm = pe.matmul(aux3[:, at:at + n], k[:, P * b:P * b + P], q[:, c0:c0 + n],
                                       start=True, stop=True, skip_group_check=True)
                mm.then_inc(SP_.sem, 1)
                pe.wait_ge(weights_split, w + 16 + hd + 1)
                pe.wait_ge(evacuated, w + 16 + hd)
                s = hd % SPLIT
                for kk in range(KT):
                    cols = slice(P * kk, P * kk + P)
                    mm = products(acc[0], wh[s][:, cols], wl[s][:, cols], ah[:, kk, :], al[:, kk, :],
                                  kk == 0, kk == KT - 1)
                mm.then_inc(tile_done, 1)
                pe.wait_ge(SD.sem, SD.at(i, "losplit"))
                if i:
                    pe.wait_ge(SD.sem, SD.at(i - 1, "sum"))
                plan = [(trilr, b, b) for b in range(TT)] + [(onesr, b, c) for b in range(TT) for c in range(b + 1, TT)]
                sums = []
                for mat, b, c in plan:
                    for at, c0, n in SB_REGIONS[c]:
                        for to, d0, m in SB_REGIONS[b]:
                            a, z = max(c0, d0), min(c0 + n, d0 + m)
                            if a < z:
                                sums += [(mat, src[:, at + a - c0:at + z - c0], to + a - d0, z - a)
                                         for src in (slh, sll)]
                banks = [to // S for _, _, to, _ in sums]
                for n, (mat, src, to, m) in enumerate(sums):
                    mm = pe.matmul(acc3[:, to:to + m], mat[:, :], src, start=banks[n] not in banks[:n],
                                   stop=banks[n] not in banks[n + 1:], skip_group_check=True)
                mm.then_inc(SP_.sem, 1)
                pe.wait_ge(SD.sem, SD.at(i, "amask"))
                if i:
                    pe.wait_ge(SD.sem, SD.at(i - 1, "y"))
                for b in range(TT):
                    for at, c0, n in SB_REGIONS[b]:
                        mm = pe.matmul(aux[3][:, c0:c0 + n], sv[:, b, P * hd:P * hd + P], st[:, at:at + n],
                                       start=at == 0, stop=b == TT - 1, skip_group_check=True)
                mm.then_inc(SP_.sem, 1)
            pe.wait_ge(SD.sem, SD.at(8 * half + 7, "ylo"))
            lin_loop(w + 24, 8, ch, cl)
        norm(5)

    @block.scalar
    def _(act):
        def evac(w, j, dst, func=ACT.Copy, bank=None, done=None):
            act.wait_ge(tile_done, w + 1 if done is None else done)
            act.activation(dst, acc[j if bank is None else bank], func).then_inc(evacuated, 1)

        def evac_loop(w, count, dst, func=ACT.Copy):
            def four(g):
                for j in range(4):
                    evac(w + 4 * g + j, j, dst[:, bass.ds(4 * g + j, 1), :].rearrange("p a n -> p (a n)"), func)
            if count == 4:
                for j in range(4):
                    evac(w + j, j, dst[:, j, :], func)
            else:
                groups(act, count // 4, four)

        def evac_tokens(w, turns, dst):
            for g in range(turns):
                for j in range(4):
                    evac(w, j, dst[:, j, S * g:S * g + S], done=w + 4 * g + 4)

        def norm(o, ready, base, split=None, shift=None):
            for k in range(KT):
                act.wait_ge(ready, base if ready is xin_here else base + k + 1)
                if k >= 2 or o:
                    act.wait_ge(nmm_done, KT * o + k - 1)
                act.activation(nsq[:, k % 2, :], xT[:, k, :], ACT.Square).then_inc(nsq_done, 1)
            act.wait_ge(nmm_done, KT * o + KT)
            act.activation(nstd[:, :], aux[0], ACT.Sqrt, scale=1.0 / D, bias=eps[:, :]).then_inc(nstd_done, 1)
            if split is not None:
                for k in range(KT):
                    act.wait_ge(nxn_done, KT * split + k + 1)
                    act.activation(ah[:, k, :], nxn[:, k % 2, :], ACT.Identity,
                                   bias=zero[:, 0:1] if shift is None else shift[:, k:k + 1]).then_inc(nhi_done, 1)

        for dst, name in ((cT, "c"), (vec, "vec"), (gwu, "gla_w_gate_up"), (keys, "peer_sub_keys")):
            src = io[name].rearrange("p a n -> p (a n)") if name == "peer_sub_keys" else io[name]
            d = dst[:, :, :].rearrange("p a n -> p (a n)") if name == "peer_sub_keys" else dst[:, :]
            act.dma_start(d, src).then_inc(small_here, 16)
        act.dma_start(xT[:, :, :], io["x"]).then_inc(xin_here, 16)

        act.wait_ge(small_here, NSMALL)
        act.activation(csil[:, :], cT[:, :], ACT.Silu).then_inc(csil_done, 1)
        act.wait_ge(const_pool, NCONST)
        act.wait_ge(ada_done, 1)
        norm(0, xin_here, 16, split=0, shift=shift1)

        evac(0, 0, misc[:, :])
        evac(1, 1, ik[:, :])
        evac(2, 2, ckv[:, 0, :])
        evac(3, 3, ckv[:, 1, :])
        evac_loop(4, 8, qk)
        evac_tokens(12, 2, gv)
        evac_loop(20, 4, iq)

        for item in SEQ_G:
            kind = item[0]
            if kind == "ckv":
                act.wait_ge(evacuated, 4)
                for k in range(2):
                    act.activation(gt1[:, k, :], ckv[:, k, :], ACT.Square).then_inc(CA.sem, 1)
                act.wait_ge(CP.sem, CP.at(0, "ms"))
                act.activation(nstd[:, :], aux[0], ACT.Sqrt, scale=1.0 / LAT, bias=eps[:, :]).then_inc(CA.sem, 1)
                act.wait_ge(CP.sem, CP.at(0, "ckvn"))
                for b in range(2):
                    act.activation(ckvn[:, 2 * b:2 * b + 2, :].rearrange("p a n -> p (a n)"), psum[:, 5 + b, :],
                                   ACT.Copy).then_inc(CA.sem, 1)
            elif kind == "lin":
                w = item[1]
                h, r = divmod(w - W_G, 4)
                if r < 2:
                    evac(w, w % 4, gr[:, 2 * h + r, :], ACT.Silu)
                else:
                    act.wait_ge(GD.sem, GD.at(h, "ke"))
                    evac(w, w % 4, qk[:, 2 * h + r - 2, :])
            elif kind == "prep":
                h = item[1]
                act.wait_ge(GP.sem, GP.at(h, "gate"))
                if h:
                    act.wait_ge(GD.sem, GD.at(h - 1, "y1"))
                act.activation(gt1[:, 0, :], aux[0], ACT.Abs, bias=VEC["gla_b_gate"][:, h:h + 1])\
                    .then_inc(GA.sem, 1)
                act.wait_ge(GA.sem, GA.at(h, "abs"))
                act.activation(gt1[:, 0, :], gt1[:, 0, :], ACT.Exp, scale=-1.0).then_inc(GA.sem, 1)
                act.wait_ge(GA.sem, GA.at(h, "exp"))
                act.activation(gt1[:, 0, :], gt1[:, 0, :], ACT.Ln, bias=one[:, :]).then_inc(GA.sem, 1)
                act.wait_ge(GD.sem, GD.at(h, "cumsum"))
                act.activation(geb[:, :], gb[:, :], ACT.Exp, scale=1.0 / TAU).then_inc(GA.sem, 1)
                act.activation(gki[:, :], gb[:, :], ACT.Exp, scale=-1.0 / TAU).then_inc(GA.sem, 1)
                act.wait_ge(GD.sem, GD.at(h, "dif"))
                act.activation(gke[:, :], gke[:, :], ACT.Exp, scale=1.0 / TAU).then_inc(GA.sem, 1)
            elif kind == "attn":
                h = item[1]
                act.wait_ge(GP.sem, GP.at(h, "ket"))
                act.activation(gket[:, :, :].rearrange("p a n -> p (a n)"), aux[0], ACT.Copy).then_inc(GA.sem, 1)
            elif kind == "o":
                h = item[1]
                act.wait_ge(GP.sem, GP.at(h, "o"))
                for v in range(2):
                    act.activation(gt1[:, v, :], aux[1 - v], ACT.Square).then_inc(GA.sem, 1)
                act.wait_ge(GP.sem, GP.at(h, "ms"))
                act.activation(gke[:, :], aux[2], ACT.Sqrt, scale=1.0 / GDV, bias=eps[:, :]).then_inc(GA.sem, 1)
            elif kind == "idx":
                tt, h = item[1:]
                i = (tt - 1) * IH + h
                n = P * (tt + 1)
                act.wait_ge(idx_mm, i + 1)
                if i >= 2:
                    act.wait_ge(idx_acc, i - 1)
                act.activation(rel[:, i % 2, 0:n], aux[3][:, 0:n], ACT.Relu, scale=IDD ** -0.5).then_inc(idx_relu, 1)

        def load_head(h):
            act.dma_start(uk[:, h % 2, :], io["dsa_w_uk"][h]).then_inc(uk_here[h % 2], 16)
            act.dma_start(uv[:, h % 2, :, :], io["dsa_w_uv"][h]).then_inc(uk_here[h % 2], 16)

        act.wait_ge(GD.sem, GD.at(GH - 1, "y1"))
        load_head(0)
        load_head(1)
        for item in SEQ_D:
            kind = item[0]
            if kind == "ga":
                n = item[1]
                act.activation(bh[:, n, :], gr[:, n, :], ACT.Copy).then_inc(ga_hi, 1)
            elif kind == "lin":
                w = item[1]
                if w < W_A:
                    act.wait_ge(ga_lo, w - W_ZA + 1)
                    evac(w, w % 4, gr[:, w - W_ZA, :], ACT.Sigmoid)
            elif kind == "qlat":
                h = item[1]
                act.wait_ge(DP_q, h + 1)
                for c in range(2):
                    ins = act.activation(qlat[:, c, :], aux[2 + c], ACT.Copy)
                ins.then_inc(DA_q, 1)
            elif kind == "score":
                i = item[1]
                n = P * (i % TT + 1)
                act.wait_ge(DD.sem, DD.at(i, "max"))
                act.activation(prob[:, i % 2, 0:n], prob[:, i % 2, 0:n], ACT.Exp, bias=rowstat[:, 0, i:i + 1],
                               accum_out=rowstat[:, 1, i:i + 1]).then_inc(DA_e, 1)
                act.wait_ge(DD.sem, DD.at(i, "inv"))
                act.activation(prob[:, i % 2, 0:n], prob[:, i % 2, 0:n], ACT.Copy, scale=rowstat[:, 2, i:i + 1])\
                    .then_inc(DA_n, 1)
            elif kind == "out":
                h = item[1]
                act.wait_ge(DP_o, h + 1)
                for c in range(2):
                    ins = act.activation(olat[:, c, :], aux[2 + c], ACT.Copy)
                ins.then_inc(DA_o, 1)
                act.wait_ge(DP_v, h + 1)
                act.activation(qk[:, h, :], aux[2], ACT.Copy).then_inc(DA_v, 1)
                if h + 2 < DH:
                    load_head(h + 2)

        act.wait_ge(evacuated, W_ZB)
        act.wait_ge(DA_v, DH)
        for n in range(KT):
            act.activation(bh[:, n, :], qk[:, n, :], ACT.Copy).then_inc(db_hi, 1)
        evac_loop(W_ZB, 8, zb, ACT.Sigmoid)
        for n in range(KT):
            act.wait_ge(y_step, n + 1)
            act.activation(ah[:, n, :], gr[:, n, :], ACT.Copy).then_inc(y_hi, 1)
        norm(1, evacuated, W_O, split=1, shift=shift2)

        for h in range(PH):
            for side in range(2):
                w = W_Q + 2 * h + side
                if h == 0 and side == 0:
                    act.wait_ge(evacuated, W_Q)
                if h >= 2:
                    act.wait_ge(ps_mm, 2 * (h - 2) + side + 1)
                act.wait_ge(tile_done, w + 1)
                act.activation(pq[:, h % 2, side, :], acc[w % 4], ACT.Copy).then_inc(evacuated, 1)
            act.wait_ge(sel, NSEL * h + SEL_SHIFTED)
            act.activation(bexp[:, :, :], bexp[:, :, :], ACT.Exp).then_inc(sel_exp, 1)

        def table(g, first):
            for q in range(TG // 4):
                act.wait_ge(table_mm, 16 * g + q + 1)
                if q == 0 and not first:
                    act.wait_ge(table_stored, 16 * g)
                act.activation(stage[:, :, 4 * q:4 * q + 4].rearrange("p b t -> p t b"),
                               aux[q % 4].rearrange("p (t b) -> p t b", t=4), ACT.Copy).then_inc(table_out, 1)
            act.wait_ge(table_out, 16 * g + 16)
            act.dma_start(item_of(gate_table, g), stage[:, :, :].rearrange("p b t -> p (b t)"))\
                .then_inc(table_stored, 16)
        table(0, True)
        with act.Fori(1, S // TG) as g:
            table(g, False)

        act.wait_ge(table_stored, 16 * S // TG)

        def chunk(g, half):
            w = W_UV + 32 * g + 16 * half
            i0 = 2 * ET * g + ET * half
            act.wait_ge(evacuated, w)
            for e in range(ET):
                act.wait_ge(tile_done, w + e + 1)
                act.activation(act_g[:, e % 2, :], acc[e % 4], ACT.Gelu).then_inc(evacuated, 1)
                act.wait_ge(e_mul, i0 + e + 1)
                act.activation(eh[:, e, :], act_m[:, e % 2, :], ACT.Copy).then_inc(e_hi, 1)
        with act.Fori(0, NCHUNK // 2) as g:
            for half in range(2):
                chunk(g, half)
        norm(2, x_ready, 0)
        norm(3, nout_done, 0, split=2)

        for half in range(2):
            w = W_POOL + 32 * half
            act.wait_ge(evacuated, w)
            for n in range(8):
                i = 8 * half + n
                act.wait_ge(const_dve, 3)
                if i >= 2:
                    act.wait_ge(pl_step, PL_END[i - 2])
                evac(w + n, n % 4, ub[:, n % 2, 16:16 + S])
                act.wait_ge(pl_step, PL_END[i])
                act.activation(ch[:, n, :], um[:, n % 2, :], ACT.Copy).then_inc(pl_hi, 1)
            evac_loop(w + 8, 8, zs, ACT.Silu)
            for n in range(8):
                act.wait_ge(evacuated, w + 17 + n)
                act.activation(dh[:, n, :], um[:, n % 2, :], ACT.Copy).then_inc(pw_hi, 1)
        norm(4, evacuated, W_SB - 8, split=3)

        for half in range(2):
            w = W_SB + 32 * half
            act.wait_ge(evacuated, w)
            evac_loop(w, 8, sqk)
            evac_tokens(w + 8, 2, sv)
            for hd in range(8):
                i = 8 * half + hd
                act.wait_ge(SP_.sem, SP_.at(i, "qk"))
                if i:
                    act.wait_ge(SP_.sem, SP_.at(i - 1, "o"))
                act.activation(st[:, :], aux3, ACT.Abs, scale=0.125).then_inc(SA.sem, 1)
                act.wait_ge(SA.sem, SA.at(i, "abs"))
                act.activation(st[:, :], st[:, :], ACT.Exp, scale=-1.0).then_inc(SA.sem, 1)
                act.wait_ge(SA.sem, SA.at(i, "exp"))
                act.activation(st[:, :], st[:, :], ACT.Ln, bias=one[:, :]).then_inc(SA.sem, 1)
                evac(w + 16 + hd, 0, zs[:, hd, :], ACT.Silu)
                act.wait_ge(SD.sem, SD.at(i, "mask"))
                act.activation(slh[:, :], slo[:, :], ACT.Copy).then_inc(SA.sem, 1)
                act.wait_ge(SD.sem, SD.at(i, "sum"))
                act.activation(st[:, :], slb[:, :], ACT.Exp).then_inc(SA.sem, 1)
                act.wait_ge(SD.sem, SD.at(i, "y"))
                act.activation(ch[:, hd, :], sy[:, :], ACT.Copy).then_inc(SA.sem, 1)
        norm(5, evacuated, W_END - 8)
        for k in range(KT):
            act.wait_ge(nout_done, KT + k + 1)
            act.dma_start(io["out"][:, k, :], outT[:, k, :]).then_inc(out_stored, 16)
        act.wait_ge(out_stored, 16 * KT)

    @block.vector
    def _(dve):
        def tt(out, a, b, op):
            return dve.tensor_tensor(out, a, b, op)

        def stt(out, a, s, b, op0, op1):
            return dve.scalar_tensor_tensor(out=out, in0=a, scalar=s, in1=b, op0=op0, op1=op1)

        def norm(o, gain, split=None, shift=None, dst=None, out=0):
            dve.wait_ge(nstd_done, o + 1)
            dve.reciprocal(nrs[:, :], nstd[:, :]).then_inc(ninv_done, 1)
            dve.wait_ge(ninv_done, o + 1)
            for k in range(KT + 1):
                if split is None:
                    if k < KT:
                        stt(dst[:, k, :], xT[:, k, :], gain[:, k:k + 1], nrs[:, :], ALU.mult, ALU.mult)\
                            .then_inc(nout_done, 1)
                    continue
                if k < KT:
                    if k >= 2:
                        dve.wait_ge(nlo_done, KT * split + k - 1)
                    stt(nxn[:, k % 2, :], xT[:, k, :], gain[:, k:k + 1], nrs[:, :], ALU.mult, ALU.mult)\
                        .then_inc(nxn_done, 1)
                if k:
                    dve.wait_ge(nhi_done, KT * split + k)
                    stt(al[:, k - 1, :], nxn[:, (k - 1) % 2, :], zero[:, 0:1] if shift is None else shift[:, k - 1:k],
                        ah[:, k - 1, :].bitcast(F32), ALU.add, ALU.subtract).then_inc(nlo_done, 1)

        dve.wait_ge(const_pool, NCONST)
        dve.wait_ge(small_here, NSMALL)
        dve.wait_ge(ada_used, NADA)
        tt(ada[:, :], psum[:, 7, 0:NADA], VEC["b_ada"], ALU.add).then_inc(ada_done, 1)
        dve.wait_ge(ada_done, 1)
        stt(gs[:, 0, :], scale1, 1.0, VEC["norm1_g"], ALU.add, ALU.mult).then_inc(const_vec, 1)
        stt(gs[:, 1, :], scale2, 1.0, VEC["norm2_g"], ALU.add, ALU.mult).then_inc(const_vec, 1)
        dve.wait_ge(const_vec, 2)
        for n, window in enumerate(WINDOWS):
            dve.tensor_scalar(inv_count[:, n, :], iota16[:, :], 1.0, float(window), ALU.add, ALU.min).then_inc(const_vec, 1)
        dve.wait_ge(const_vec, 6)
        dve.reciprocal(inv_count[:, :, :], inv_count[:, :, :]).then_inc(const_dve, 1)
        dve.wait_ge(const_dve, 1)
        norm(0, gs[:, 0, :], split=0, shift=shift1)


        top = [0]

        def chain(ins):
            top[0] += 1
            ins.then_inc(top_step, 1)
            dve.wait_ge(top_step, top[0])

        for item in SEQ_G:
            kind = item[0]
            if kind == "ckv":
                dve.wait_ge(CA.sem, CA.at(0, "std"))
                dve.reciprocal(nrs[:, :], nstd[:, :]).then_inc(CD.sem, 1)
                dve.wait_ge(CD.sem, CD.at(0, "rstd"))
                for k in range(2):
                    stt(ckv[:, k, :], ckv[:, k, :], VEC["dsa_kv_norm_g"][:, k:k + 1], nrs[:, :], ALU.mult, ALU.mult)\
                        .then_inc(CD.sem, 1)
                dve.wait_ge(CP.sem, CP.at(0, "iw"))
                dve.tensor_scalar(iwn[:, :, :], aux[3].rearrange("p (t n) -> p t n", t=TT)[:, :, 32:32 + IH],
                                  IH ** -0.5, None, ALU.mult).then_inc(CD.sem, 1)
                dve.wait_ge(CD.sem, CD.at(0, "c1"))
                dve.memset(gat[:, :, :], 0.0).then_inc(const_vec, 1)
                dve.wait_ge(const_vec, 7)
                dve.wait_ge(evacuated, W_G)
            elif kind == "prep":
                h = item[1]
                m = gt1[:, 1, :]
                dve.wait_ge(GP.sem, GP.at(h, "gate"))
                dve.wait_ge(GA.sem, GA.at(h, "abs"))
                dve.tensor_scalar(m, aux[0], VEC["gla_b_gate"][:, h:h + 1], 0.0, ALU.add, ALU.min).then_inc(GD.sem, 1)
                dve.wait_ge(GD.sem, GD.at(h, "min"))
                dve.wait_ge(GA.sem, GA.at(h, "ln"))
                tt(m, m, gt1[:, 0, :], ALU.subtract).then_inc(GD.sem, 1)
                dve.wait_ge(GD.sem, GD.at(h, "logalpha"))
                dve.tensor_tensor_scan(gb[:, :], chunk_start[:, :], m, 0.0, ALU.mult, ALU.add).then_inc(GD.sem, 1)
                dve.wait_ge(GD.sem, GD.at(h, "cumsum"))
                b3 = gb[:, :].rearrange("p (c t) -> p c t", t=CH)
                tt(gke[:, :].rearrange("p (c t) -> p c t", t=CH), b3[:, :, CH - 1:CH].broadcast_to([P, S // CH, CH]),
                   b3, ALU.subtract).then_inc(GD.sem, 1)
                dve.wait_ge(GA.sem, GA.at(h, "eb"))
                stt(gqd[:, :], qk[:, 2 * h, :], GDK ** -0.5, geb[:, :], ALU.mult, ALU.mult).then_inc(GD.sem, 1)
                dve.wait_ge(GA.sem, GA.at(h, "enb"))
                tt(gki[:, :], gki[:, :], qk[:, 2 * h + 1, :], ALU.mult).then_inc(GD.sem, 1)
                dve.wait_ge(GA.sem, GA.at(h, "ekd"))
                tt(gke[:, :], gke[:, :], qk[:, 2 * h + 1, :], ALU.mult).then_inc(GD.sem, 1)
            elif kind == "attn":
                h = item[1]
                dve.wait_ge(GP.sem, GP.at(h, "attn"))
                dve.copy_predicated(gat[:, :, :], block_causal[:, :].bitcast(U32).unsqueeze(1).broadcast_to([P, TT, P]),
                                    aux[1].rearrange("p (t n) -> p t n", t=TT)).then_inc(GD.sem, 1)
            elif kind == "kv":
                h, t = item[1:]
                dve.wait_ge(GP.sem, GP.at(h, f"kv{t}"))
                for c in range(2 * t, min(2 * t + 2, 7)):
                    new = aux[2 - c % 2][:, 0:GDV]
                    if c == 0:
                        dve.tensor_copy(gst[:, 0, :], new).then_inc(GD.sem, 1)
                    else:
                        dve.wait_ge(GD.sem, GD.at(h, f"s{c}"))
                        stt(gst[:, c, :], gst[:, c - 1, :], geb[:, CH * c + CH - 1:CH * c + CH], new,
                            ALU.mult, ALU.add).then_inc(GD.sem, 1)
            elif kind == "o":
                h = item[1]
                dve.wait_ge(GA.sem, GA.at(h, "std"))
                dve.reciprocal(gke[:, :], gke[:, :]).then_inc(GD.sem, 1)
                dve.wait_ge(GD.sem, GD.at(h, "rstd"))
                dve.wait_ge(evacuated, W_G + 4 * h + 2)
                for v in range(2):
                    stt(gt1[:, v, :], aux[1 - v], VEC["gla_norm_g"][:, 2 * h + v:2 * h + v + 1], gke[:, :],
                        ALU.mult, ALU.mult).then_inc(GD.sem, 1)
                for v in range(2):
                    dve.wait_ge(GD.sem, GD.at(h, f"og{v}"))
                    tt(gr[:, 2 * h + v, :], gr[:, 2 * h + v, :], gt1[:, v, :], ALU.mult).then_inc(GD.sem, 1)
            elif kind == "idx":
                t, h = item[1:]
                i = (t - 1) * IH + h
                n = P * (t + 1)
                dve.wait_ge(idx_relu, i + 1)
                dve.wait_ge(CD.sem, CD.at(0, "iw"))
                if h == 0:
                    dve.tensor_scalar(score[:, 0:n], rel[:, i % 2, 0:n], iwn[:, t, h:h + 1], None, ALU.mult)\
                        .then_inc(idx_acc, 1)
                else:
                    dve.wait_ge(idx_acc, i)
                    stt(score[:, 0:n], rel[:, i % 2, 0:n], iwn[:, t, h:h + 1], score[:, 0:n], ALU.mult, ALU.add)\
                        .then_inc(idx_acc, 1)
            elif kind == "fill":
                t = item[1]
                dve.wait_ge(idx_acc, t * IH)
                chain(dve.copy_predicated(score[:, P * t:P * t + P], strict[:, :].bitcast(U32), neg[:, :]))
            elif kind == "top":
                n = P * (item[1] + 1)
                chain(dve.max(m8[:, :], score[:, 0:n]))
                chain(dve.match_replace(score[:, 0:n], m8[:, :], score[:, 0:n], TAKEN))
            elif kind == "mask":
                t = item[1]
                n = P * (t + 1)
                if t == 0:
                    chain(dve.memset(maskneg[:, 0, 0:P], 0.0))
                else:
                    chain(dve.tensor_scalar(maskneg[:, t, 0:n], score[:, 0:n], -1e38, NEG, ALU.is_ge, ALU.mult))
                chain(dve.copy_predicated(maskneg[:, t, P * t:P * t + P], strict[:, :].bitcast(U32), neg[:, :]))

        for item in SEQ_D:
            kind = item[0]
            if kind == "ga":
                n = item[1]
                dve.wait_ge(ga_hi, n + 1)
                tt(bl[:, n, :], gr[:, n, :], bh[:, n, :].bitcast(F32), ALU.subtract).then_inc(ga_lo, 1)
            elif kind == "lin":
                w = item[1]
                if w >= W_A:
                    n = w - W_A
                    if n == 0:
                        dve.wait_ge(evacuated, W_A)
                    dve.wait_ge(tile_done, w + 1)
                    tt(gr[:, n, :], acc[w % 4], gr[:, n, :], ALU.mult).then_inc(evacuated, 1)
            elif kind == "score":
                i = item[1]
                h, t = divmod(i, TT)
                n = P * (t + 1)
                if i:
                    dve.wait_ge(DD.sem, DD.at(i - 1, "logit"))
                stt(tneg[:, 0:n], relpos[:, 384 - P * t:384 - P * t + n], 2.0 ** -(h + 1), maskneg[:, t, 0:n],
                    ALU.mult, ALU.add).then_inc(DD.sem, 1)
                dve.wait_ge(DD.sem, DD.at(i, "bias"))
                dve.wait_ge(DP_s, i + 1)
                if i >= 2:
                    dve.wait_ge(DP_t, i - 1)
                stt(prob[:, i % 2, 0:n], aux[0][:, 0:n], P ** -0.5, tneg[:, 0:n], ALU.mult, ALU.add)\
                    .then_inc(DD.sem, 1)
                dve.wait_ge(DD.sem, DD.at(i, "logit"))
                dve.tensor_reduce(rowstat[:, 0, i:i + 1], prob[:, i % 2, 0:n], AX.X, ALU.max, negate=True)\
                    .then_inc(DD.sem, 1)
                dve.wait_ge(DA_e, i + 1)
                dve.reciprocal(rowstat[:, 2, i:i + 1], rowstat[:, 1, i:i + 1]).then_inc(DD.sem, 1)
            elif kind == "pt":
                i = item[1]
                t = i % TT
                dve.wait_ge(DP_t, i + 1)
                if i >= TT and t == 0:
                    dve.wait_ge(DP_o, i // TT)
                dve.tensor_copy(pT[:, 0:t + 1, P * t:P * t + P],
                                aux[1][:, 0:P * (t + 1)].rearrange("p (b n) -> p b n", n=P)).then_inc(pT_out, 1)

        for n in range(KT):
            dve.wait_ge(db_hi, n + 1)
            tt(bl[:, n, :], qk[:, n, :], bh[:, n, :].bitcast(F32), ALU.subtract).then_inc(db_lo, 1)
        dve.wait_ge(evacuated, W_B)
        for n in range(KT + 1):
            if n < KT:
                w = W_B + n
                dve.wait_ge(tile_done, w + 1)
                tt(zb[:, n, :], acc[w % 4], zb[:, n, :], ALU.mult).then_inc(evacuated, 1)
                dve.wait_ge(evacuated, w + 1)
                tt(gr[:, n, :], gr[:, n, :], zb[:, n, :], ALU.add).then_inc(y_step, 1)
            if n:
                dve.wait_ge(y_hi, n)
                tt(al[:, n - 1, :], gr[:, n - 1, :], ah[:, n - 1, :].bitcast(F32), ALU.subtract).then_inc(y_lo, 1)
        for n in range(KT):
            w = W_O + n
            dve.wait_ge(tile_done, w + 1)
            stt(xT[:, n, :], acc[w % 4], gate1[:, n:n + 1], xT[:, n, :], ALU.mult, ALU.add).then_inc(evacuated, 1)
        norm(1, gs[:, 1, :], split=1, shift=shift2)

        for h in range(PH):
            n = [NSEL * h]

            def step(ins):
                n[0] += 1
                return ins.then_inc(sel, 1)

            def settle():
                dve.wait_ge(sel, n[0])

            pairs = [(side, t) for side in range(2) for t in range(TT)]
            scores = [psum[:, 4 + 2 * (h % 2) + side, :] for side in range(2)]
            dve.wait_ge(ps_mm, 2 * h + 2)
            for side, t in pairs:
                step(dve.max(topv[:, side, t, 0:8], scores[side][:, P * t:P * t + P]))
            settle()
            for side, t in pairs:
                step(dve.max_index(topi[:, side, t, 0:8], topv[:, side, t, 0:8], scores[side][:, P * t:P * t + P]))
            for side, t in pairs:
                step(dve.match_replace(swork[:, side, t, :], topv[:, side, t, 0:8], scores[side][:, P * t:P * t + P],
                                       TAKEN))
            settle()
            for side, t in pairs:
                step(dve.max(topv[:, side, t, 8:16], swork[:, side, t, :]))
            settle()
            for side, t in pairs:
                step(dve.max_index(topi[:, side, t, 8:16], topv[:, side, t, 8:16], swork[:, side, t, :]))
            grid = [P, TT, PK, PK]
            step(tt(cand[:, :, :].rearrange("p t (a b) -> p t a b", a=PK), topv[:, 0, :, :].unsqueeze(3).broadcast_to(grid),
                    topv[:, 1, :, :].unsqueeze(2).broadcast_to(grid), ALU.add))
            settle()
            step(dve.tensor_copy(topf[:, :, :, :].rearrange("p s t k -> p (s t k)"),
                                 topi[:, :, :, :].rearrange("p s t k -> p (s t k)")))
            for t in range(TT):
                step(dve.max(best[:, t, 0:8], cand[:, t, :]))
            settle()
            for t in range(TT):
                step(dve.max_index(besti[:, t, 0:8], best[:, t, 0:8], cand[:, t, :]))
            settle()
            for t in range(TT):
                step(dve.match_replace(cand[:, t, :], best[:, t, 0:8], cand[:, t, :], TAKEN))
            settle()
            for t in range(TT):
                step(dve.max(best[:, t, 8:16], cand[:, t, :]))
            settle()
            for t in range(TT):
                step(dve.max_index(besti[:, t, 8:16], best[:, t, 8:16], cand[:, t, :]))
            step(tt(bexp[:, :, :], best[:, :, :], best[:, :, 0:1].broadcast_to([P, TT, PK]), ALU.subtract))
            assert n[0] == NSEL * h + SEL_SHIFTED
            settle()
            step(dve.tensor_scalar(bestij[:, 0, :, :], besti[:, :, :], 4, None, ALU.logical_shift_right))
            step(dve.tensor_scalar(bestij[:, 1, :, :], besti[:, :, :], 15, None, ALU.bitwise_and))
            settle()
            step(dve.tensor_copy(bestf[:, :, :, :].rearrange("p s t k -> p (s t k)"),
                                 bestij[:, :, :, :].rearrange("p s t k -> p (s t k)")))
            settle()
            for side in range(2):
                step(tt(onehot[:, :, :], bestf[:, side, :, :].rearrange("p t k -> p (t k)").unsqueeze(2)
                        .broadcast_to([P, TT * PK, PK]), iota16[:, :].unsqueeze(1).broadcast_to([P, TT * PK, PK]),
                        ALU.is_equal))
                settle()
                hot4 = onehot[:, :, :].rearrange("p (t k) j -> p t k j", t=TT)
                step(tt(hot4, hot4, topf[:, side, :, :].unsqueeze(2).broadcast_to(grid), ALU.mult))
                settle()
                step(dve.tensor_reduce(slots[:, side, :, PK * h:PK * h + PK], hot4, AX.X, ALU.add))
                settle()
            dve.wait_ge(sel_exp, h + 1)
            step(dve.tensor_reduce(bsum[:, :], bexp[:, :, :], AX.X, ALU.add))
            settle()
            step(dve.reciprocal(binv[:, :], bsum[:, :]))
            settle()
            step(tt(slots[:, 2, :, PK * h:PK * h + PK], bexp[:, :, :], binv[:, :].unsqueeze(2).broadcast_to([P, TT, PK]),
                    ALU.mult))
            assert n[0] == NSEL * (h + 1)

        for part in range(2):
            dve.wait_ge(sT_mm, part + 1)
            dve.tensor_copy(slotT[:, part, :], aux[part]).then_inc(sT_step, 1)
        dve.wait_ge(sT_mm, 3)
        dve.tensor_copy(gpart[:, 0, :], aux[2]).then_inc(sT_step, 1)
        for part in range(2):
            dve.wait_ge(sT_step, 3 + 2 * part)
            dve.tensor_copy(gp16[:, part, :], gpart[:, part, :]).then_inc(sT_step, 1)
            dve.wait_ge(sT_step, 4 + 2 * part)
            tt(gpart[:, part + 1, :], gpart[:, part, :], gp16[:, part, :], ALU.subtract).then_inc(sT_step, 1)
        dve.wait_ge(sT_step, 7)

        def one_hots(g, first):
            for b in range(TG // 8):
                if not (first and b < 2):
                    dve.wait_ge(table_mm, 16 * g + 2 * b - 2)
                for u in range(8):
                    tok = bass.ds(TG * g + 8 * b + u, 1)
                    dve.tensor_scalar(hot[:, b % 2, u, 0, :], iota_row[:, :], slotT[:, 0, tok], None, ALU.is_equal)
                    for part in range(3):
                        ins = dve.tensor_scalar(hot[:, b % 2, u, 1 + part, :], iota_row[:, :], slotT[:, 1, tok],
                                                gpart[:, part, tok], ALU.is_equal, ALU.mult)
                ins.then_inc(hot_done, 1)
        one_hots(0, True)
        with dve.Fori(1, S // TG) as g:
            one_hots(g, False)

        dve.wait_ge(table_stored, 16 * S // TG)
        dve.memset(yT[:, :, :], 0.0).then_inc(y_zero, 1)
        dve.wait_ge(y_zero, 1)
        with dve.Fori(0, NCHUNK // 2) as g:
            for half in range(2):
                w = W_UV + 32 * g + 16 * half
                i0 = 2 * ET * g + ET * half
                dve.wait_ge(gt_here[half], 16 * g + 16)
                for e in range(ET):
                    dve.wait_ge(evacuated, w + e + 1)
                    tt(act_m[:, e % 2, :].rearrange("p (g t) -> p g t", t=TG),
                       act_g[:, e % 2, :].rearrange("p (g t) -> p g t", t=TG), gt[:, half, :, TG * e:TG * e + TG],
                       ALU.mult).then_inc(e_mul, 1)
                    dve.wait_ge(e_hi, i0 + e + 1)
                    tt(el[:, e, :], act_m[:, e % 2, :], eh[:, e, :].bitcast(F32), ALU.subtract).then_inc(e_lo, 1)
                for hf in range(2):
                    dve.wait_ge(tile_done, w + ET + 4 * hf + 4)
                    for d in range(4):
                        tt(yT[:, 4 * hf + d, :], acc[d], yT[:, 4 * hf + d, :], ALU.add).then_inc(evacuated, 1)
        dve.wait_ge(evacuated, W_POOL)
        for n in range(KT):
            stt(xT[:, n, :], yT[:, n, :], gate2[:, n:n + 1], xT[:, n, :], ALU.mult, ALU.add).then_inc(x_ready, 1)
        dve.wait_ge(x_ready, KT)
        norm(2, VEC["final_norm_g"], dst=xT)
        dve.wait_ge(nout_done, KT)
        norm(3, VEC["norm_g0"], split=2)

        dve.wait_ge(nlo_done, 3 * KT)
        dve.memset(ub[:, :, 0:16], 0.0).then_inc(const_dve, 1)
        dve.memset(us[:, :, 0:16], 0.0).then_inc(const_dve, 1)
        dve.wait_ge(const_dve, 3)
        n_step = 0
        for half in range(2):
            w = W_POOL + 32 * half
            for n in range(8):
                i = 8 * half + n
                which = 2 * half + n // 4
                window = WINDOWS[which]
                u, src, m = ub[:, n % 2, :], ub[:, n % 2, :], um[:, n % 2, :]
                dve.wait_ge(evacuated, w + n + 1)
                for level in range(which + 1):
                    dst = us[:, level % 2, :]
                    tt(dst[:, 16:16 + S], src[:, 16:16 + S], src[:, 16 - 2 ** level:16 + S - 2 ** level], ALU.add)\
                        .then_inc(pl_step, 1)
                    n_step += 1
                    dve.wait_ge(pl_step, n_step)
                    src = dst
                stt(m[:, 16:S], src[:, 32:16 + S], 1.0 / window, u[:, 32:16 + S], ALU.mult, ALU.subtract)\
                    .then_inc(pl_step, 1)
                tt(m[:, 0:16], src[:, 16:32], inv_count[:, which, :], ALU.mult).then_inc(pl_step, 1)
                n_step += 2
                dve.wait_ge(pl_step, n_step)
                tt(m[:, 0:16], m[:, 0:16], u[:, 16:32], ALU.subtract).then_inc(pl_step, 1)
                n_step += 1
                assert n_step == PL_END[i]
                dve.wait_ge(pl_hi, i + 1)
                tt(cl[:, n, :], m, ch[:, n, :].bitcast(F32), ALU.subtract).then_inc(pl_lo, 1)
            dve.wait_ge(evacuated, w + 16)
            for n in range(8):
                m = um[:, n % 2, :]
                dve.wait_ge(tile_done, w + 17 + n)
                stt(m, acc[n % 4], VEC["pool_scale"][:, 8 * half + n:8 * half + n + 1], zs[:, n, :], ALU.mult, ALU.mult)\
                    .then_inc(evacuated, 1)
                dve.wait_ge(pw_hi, 8 * half + n + 1)
                tt(dl[:, n, :], m, dh[:, n, :].bitcast(F32), ALU.subtract).then_inc(pw_lo, 1)
            for n in range(8):
                dve.wait_ge(tile_done, w + 25 + n)
                tt(xT[:, n, :], acc[n % 4], xT[:, n, :], ALU.add).then_inc(evacuated, 1)
        norm(4, VEC["norm_g1"], split=3)

        diag = strict[:, :].unsqueeze(1).broadcast_to([P, TT, P])
        for half in range(2):
            w = W_SB + 32 * half
            for hd in range(8):
                i = 8 * half + hd
                dve.wait_ge(SP_.sem, SP_.at(i, "qk"))
                dve.wait_ge(SA.sem, SA.at(i, "abs"))
                dve.tensor_scalar(slb[:, :], aux3, 0.125, 0.0, ALU.mult, ALU.min).then_inc(SD.sem, 1)
                dve.wait_ge(SD.sem, SD.at(i, "min"))
                dve.wait_ge(SA.sem, SA.at(i, "ln"))
                tt(slb[:, :], slb[:, :], st[:, :], ALU.subtract).then_inc(SD.sem, 1)
                dve.wait_ge(SD.sem, SD.at(i, "lb"))
                stt(slo[:, :], aux3, -0.125, slb[:, :], ALU.mult, ALU.add).then_inc(SD.sem, 1)
                dve.wait_ge(SD.sem, SD.at(i, "lo"))
                square = slo[:, 0:S].rearrange("p (b n) -> p b n", n=P)
                tt(square, square, diag, ALU.mult).then_inc(SD.sem, 1)
                dve.wait_ge(SD.sem, SD.at(i, "mask"))
                dve.wait_ge(SA.sem, SA.at(i, "hi"))
                tt(sll[:, :], slo[:, :], slh[:, :].bitcast(F32), ALU.subtract).then_inc(SD.sem, 1)
                dve.wait_ge(SP_.sem, SP_.at(i, "cum"))
                tt(slb[:, :], acc3, slb[:, :], ALU.add).then_inc(SD.sem, 1)
                dve.wait_ge(SA.sem, SA.at(i, "a"))
                square = st[:, 0:S].rearrange("p (b n) -> p b n", n=P)
                tt(square, square, diag, ALU.mult).then_inc(SD.sem, 1)
                dve.wait_ge(SP_.sem, SP_.at(i, "o"))
                dve.wait_ge(evacuated, w + 16 + hd + 1)
                tt(sy[:, :], aux[3], zs[:, hd, :], ALU.mult).then_inc(SD.sem, 1)
                dve.wait_ge(SA.sem, SA.at(i, "yhi"))
                tt(cl[:, hd, :], sy[:, :], ch[:, hd, :].bitcast(F32), ALU.subtract).then_inc(SD.sem, 1)
            for n in range(8):
                dve.wait_ge(tile_done, w + 25 + n)
                tt(xT[:, n, :], acc[n % 4], xT[:, n, :], ALU.add).then_inc(evacuated, 1)
        norm(5, VEC["norm_f"], dst=outT)

    block_cm.__exit__(None, None, None)


def _tiles(w):
    k, n = w.shape[0] // 128, w.shape[1] // 128
    return w.reshape(k, 128, n, 128).transpose(2, 1, 0, 3).reshape(n, 128, k * 128)


def _token_tiles(w):
    n = w.shape[1] // 512
    return w.reshape(4, 2, 128, n, 512).transpose(3, 0, 2, 1, 4).reshape(4 * n, 128, 1024)


def _columns(v):
    return v.reshape(-1, 128).T


def _layout(i):
    import numpy as np

    cut = np.cumsum((512, 512, 1024, 1024, 16, 1024, 256, 512, 64, 8, 1024))
    gq, gk, gv, gr, glow, dq, dkv, iq, ik, iw, za, zb = np.split(i["w_in"][0], cut, axis=1)
    cat = np.concatenate
    head = lambda w, h, n=128: w[:, n * h:n * h + n]
    w_in = cat([
        _tiles(cat([glow, glow] + [iw] * 12, axis=1)), _tiles(cat([ik, ik], axis=1)), _tiles(dkv),
        _tiles(cat([head(w, h) for h in range(4) for w in (gq, gk)], axis=1)),
        _token_tiles(gv), _tiles(iq),
        *[_tiles(cat([head(gr, h, 256), head(dq, h, 256)], axis=1)) for h in range(4)],
        _tiles(za), _tiles(zb),
    ])
    vec = cat([_columns(v) for v in (
        i["b_ada"][0], i["norm1_g"][0], i["norm2_g"][0], i["final_norm_g"], i["gla_b_gate"][0], i["gla_norm_g"][0],
        i["dsa_kv_norm_g"][0], i["norm_g_2"][0], i["norm_g_2"][1], i["norm_f_2"], i["pool_scale_2"][0])], axis=1)
    xb, z = np.split(i["pool_w_in_2"][0], 2, axis=1)
    pool_in = cat([_tiles(w[:, 1024 * h:1024 * h + 1024]) for h in range(2) for w in (xb, z)])
    pool_w = cat([_tiles(w) for w in i["pool_w_2"][0]])
    halves = lambda w: cat([_tiles(w[1024 * h:1024 * h + 1024]) for h in range(2)])
    q, k, v, z = np.split(i["sb_w_in_2"][0], (1024, 2048, 4096), axis=1)
    sb_in = cat([t for h in range(2) for t in (
        _tiles(q[:, 512 * h:512 * h + 512]), _tiles(k[:, 512 * h:512 * h + 512]),
        _token_tiles(v[:, 1024 * h:1024 * h + 1024]), _tiles(z[:, 1024 * h:1024 * h + 1024]))])
    u = i["peer_u"][0].reshape(128, 128, 8, 128).transpose(1, 3, 2, 0).reshape(128, 128, 1024)
    v = i["peer_v"][0].reshape(128, 16, 4, 2, 2, 512).transpose(1, 4, 2, 0, 3, 5).reshape(128, 128, 1024)
    return {
        "x": i["x"][0].T.reshape(8, 128, 512).transpose(1, 0, 2),
        "c": _columns(i["c"][0]),
        "vec": vec,
        "w_ada": _tiles(i["w_ada"][0]),
        "w_in": w_in,
        "gla_w_gate_up": i["gla_w_gate_up"][0],
        "dsa_w_uk": i["dsa_w_uk"][0],
        "dsa_w_uv": i["dsa_w_uv"][0].reshape(8, 2, 128, 128).transpose(0, 2, 1, 3),
        "w_branch_a": _tiles(i["w_branch_a"][0]),
        "w_branch_b": _tiles(i["w_branch_b"][0]),
        "w_out": _tiles(i["w_out"][0]),
        "peer_w_q": _tiles(i["peer_w_q"][0]),
        "peer_sub_keys": np.stack([i["peer_sub_keys_1"][0].T, i["peer_sub_keys_2"][0].T], axis=1),
        "peer_u": u,
        "peer_v": v,
        "pool_w_in": pool_in,
        "pool_w": pool_w,
        "pool_w_out": halves(i["pool_w_out_2"][0]),
        "sb_w_in": sb_in,
        "sb_w_out": halves(i["sb_w_out_2"][0]),
    }


def kernel(**inputs):
    import numpy as _np
    import concourse.bacc as _bacc
    from concourse.bass_utils import run_bass_kernel_spmd as _run

    nc = _bacc.Bacc("TRN2", target_bir_lowering=False, num_devices=1)
    arrays, io = {}, {}
    for name, a in _layout({k: _np.asarray(v) for k, v in inputs.items()}).items():
        a = _np.ascontiguousarray(a)
        arrays[f"in_{name}"] = a
        io[name] = nc.dram_tensor(f"in_{name}", a.shape, mybir.dt.from_np(a.dtype), kind="ExternalInput").ap()
    io["out"] = nc.dram_tensor("out", (128, 8, 512), F32, kind="ExternalOutput").ap()
    build(nc, io)
    r = _run(nc, [arrays], core_ids=[0])
    out = r.results[0]["out"]
    return _np.ascontiguousarray(out.transpose(1, 0, 2).reshape(1024, 512).T)[None]
```

```python
import concourse.bass as bass
from concourse import mybir

P = 128
F32 = mybir.dt.float32
F32R = mybir.dt.float32r
BF16 = mybir.dt.bfloat16
U32 = mybir.dt.uint32
I32 = mybir.dt.int32
ACT = mybir.ActivationFunctionType
ALU = mybir.AluOpType
AX = mybir.AxisListType

S = 512
TT = S // P
D = 1024
KT = D // P
EPS = 1e-6

GH, GDK, GDV, CH = 4, 128, 256, 64
TAU = 16.0
DH, LAT, IH, IDD, TOPK = 8, 256, 8, 64, 128
PH, NK, PK = 8, 128, 16
ET = 8
NCHUNK = NK // ET
UH = 6
VEC_PARTS = (("b_ada", 48), ("norm1_g", 8), ("norm2_g", 8), ("final_norm_g", 8), ("gla_b_gate", 4),
             ("gla_norm_g", 8), ("dsa_kv_norm_g", 2), ("norm_g0", 8), ("norm_g1", 8), ("norm_f", 8),
             ("pool_scale", 16))
TG = 32
WINDOWS = (2, 4, 8, 16)
SBH = 16
NEG = -1e30
TAKEN = -3e38

NADA = 6 * KT
W_L1, W_G, W_ZA, W_A, W_ZB, W_B, W_O = 0, 24, 40, 48, 56, 64, 72
W_Q = 80
W_U = W_Q + PH * (2 + UH)
W_TAB = W_U + 8
W_V = W_Q + 2 * PH + NK
W_POOL = W_V + NK
W_SB = W_POOL + 64
W_END = W_SB + 64
RAW, SPLIT = 4, 2


NCONST = 20
NSMALL = 16 * 4
NSEL = 75
SEL_SHIFTED = 63
SB_REGIONS = [[(0, 0, 128), (512, 128, 384)], [(128, 128, 128), (1024, 256, 256)],
              [(256, 256, 128), (896, 384, 128)], [(384, 384, 128)]]


class Steps:

    def __init__(self, sem, *names):
        self.sem, self.names = sem, names

    def at(self, turn, name):
        return len(self.names) * turn + self.names.index(name) + 1


def schedule_gla():
    main = []
    for h in range(GH):
        w = W_G + 4 * h
        main += [("prep", h), ("lin", w), ("attn", h), ("lin", w + 1), ("kv", h, 0), ("kv", h, 1), ("lin", w + 2),
                 ("kv", h, 2), ("kv", h, 3), ("lin", w + 3), ("o", h)]
    side = [("mask", 0)]
    for tt in range(1, TT):
        side += [("idx", tt, h) for h in range(IH)] + [("fill", tt)]
        side += [("top", tt, r) for r in range(TOPK // 8)] + [("mask", tt)]
    out, done = [("ckv",)], 0
    for n, item in enumerate(main):
        out.append(item)
        upto = len(side) * (n + 1) // len(main)
        out += side[done:upto]
        done = upto
    return out


def schedule_dsa():
    steps = [("qlat", 0)]
    for i in range(DH * TT + 1):
        if i < DH * TT:
            steps.append(("score", i))
        if i >= 1:
            steps.append(("pt", i - 1))
            if i % TT == 0:
                steps.append(("out", i // TT - 1))
        if i % TT == TT - 1 and i // TT + 1 < DH:
            steps.append(("qlat", i // TT + 1))
    lin = [("lin", w) for w in range(W_ZA, W_A + KT)]
    out, done = [("ga", n) for n in range(KT)], 0
    for n, item in enumerate(steps):
        out.append(item)
        upto = len(lin) * (n + 1) // len(steps)
        out += lin[done:upto]
        done = upto
    return out


def build(nc, io):
    base = 16512

    def sb(name, shape, dt, kb):
        return nc.alloc_sbuf_tensor_at(name, shape, dt, offset=base + int(kb * 1024))

    xT = sb("xT", [P, KT, S], F32, 0)
    ah = sb("ah", [P, KT, S], F32R, 16)
    al = sb("al", [P, KT, S], F32R, 32)
    raw = [sb(f"raw{i}", [P, D], F32, 48 + 4 * i) for i in range(RAW)]
    wh = [sb(f"wh{i}", [P, D], F32R, 64 + 4 * i) for i in range(SPLIT)]
    wl = [sb(f"wl{i}", [P, D], F32R, 72 + 4 * i) for i in range(SPLIT)]
    cpos = [80.0]

    def const(name, shape, dt=F32):
        n = 1
        for d in shape[1:]:
            n *= d
        size = n * (2 if dt == BF16 else 4)
        t = sb(name, shape, dt, cpos[0])
        cpos[0] += (size + 31) // 32 * 32 / 1024
        return t

    ident = const("ident", [P, P])
    ones = const("ones", [P, P])
    onesr = const("onesr", [P, P], F32R)
    strict = const("strict", [P, P])
    block_causal = const("block_causal", [P, P])
    trilr = const("trilr", [P, P], F32R)
    neg = const("neg", [P, P])
    chunk_start = const("chunk_start", [P, S])
    iota_row = const("iota_row", [P, P], BF16)
    iota16 = const("iota16", [P, PK])
    zero = const("zero", [P, 8])
    eps = const("eps", [P, 1])
    one = const("one", [P, 1])
    ada = const("ada", [P, NADA])
    vec = const("vec", [P, io["vec"].shape[1]])
    cT = const("c_col", [P, KT])
    csil = const("csil", [P, KT])
    gs = const("gs", [P, 2, KT])
    inv_count = const("inv_count", [P, 4, 16])
    assert cpos[0] <= 89, cpos[0]
    VEC, at = {}, 0
    for name, n in VEC_PARTS:
        VEC[name] = vec[:, at:at + n]
        at += n
    ada_part = [ada[:, KT * i:KT * i + KT] for i in range(6)]
    shift1, scale1, gate1, shift2, scale2, gate2 = ada_part

    nsq = sb("nsq", [P, 2, S], F32, 169)
    nxn = sb("nxn", [P, 2, S], F32, 173)
    nstd = sb("nstd", [P, S], F32, 177)
    nrs = sb("nrs", [P, S], F32, 179)

    qk = sb("qk", [P, 2 * GH, S], F32, 89)
    gr = sb("gr", [P, KT, S], F32, 105)
    maskneg = sb("maskneg", [P, TT, S], F32, 121)
    ckv = sb("ckv", [P, 2, S], F32, 129)
    ckvn = sb("ckvn", [P, TT, LAT], F32, 133)
    gv = sb("gv", [P, TT, D], F32, 137)
    iq = sb("iq", [P, 4, S], F32, 153)
    ik = sb("ik", [P, S], F32, 161)
    misc = sb("misc", [P, S], F32, 163)
    gt1 = sb("gt1", [P, 2, S], F32, 165)
    gb = sb("gb", [P, S], F32, 169)
    geb = sb("geb", [P, S], F32, 171)
    gki = sb("gki", [P, S], F32, 173)
    gke = sb("gke", [P, S], F32, 175)
    gqd = sb("gqd", [P, S], F32, 177)
    gat = sb("gat", [P, TT, P], F32, 179)
    gket = sb("gket", [P, TT, P], F32, 181)
    gst = sb("gst", [P, 7, GDV], F32, 183)
    score = sb("score", [P, S], F32, 190)
    rel = sb("rel", [P, 2, S], F32, 192)
    iwn = sb("iwn", [P, TT, IH], F32, 196)
    m8 = sb("m8", [P, 8], F32, 197)
    relpos = sb("relpos", [P, 896], F32, 198)
    relpos_i = sb("relpos_i", [P, 896], I32, 190)
    gwu = sb("gwu", [16, GH * GDK], F32, 202)
    bh = sb("bh", [P, KT, S], F32R, 137)
    bl = sb("bl", [P, KT, S], F32R, 153)
    qlat = sb("qlat", [P, 2, S], F32, 169)
    uk = sb("uk", [P, 2, LAT], F32, 173)
    uv = sb("uv", [P, 2, 2, P], F32, 175)
    prob = sb("prob", [P, 2, S], F32, 177)
    tneg = sb("tneg", [P, S], F32, 181)
    pT = sb("pT", [P, TT, S], F32, 183)
    olat = sb("olat", [P, 2, S], F32, 191)
    rowstat = sb("rowstat", [P, 3, DH * TT], F32, 196.5)
    zb = sb("zb", [P, KT, S], F32, 169)
    pq = sb("pq", [P, 2, 2, S], F32, 89)
    keys = sb("keys", [P, 2, P], F32, 204)
    topv = sb("topv", [P, 2, TT, PK], F32, 98)
    topi = sb("topi", [P, 2, TT, PK], U32, 98.5)
    topf = sb("topf", [P, 2, TT, PK], F32, 99)
    swork = sb("swork", [P, 2, TT, P], F32, 100)
    cand = sb("cand", [P, TT, PK * PK], F32, 104)
    best = sb("best", [P, TT, PK], F32, 108)
    besti = sb("besti", [P, TT, PK], U32, 108.25)
    bestij = sb("bestij", [P, 2, TT, PK], U32, 108.5)
    bestf = sb("bestf", [P, 2, TT, PK], F32, 109)
    bexp = sb("bexp", [P, TT, PK], F32, 109.5)
    bsum = sb("bsum", [P, TT], F32, 109.75)
    binv = sb("binv", [P, TT], F32, 109.875)
    onehot = sb("onehot", [P, TT * PK, PK], F32, 110)
    slots = sb("slots", [P, 3, TT, PH * PK], F32, 114)
    slotT = sb("slotT", [P, 2, S], F32, 120)
    gp16 = sb("gp16", [P, 3, S], BF16, 124)
    gpart = sb("gpart", [P, 3, S], F32, 127)
    hot = sb("hot", [P, 2, 4, 8, P], BF16, 133)
    hotb = sb("hotb", [P, 8, P], BF16, 149)
    stage = sb("stage", [P, 2, NK, TG], F32, 151)
    act_out = sb("act_out", [P, 4, S], F32, 183)
    act_in = sb("act_in", [P, 2, ET, S], F32, 89)
    act_m = sb("act_m", [P, 2, S], F32, 121)
    eh = sb("eh", [P, 4, S], F32R, 125)
    el = sb("el", [P, 4, S], F32R, 133)
    gt = sb("gt", [P, 2, S // TG, ET * TG], F32, 141)
    ch = sb("ch", [P, KT, S], F32R, 89)
    cl = sb("cl", [P, KT, S], F32R, 105)
    dh = sb("dh", [P, KT, S], F32R, 121)
    dl = sb("dl", [P, KT, S], F32R, 137)
    zs = sb("zs", [P, KT, S], F32, 153)
    ub = sb("ub", [P, 2, 16 + S], F32, 169)
    us = sb("us", [P, 2, 16 + S], F32, 174)
    um = sb("um", [P, 2, S], F32, 179)
    sqk = sb("sqk", [P, KT, S], F32, 121)
    sv = sb("sv", [P, TT, D], F32, 137)
    SW = 1280
    st = sb("st", [P, SW], F32, 169)
    slb0 = sb("slb0", [P, SW], F32, 174)
    slo = sb("slo", [P, SW], F32, 179)
    slh = sb("slh", [P, SW], F32R, 184)
    sll = sb("sll", [P, SW], F32R, 189)
    sy = sb("sy", [P, S], F32, 194)
    sa = sb("sa", [P, SW], F32, 196)
    slb1 = sb("slb1", [P, SW], F32, 201)
    slb = [slb0, slb1]
    outT = sb("outT", [P, KT, S], F32, 121)

    psum = nc.alloc_psum_tensor("psum", [P, 8, S], F32)
    acc = [psum[:, i, :] for i in range(4)]
    aux = [psum[:, 4 + i, :] for i in range(4)]
    aux3 = psum[:, 4:7, :].rearrange("p a n -> p (a n)")[:, 0:SW]
    acc3 = psum[:, 1:4, :].rearrange("p a n -> p (a n)")[:, 0:SW]

    gate_table = nc.dram_tensor("gate_table", (S // TG, P, NK * TG), F32, kind="Internal").ap()
    act_table = nc.dram_tensor("act_table", (NK, P, S), F32, kind="Internal").ap()

    sem = nc.alloc_semaphore
    raw_here = [sem(f"raw_here{i}") for i in range(RAW)]
    ada_used = sem("ada_used")
    weights_split = sem("weights_split")
    split_step = sem("split_step")
    tile_done = sem("tile_done")
    evacuated = sem("evacuated")
    small_here = sem("small_here")
    xin_here = sem("xin_here")
    const_pool = sem("const_pool")
    const_dve = sem("const_dve")
    const_vec = sem("const_vec")
    csil_done = sem("csil_done")
    ada_done = sem("ada_done")
    nsq_done, nmm_done, nstd_done, ninv_done = sem("nsq_done"), sem("nmm_done"), sem("nstd_done"), sem("ninv_done")
    nxn_done, nhi_done, nlo_done, nout_done = sem("nxn_done"), sem("nhi_done"), sem("nlo_done"), sem("nout_done")
    out_stored = sem("out_stored")

    GP = Steps(sem("gla_pe"), "gate", "attn", "ket", "kv0", "kv1", "kv2", "kv3", "o", "ms")
    GA = Steps(sem("gla_act"), "abs", "exp", "ln", "eb", "enb", "ekd", "ket", "sq0", "sq1", "std")
    GD = Steps(sem("gla_dve"), "min", "logalpha", "cumsum", "dif", "qd", "ki", "ke", "attn",
               *[f"s{c}" for c in range(1, 8)], "rstd", "og0", "og1", "y0", "y1")
    CP = Steps(sem("ckv_pe"), "ms", "iw", "ckvn")
    CA = Steps(sem("ckv_act"), "sq0", "sq1", "std", "n0", "n1")
    CD = Steps(sem("ckv_dve"), "rstd", "c0", "c1", "iw")
    idx_mm, idx_relu, idx_acc = sem("idx_mm"), sem("idx_relu"), sem("idx_acc")
    top_step = sem("top_step")
    ga_hi, ga_lo = sem("ga_hi"), sem("ga_lo")
    uk_here = [sem("uk_here0"), sem("uk_here1")]
    DP_q, DP_s, DP_t, DP_o, DP_v = sem("qlat_mm"), sem("logit_mm"), sem("probT_mm"), sem("olat_mm"), sem("oval_mm")
    DA_q, DA_e, DA_n, DA_o, DA_v = sem("qlat_out"), sem("prob_exp"), sem("prob_norm"), sem("olat_out"), sem("oval_out")
    DD = Steps(sem("dsa_dve"), "bias", "logit", "max", "inv")
    pT_out = sem("probT_out")
    y_step, y_hi, y_lo = sem("y_step"), sem("y_hi"), sem("y_lo")
    db_hi, db_lo = sem("dsaout_hi"), sem("dsaout_lo")
    pq_out, ps_mm = sem("pq_out"), sem("ps_mm")
    sel = sem("sel_step")
    sel_exp = sem("sel_exp")
    sT_mm, sT_step = sem("slotT_mm"), sem("slotT_step")
    HOT = Steps(sem("hot_step"), "key1", "key2", "gates")
    table_mm, table_out = sem("table_mm"), sem("table_out")
    table_stored = [sem("table_stored0"), sem("table_stored1")]
    act_stored = [sem(f"act_stored{j}") for j in range(4)]
    chunk_here = [sem("chunk_here0"), sem("chunk_here1")]
    e_mul, e_hi, e_lo = sem("e_mul"), sem("e_hi"), sem("e_lo")
    pl_step, pl_hi, pl_lo = sem("pool_step"), sem("pool_hi"), sem("pool_lo")
    pw_y, pw_hi, pw_lo = sem("pooly"), sem("pooly_hi"), sem("pooly_lo")
    SB = {name: sem("sb_" + name) for name in ("qk", "cum", "o",
                                               "abs", "exp", "ln", "hi", "a", "yhi",
                                               "lb", "lo", "mask", "losplit", "sum", "amask", "y", "ylo")}

    def groups(eng, count, body):
        if count == 1:
            body(0)
        else:
            with eng.Fori(0, count) as g:
                body(g)

    def item_of(table, index):
        return table[bass.ds(index, 1), :, :].rearrange("a p n -> p (a n)")


    PL_END, n = [], 0
    for half in range(2):
        for t in range(8):
            n += 2 * half + t // 4 + 1 + 3
            PL_END.append(n)
    SEQ_G, SEQ_D = schedule_gla(), schedule_dsa()
    block_cm = nc.Block()
    block = block_cm.__enter__()
    lin_segments = [("w_in", 0, W_L1, W_A), ("w_branch_a", 0, W_A, W_ZB), ("w_in", W_A, W_ZB, W_B),
                    ("w_branch_b", 0, W_B, W_O), ("w_out", 0, W_O, W_Q)]

    @block.sync
    def _(sp):
        def load(table, first, count, w, width=D):
            def four(g):
                for j in range(RAW):
                    sp.wait_ge(weights_split, w + 4 * g + j - RAW + 1)
                    sp.dma_start(raw[j][:, 0:width], item_of(table, first + 4 * g + j)).then_inc(raw_here[j], 16)
            groups(sp, count // RAW, four)

        for j in range(RAW):
            sp.dma_start(raw[j][:, :], item_of(io["w_ada"], j)).then_inc(raw_here[j], 16)
        with sp.Fori(0, NADA // RAW - 1) as g:
            for j in range(RAW):
                sp.wait_ge(ada_used, 4 * g + j + 1)
                sp.dma_start(raw[j][:, :], item_of(io["w_ada"], 4 * g + j + RAW)).then_inc(raw_here[j], 16)
        for j in range(RAW):
            sp.wait_ge(ada_used, NADA - RAW + j + 1)
            sp.dma_start(raw[j][:, :], item_of(io["w_in"], j)).then_inc(raw_here[j], 16)
        load(io["w_in"], RAW, W_A - RAW, RAW)
        for name, first, w, end in lin_segments[1:]:
            load(io[name], first, end - w, w)

        with sp.Fori(0, PH) as h:
            for t in range(2 + UH):
                table, at = (io["peer_w_q"], 2 * h + t) if t < 2 else (io["peer_u"], UH * h + t - 2)
                sp.wait_ge(weights_split, W_Q + (2 + UH) * h + t - RAW + 1)
                sp.dma_start(raw[t % RAW][:, :], item_of(table, at)).then_inc(raw_here[t % RAW], 16)
        load(io["peer_u"], PH * UH, NK - PH * UH, W_U)
        load(io["peer_v"], 0, NK, W_V)

        for half in range(2):
            w = W_POOL + 32 * half
            load(io["pool_w_in"], 16 * half, 16, w)
            load(io["pool_w"], 8 * half, 8, w + 16, width=D // 2)
            load(io["pool_w_out"], 8 * half, 8, w + 24)
        for half in range(2):
            w = W_SB + 32 * half
            load(io["sb_w_in"], 24 * half, 24, w)
            load(io["sb_w_out"], 8 * half, 8, w + 24)

    @block.gpsimd
    def _(pool):
        steps = [
            pool.memset(ident[:, :], 0.0), pool.memset(ones[:, :], 1.0), pool.memset(strict[:, :], 1.0),
            pool.memset(block_causal[:, :], 1.0), pool.memset(neg[:, :], NEG),
            pool.memset(chunk_start[:, :], 1.0), pool.memset(zero[:, :], 0.0), pool.memset(eps[:, :], EPS),
            pool.memset(one[:, :], 1.0),
            pool.iota(iota_row[:, :], pattern=[[1, P]], base=0, channel_multiplier=0,
                      allow_small_or_imprecise_dtypes=True),
            pool.iota(iota16[:, :], pattern=[[1, PK]], base=0, channel_multiplier=0,
                      allow_small_or_imprecise_dtypes=True),
            pool.iota(relpos[:, :], pattern=[[1, 896]], base=-384, channel_multiplier=-1,
                      allow_small_or_imprecise_dtypes=True),
        ]
        for ins in steps:
            ins.then_inc(const_pool, 1)
        n = len(steps)
        pool.wait_ge(const_pool, n)
        for ins in (
            pool.affine_select(out=ident[:, :], in_=ident[:, :], compare_op=ALU.not_equal, fill=1.0, base=0,
                               pattern=[[-1, P]], channel_multiplier=1),
            pool.affine_select(out=strict[:, :], in_=strict[:, :], compare_op=ALU.is_gt, fill=0.0, base=0,
                               pattern=[[1, P]], channel_multiplier=-1),
            pool.affine_select(out=block_causal[:, :], in_=block_causal[:, :], compare_op=ALU.is_ge, fill=0.0,
                               base=0, pattern=[[1, P]], channel_multiplier=-1),
            pool.memset(chunk_start[:, :].rearrange("p (c t) -> p c t", t=CH)[:, :, 0:1], 0.0),
        ):
            ins.then_inc(const_pool, 1)
        pool.wait_ge(const_pool, n + 4)
        pool.memset(block_causal[0:CH, CH:P], 0.0).then_inc(const_pool, 1)
        pool.tensor_tensor(trilr[:, :], ones[:, :], strict[:, :], ALU.subtract).then_inc(const_pool, 1)
        pool.wait_ge(const_pool, n + 6)
        pool.tensor_tensor(trilr[:, :], trilr[:, :].bitcast(F32), ident[:, :], ALU.subtract).then_inc(const_pool, 1)
        pool.tensor_tensor(onesr[:, :], ones[:, :], zero[:, 0:1].broadcast_to([P, P]), ALU.add)\
            .then_inc(const_pool, 1)
        assert n + 8 == NCONST

        def split(w, j, g, width, first=False):
            s = j % SPLIT
            pool.wait_ge(raw_here[j], 16 * (g + 1))
            if not first:
                pool.wait_ge(tile_done, w - SPLIT + 1)
            pool.tensor_tensor(wh[s][:, 0:width], raw[j][:, 0:width], zero[:, 0:1].broadcast_to([P, width]),
                               ALU.add).then_inc(split_step, 1)
            pool.wait_ge(split_step, w + 1)
            pool.tensor_tensor(wl[s][:, 0:width], raw[j][:, 0:width], wh[s][:, 0:width].bitcast(F32),
                               ALU.subtract).then_inc(weights_split, 1)

        G0 = NADA // RAW
        for j in range(RAW):
            split(j, j, G0, D, first=j < SPLIT)
        for w, count, width in [(RAW, W_POOL + 16 - RAW, D), (W_POOL + 16, 8, D // 2), (W_POOL + 24, 24, D),
                                (W_POOL + 48, 8, D // 2), (W_POOL + 56, W_END - W_POOL - 56, D)]:
            with pool.Fori(0, count // RAW) as g:
                for j in range(RAW):
                    split(w + 4 * g + j, j, G0 + w // 4 + g, width)

    @block.tensor
    def _(pe):
        def products(out, whi, wlo, ahi, alo, start, stop):
            pe.matmul(out, whi, ahi, start=start, stop=False, skip_group_check=True)
            pe.matmul(out, whi, alo, start=False, stop=False, skip_group_check=True)
            return pe.matmul(out, wlo, ahi, start=False, stop=stop, skip_group_check=True)

        def lin(w, j, hi, lo, k0=0, kt=KT, bank=None, free=True):
            pe.wait_ge(weights_split, w + 1)
            if free:
                pe.wait_ge(evacuated, w - 3)
            s = j % SPLIT
            out = acc[j if bank is None else bank]
            for k in range(kt):
                cols = slice(P * k, P * k + P)
                mm = products(out, wh[s][:, cols], wl[s][:, cols], hi[:, k0 + k, :], lo[:, k0 + k, :],
                              k == 0, k == kt - 1)
            mm.then_inc(tile_done, 1)

        def lin_loop(w, count, hi, lo):
            def four(g):
                for j in range(4):
                    lin(w + 4 * g + j, j, hi, lo)
            groups(pe, count // 4, four)

        def lin_tokens(w, turns, hi, lo):
            def turn(g):
                for j in range(4):
                    pe.wait_ge(weights_split, w + 4 * g + j + 1)
                    if j == 0:
                        pe.wait_ge(evacuated, w + 4 * g)
                    s = j % SPLIT
                    for kk in range(2):
                        k = 2 * j + kk
                        cols = slice(S * kk, S * kk + S)
                        for t in range(TT):
                            tok = slice(P * t, P * t + P)
                            first, last = k == 0, k == KT - 1
                            pe.matmul(acc[t], hi[:, k, tok], wh[s][:, cols], start=first, stop=False,
                                      skip_group_check=True)
                            pe.matmul(acc[t], lo[:, k, tok], wh[s][:, cols], start=False, stop=False,
                                      skip_group_check=True)
                            mm = pe.matmul(acc[t], hi[:, k, tok], wl[s][:, cols], start=False, stop=last,
                                           skip_group_check=True)
                    mm.then_inc(tile_done, 1)
            groups(pe, turns, turn)

        def norm(o):
            for k in range(KT):
                pe.wait_ge(nsq_done, KT * o + k + 1)
                pe.matmul(aux[0], ones[:, :], nsq[:, k % 2, :], start=k == 0, stop=k == KT - 1)\
                    .then_inc(nmm_done, 1)

        pe.wait_ge(const_pool, NCONST)
        pe.wait_ge(csil_done, 1)
        with pe.Fori(0, NADA // RAW) as g:
            for j in range(RAW):
                pe.wait_ge(raw_here[j], 16 * (g + 1))
                for k in range(KT):
                    mm = pe.matmul(psum[:, 7, bass.ds(4 * g + j, 1)], raw[j][:, P * k:P * k + P],
                                   csil[:, k:k + 1], start=k == 0, stop=k == KT - 1)
                mm.then_inc(ada_used, 1)

        norm(0)
        pe.wait_ge(nlo_done, KT)
        for j in range(4):
            lin(j, j, ah, al, free=False)
        lin_loop(4, 8, ah, al)
        lin_tokens(12, 2, ah, al)
        lin_loop(20, 4, ah, al)

        pe.wait_ge(small_here, NSMALL)
        for item in SEQ_G:
            kind = item[0]
            if kind == "ckv":
                for k in range(2):
                    pe.wait_ge(CA.sem, CA.at(0, f"sq{k}"))
                    mm = pe.matmul(aux[0], ones[:, :], gt1[:, k, :], start=k == 0, stop=k == 1)
                mm.then_inc(CP.sem, 1)
                pe.wait_ge(ada_done, 1)
                for t in range(TT):
                    mm = pe.transpose(aux[3][:, P * t:P * t + P], misc[:, P * t:P * t + P], ident[:, :])
                mm.then_inc(CP.sem, 1)
                pe.wait_ge(CD.sem, CD.at(0, "c1"))
                for t in range(TT):
                    for c in range(2):
                        mm = pe.transpose(psum[:, 5 + t // 2, LAT * (t % 2) + P * c:LAT * (t % 2) + P * c + P],
                                          ckv[:, c, P * t:P * t + P], ident[:, :])
                mm.then_inc(CP.sem, 1)
            elif kind == "lin":
                w = item[1]
                lin(w, w % 4, ah, al)
            elif kind == "prep":
                h = item[1]
                if h:
                    pe.wait_ge(GD.sem, GD.at(h - 1, "og1"))
                else:
                    pe.wait_ge(CA.sem, CA.at(0, "std"))
                pe.matmul(aux[0], gwu[:, GDK * h:GDK * h + GDK], misc[0:16, :], start=True, stop=True)\
                    .then_inc(GP.sem, 1)
            elif kind == "attn":
                h = item[1]
                if h == 0:
                    pe.wait_ge(CA.sem, CA.at(0, "n1"))
                pe.wait_ge(GD.sem, GD.at(h, "ki"))
                for t in range(TT):
                    tok = slice(P * t, P * t + P)
                    mm = pe.matmul(aux[1][:, tok], gki[:, tok], gqd[:, tok], start=True, stop=True)
                mm.then_inc(GP.sem, 1)
                pe.wait_ge(GD.sem, GD.at(h, "ke"))
                for t in range(TT):
                    tok = slice(P * t, P * t + P)
                    mm = pe.transpose(aux[0][:, tok], gke[:, tok], ident[:, :])
                mm.then_inc(GP.sem, 1)
            elif kind == "kv":
                h, t = item[1:]
                if t == 0:
                    pe.wait_ge(GA.sem, GA.at(h, "ket"))
                    pe.wait_ge(GD.sem, GD.at(h, "attn"))
                    if h:
                        pe.wait_ge(GA.sem, GA.at(h - 1, "std"))
                else:
                    pe.wait_ge(GD.sem, GD.at(h, f"s{2 * t}"))
                for c in range(2 if t < 3 else 1):
                    rows = slice(CH * c, CH * c + CH)
                    mm = pe.matmul(aux[2 - c][:, 0:GDV], gket[rows, t, :],
                                   gv[rows, t, GDV * h:GDV * h + GDV], start=True, stop=True)
                mm.then_inc(GP.sem, 1)
            elif kind == "o":
                h = item[1]
                pe.wait_ge(GD.sem, GD.at(h, "s7"))
                for v in range(2):
                    out = aux[1 - v]
                    val = slice(GDV * h + P * v, GDV * h + P * v + P)
                    for t in range(TT):
                        tok = slice(P * t, P * t + P)
                        mm = pe.matmul(out[:, tok], gv[:, t, val], gat[:, t, :], start=t == 0, stop=False,
                                       skip_group_check=True)
                    for c in range(1, 8):
                        tok = slice(CH * c, CH * c + CH)
                        mm = pe.matmul(out[:, tok], gst[:, c - 1, P * v:P * v + P], gqd[:, tok], start=False,
                                       stop=c == 7, skip_group_check=True)
                mm.then_inc(GP.sem, 1)
                for v in range(2):
                    pe.wait_ge(GA.sem, GA.at(h, f"sq{v}"))
                    mm = pe.matmul(aux[2], ones[:, :], gt1[:, v, :], start=v == 0, stop=v == 1)
                mm.then_inc(GP.sem, 1)
            elif kind == "idx":
                tt, h = item[1:]
                i = (tt - 1) * IH + h
                if i:
                    pe.wait_ge(idx_relu, i)
                else:
                    pe.wait_ge(evacuated, W_G)
                    pe.wait_ge(CD.sem, CD.at(0, "iw"))
                rows = slice(IDD * (h % 2), IDD * (h % 2) + IDD)
                pe.matmul(aux[3][:, 0:P * (tt + 1)], iq[rows, h // 2, P * tt:P * tt + P],
                          ik[rows, 0:P * (tt + 1)], start=True, stop=True).then_inc(idx_mm, 1)

        for item in SEQ_D:
            kind = item[0]
            if kind == "lin":
                w = item[1]
                if w == W_A:
                    pe.wait_ge(ga_lo, KT)
                if w < W_A:
                    lin(w, w % 4, ah, al)
                else:
                    lin(w, w % 4, bh, bl)
            elif kind == "qlat":
                h = item[1]
                pe.wait_ge(uk_here[h % 2], 32 * (h // 2 + 1))
                if h >= 2:
                    pe.wait_ge(DA_v, h - 1)
                elif h == 0:
                    pe.wait_ge(GA.sem, GA.at(GH - 1, "std"))
                    pe.wait_ge(idx_relu, 3 * IH)
                    pe.wait_ge(evacuated, W_ZA)
                for c in range(2):
                    mm = pe.matmul(aux[2 + c], uk[:, h % 2, P * c:P * c + P], qk[:, h, :], start=True, stop=True)
                mm.then_inc(DP_q, 1)
            elif kind == "score":
                h, t = divmod(item[1], TT)
                i = item[1]
                n = P * (t + 1)
                pe.wait_ge(DA_q, h + 1)
                if i:
                    pe.wait_ge(DD.sem, DD.at(i - 1, "logit"))
                else:
                    pe.wait_ge(GD.sem, GD.at(GH - 1, "og1"))
                for c in range(2):
                    mm = pe.matmul(aux[0][:, 0:n], qlat[:, c, P * t:P * t + P], ckv[:, c, 0:n],
                                   start=c == 0, stop=c == 1)
                mm.then_inc(DP_s, 1)
            elif kind == "pt":
                i = item[1]
                t = i % TT
                pe.wait_ge(DA_n, i + 1)
                if i:
                    pe.wait_ge(pT_out, i)
                for b in range(t + 1):
                    mm = pe.transpose(aux[1][:, P * b:P * b + P], prob[:, i % 2, P * b:P * b + P], ident[:, :])
                mm.then_inc(DP_t, 1)
            elif kind == "out":
                h = item[1]
                pe.wait_ge(pT_out, TT * (h + 1))
                if h + 1 < DH:
                    pe.wait_ge(DA_q, h + 2)
                for c in range(2):
                    for b in range(TT):
                        mm = pe.matmul(aux[2 + c][:, P * b:S], ckvn[:, b, P * c:P * c + P], pT[:, b, P * b:S],
                                       start=b == 0, stop=b == TT - 1, skip_group_check=True)
                mm.then_inc(DP_o, 1)
                pe.wait_ge(DA_o, h + 1)
                for c in range(2):
                    mm = pe.matmul(aux[2], uv[:, h % 2, c, :], olat[:, c, :], start=c == 0, stop=c == 1)
                mm.then_inc(DP_v, 1)

        lin_loop(W_ZB, 8, ah, al)
        pe.wait_ge(db_lo, KT)
        lin_loop(W_B, 8, bh, bl)
        pe.wait_ge(y_lo, KT)
        lin_loop(W_O, 8, ah, al)
        norm(1)
        pe.wait_ge(nlo_done, 2 * KT)

        for h in range(PH):
            w = W_Q + (2 + UH) * h
            for t in range(3):
                lin(w + t, t, ah, al)
            for side in range(2):
                pe.wait_ge(evacuated, w + side + 1)
                if h >= 2:
                    pe.wait_ge(sel, NSEL * (h - 2) + 24)
                for t in range(TT):
                    mm = pe.matmul(aux[2 * (h % 2) + side][:, P * t:P * t + P], pq[:, h % 2, side, P * t:P * t + P],
                                   keys[:, side, :], start=True, stop=True)
                mm.then_inc(ps_mm, 1)
            for t in range(3, 2 + UH):
                lin(w + t, t % 4, ah, al)
        lin_loop(W_U, 4, ah, al)
        pe.wait_ge(sel, NSEL * PH)
        for part in range(3):
            for t in range(TT):
                mm = pe.transpose(aux[part][:, P * t:P * t + P], slots[:, part, t, :], ident[:, :])
            mm.then_inc(sT_mm, 1)
        lin_loop(W_U + 4, 4, ah, al)
        pe.wait_ge(sT_step, 8)
        def table(g, first):
            for b in range(8):
                lin(W_TAB + 8 * g + b, b % 4, ah, al)
                pe.wait_ge(HOT.sem, HOT.at(8 * g + b, "gates"))
                for q in (2 * b, 2 * b + 1):
                    if not (first and q < 4):
                        pe.wait_ge(table_out, 16 * g + q - 3)
                    for t in range(4):
                        u = 4 * (q % 2) + t
                        for part in range(3):
                            mm = pe.matmul(aux[q % 4][:, P * t:P * t + P], hot[:, b % 2, 0, u, :],
                                           hot[:, b % 2, 1 + part, u, :], start=part == 0, stop=part == 2)
                    mm.then_inc(table_mm, 1)
        table(0, True)
        with pe.Fori(1, 8) as g:
            table(g, False)
        lin_loop(W_V - 8, 8, ah, al)

        def experts(g, first=False, last=False):
            for e in range(2 * ET):
                v = W_V + 2 * ET * g + e
                pe.wait_ge(weights_split, v + 1)
                if first and e == 0:
                    pe.wait_ge(evacuated, W_V)
                    pe.wait_ge(table_out, S // 4)
                pe.wait_ge(e_lo, 2 * ET * g + e + 1)
                for d in range(KT):
                    cols = slice(P * d, P * d + P)
                    mm = products(psum[:, (d + 4) % 8, :], wh[e % 2][:, cols], wl[e % 2][:, cols], eh[:, e % 4, :],
                                  el[:, e % 4, :], first and e == 0, last and e == 2 * ET - 1)
                mm.then_inc(tile_done, 1)
        experts(0, first=True)
        with pe.Fori(1, NCHUNK // 2 - 1) as g:
            experts(g)
        experts(NCHUNK // 2 - 1, last=True)
        norm(2)
        norm(3)
        pe.wait_ge(nlo_done, 3 * KT)

        for half in range(2):
            w = W_POOL + 32 * half
            lin_loop(w, 16, ah, al)
            for n in range(8):
                if n % 4 == 0:
                    pe.wait_ge(pl_lo, 8 * half + n + 4)
                lin(w + 16 + n, n % 4, ch, cl, k0=n // 4 * 4, kt=4)
            pe.wait_ge(pw_lo, 8 * half + 8)
            lin_loop(w + 24, 8, dh, dl)
        norm(4)
        pe.wait_ge(nlo_done, 4 * KT)

        def scores(i):
            hd = i % 8
            rows = slice(64 * (hd % 2), 64 * (hd % 2) + 64)
            q, k = sqk[rows, hd // 2, :], sqk[rows, 4 + hd // 2, :]
            if i:
                pe.wait_ge(SB["lo"], i)
            for b in range(TT):
                for at, c0, n in SB_REGIONS[b]:
                    mm = pe.matmul(aux3[:, at:at + n], k[:, P * b:P * b + P], q[:, c0:c0 + n],
                                   start=True, stop=True, skip_group_check=True)
            mm.then_inc(SB["qk"], 1)

        for half in range(2):
            w = W_SB + 32 * half
            lin_loop(w, 8, ah, al)
            lin_tokens(w + 8, 2, ah, al)
            pe.wait_ge(evacuated, w + 16)
            scores(8 * half)
            for hd in range(8):
                i = 8 * half + hd
                if hd < 7:
                    scores(i + 1)
                pe.wait_ge(SB["losplit"], i + 1)
                if i:
                    pe.wait_ge(SB["sum"], i)
                plan = [(trilr, b, b) for b in range(TT)] + [(onesr, b, c) for b in range(TT) for c in range(b + 1, TT)]
                sums = []
                for mat, b, c in plan:
                    for at, c0, n in SB_REGIONS[c]:
                        for to, d0, m in SB_REGIONS[b]:
                            a, z = max(c0, d0), min(c0 + n, d0 + m)
                            if a < z:
                                sums += [(mat, src[:, at + a - c0:at + z - c0], to + a - d0, z - a)
                                         for src in (slh, sll)]
                banks = [to // S for _, _, to, _ in sums]
                for n, (mat, src, to, m) in enumerate(sums):
                    mm = pe.matmul(acc3[:, to:to + m], mat[:, :], src, start=banks[n] not in banks[:n],
                                   stop=banks[n] not in banks[n + 1:], skip_group_check=True)
                mm.then_inc(SB["cum"], 1)
                pe.wait_ge(weights_split, w + 16 + hd + 1)
                pe.wait_ge(evacuated, w + 16 + hd)
                s = hd % SPLIT
                for kk in range(KT):
                    cols = slice(P * kk, P * kk + P)
                    mm = products(acc[0], wh[s][:, cols], wl[s][:, cols], ah[:, kk, :], al[:, kk, :],
                                  kk == 0, kk == KT - 1)
                mm.then_inc(tile_done, 1)
                pe.wait_ge(SB["amask"], i + 1)
                if i:
                    pe.wait_ge(SB["y"], i)
                for b in range(TT):
                    for at, c0, n in SB_REGIONS[b]:
                        mm = pe.matmul(aux[3][:, c0:c0 + n], sv[:, b, P * hd:P * hd + P], sa[:, at:at + n],
                                       start=at == 0, stop=b == TT - 1, skip_group_check=True)
                mm.then_inc(SB["o"], 1)
            pe.wait_ge(SB["ylo"], 8 * half + 8)
            lin_loop(w + 24, 8, ch, cl)
        norm(5)

    @block.scalar
    def _(act):
        def evac(w, j, dst, func=ACT.Copy, done=None, scale=1.0):
            act.wait_ge(tile_done, w + 1 if done is None else done)
            act.activation(dst, acc[j], func, scale=scale).then_inc(evacuated, 1)

        def evac_loop(w, count, dst, func=ACT.Copy, scale=1.0):
            def four(g):
                for j in range(4):
                    evac(w + 4 * g + j, j, dst[:, bass.ds(4 * g + j, 1), :].rearrange("p a n -> p (a n)"), func,
                         scale=scale)
            if count == 4:
                for j in range(4):
                    evac(w + j, j, dst[:, j, :], func, scale=scale)
            else:
                groups(act, count // 4, four)

        def evac_tokens(w, turns, dst):
            for g in range(turns):
                for j in range(4):
                    evac(w, j, dst[:, j, S * g:S * g + S], done=w + 4 * g + 4)

        def norm(o, ready, base, split=None, shift=None, per=1):
            for k in range(KT):
                act.wait_ge(ready, base if ready is xin_here else base + per * (k + 1))
                if k >= 2 or o:
                    act.wait_ge(nmm_done, KT * o + k - 1)
                act.activation(nsq[:, k % 2, :], xT[:, k, :], ACT.Square).then_inc(nsq_done, 1)
            act.wait_ge(nmm_done, KT * o + KT)
            act.activation(nstd[:, :], aux[0], ACT.Sqrt, scale=1.0 / D, bias=eps[:, :]).then_inc(nstd_done, 1)
            if split is not None:
                for k in range(KT):
                    act.wait_ge(nxn_done, KT * split + k + 1)
                    act.activation(ah[:, k, :], nxn[:, k % 2, :], ACT.Identity,
                                   bias=zero[:, 0:1] if shift is None else shift[:, k:k + 1]).then_inc(nhi_done, 1)

        for dst, name in ((cT, "c"), (vec, "vec"), (gwu, "gla_w_gate_up"), (keys, "peer_sub_keys")):
            src = io[name].rearrange("p a n -> p (a n)") if name == "peer_sub_keys" else io[name]
            d = dst[:, :, :].rearrange("p a n -> p (a n)") if name == "peer_sub_keys" else dst[:, :]
            act.dma_start(d, src).then_inc(small_here, 16)
        act.dma_start(xT[:, :, :], io["x"]).then_inc(xin_here, 16)

        act.wait_ge(small_here, NSMALL)
        act.activation(csil[:, :], cT[:, :], ACT.Silu).then_inc(csil_done, 1)
        act.wait_ge(const_pool, NCONST)
        act.wait_ge(ada_done, 1)
        norm(0, xin_here, 16, split=0, shift=shift1)

        evac(0, 0, misc[:, :])
        evac(1, 1, ik[:, :])
        evac(2, 2, ckv[:, 0, :])
        evac(3, 3, ckv[:, 1, :])
        evac_loop(4, 8, qk)
        evac_tokens(12, 2, gv)
        evac_loop(20, 4, iq)

        for item in SEQ_G:
            kind = item[0]
            if kind == "ckv":
                act.wait_ge(evacuated, 4)
                for k in range(2):
                    act.activation(gt1[:, k, :], ckv[:, k, :], ACT.Square).then_inc(CA.sem, 1)
                act.wait_ge(CP.sem, CP.at(0, "ms"))
                act.activation(nstd[:, :], aux[0], ACT.Sqrt, scale=1.0 / LAT, bias=eps[:, :]).then_inc(CA.sem, 1)
                act.wait_ge(CP.sem, CP.at(0, "ckvn"))
                for b in range(2):
                    act.activation(ckvn[:, 2 * b:2 * b + 2, :].rearrange("p a n -> p (a n)"), psum[:, 5 + b, :],
                                   ACT.Copy).then_inc(CA.sem, 1)
            elif kind == "lin":
                w = item[1]
                h, r = divmod(w - W_G, 4)
                if r < 2:
                    evac(w, w % 4, gr[:, 2 * h + r, :], ACT.Silu)
                else:
                    act.wait_ge(GD.sem, GD.at(h, "ke"))
                    evac(w, w % 4, qk[:, 2 * h + r - 2, :])
            elif kind == "prep":
                h = item[1]
                act.wait_ge(GP.sem, GP.at(h, "gate"))
                if h:
                    act.wait_ge(GD.sem, GD.at(h - 1, "y1"))
                act.activation(gt1[:, 0, :], aux[0], ACT.Abs, bias=VEC["gla_b_gate"][:, h:h + 1])\
                    .then_inc(GA.sem, 1)
                act.wait_ge(GA.sem, GA.at(h, "abs"))
                act.activation(gt1[:, 0, :], gt1[:, 0, :], ACT.Exp, scale=-1.0).then_inc(GA.sem, 1)
                act.wait_ge(GA.sem, GA.at(h, "exp"))
                act.activation(gt1[:, 0, :], gt1[:, 0, :], ACT.Ln, bias=one[:, :]).then_inc(GA.sem, 1)
                act.wait_ge(GD.sem, GD.at(h, "cumsum"))
                act.activation(geb[:, :], gb[:, :], ACT.Exp, scale=1.0 / TAU).then_inc(GA.sem, 1)
                act.activation(gki[:, :], gb[:, :], ACT.Exp, scale=-1.0 / TAU).then_inc(GA.sem, 1)
                act.wait_ge(GD.sem, GD.at(h, "dif"))
                act.activation(gke[:, :], gke[:, :], ACT.Exp, scale=1.0 / TAU).then_inc(GA.sem, 1)
            elif kind == "attn":
                h = item[1]
                act.wait_ge(GP.sem, GP.at(h, "ket"))
                act.activation(gket[:, :, :].rearrange("p a n -> p (a n)"), aux[0], ACT.Copy).then_inc(GA.sem, 1)
            elif kind == "o":
                h = item[1]
                act.wait_ge(GP.sem, GP.at(h, "o"))
                for v in range(2):
                    act.activation(gt1[:, v, :], aux[1 - v], ACT.Square).then_inc(GA.sem, 1)
                act.wait_ge(GP.sem, GP.at(h, "ms"))
                act.activation(gke[:, :], aux[2], ACT.Sqrt, scale=1.0 / GDV, bias=eps[:, :]).then_inc(GA.sem, 1)
            elif kind == "idx":
                tt, h = item[1:]
                i = (tt - 1) * IH + h
                n = P * (tt + 1)
                act.wait_ge(idx_mm, i + 1)
                if i >= 2:
                    act.wait_ge(idx_acc, i - 1)
                act.activation(rel[:, i % 2, 0:n], aux[3][:, 0:n], ACT.Relu, scale=IDD ** -0.5).then_inc(idx_relu, 1)

        def load_head(h):
            act.dma_start(uk[:, h % 2, :], io["dsa_w_uk"][h]).then_inc(uk_here[h % 2], 16)
            act.dma_start(uv[:, h % 2, :, :], io["dsa_w_uv"][h]).then_inc(uk_here[h % 2], 16)

        act.wait_ge(GD.sem, GD.at(GH - 1, "y1"))
        load_head(0)
        load_head(1)
        for item in SEQ_D:
            kind = item[0]
            if kind == "ga":
                n = item[1]
                act.activation(bh[:, n, :], gr[:, n, :], ACT.Copy).then_inc(ga_hi, 1)
            elif kind == "lin":
                w = item[1]
                if w < W_A:
                    act.wait_ge(ga_lo, w - W_ZA + 1)
                    evac(w, w % 4, gr[:, w - W_ZA, :], ACT.Sigmoid)
            elif kind == "qlat":
                h = item[1]
                act.wait_ge(DP_q, h + 1)
                for c in range(2):
                    ins = act.activation(qlat[:, c, :], aux[2 + c], ACT.Copy)
                ins.then_inc(DA_q, 1)
            elif kind == "score":
                i = item[1]
                n = P * (i % TT + 1)
                act.wait_ge(DD.sem, DD.at(i, "max"))
                act.activation(prob[:, i % 2, 0:n], prob[:, i % 2, 0:n], ACT.Exp, bias=rowstat[:, 0, i:i + 1],
                               accum_out=rowstat[:, 1, i:i + 1]).then_inc(DA_e, 1)
                act.wait_ge(DD.sem, DD.at(i, "inv"))
                act.activation(prob[:, i % 2, 0:n], prob[:, i % 2, 0:n], ACT.Copy, scale=rowstat[:, 2, i:i + 1])\
                    .then_inc(DA_n, 1)
            elif kind == "out":
                h = item[1]
                act.wait_ge(DP_o, h + 1)
                for c in range(2):
                    ins = act.activation(olat[:, c, :], aux[2 + c], ACT.Copy)
                ins.then_inc(DA_o, 1)
                act.wait_ge(DP_v, h + 1)
                act.activation(qk[:, h, :], aux[2], ACT.Copy).then_inc(DA_v, 1)
                if h + 2 < DH:
                    load_head(h + 2)

        act.wait_ge(evacuated, W_ZB)
        act.wait_ge(DA_v, DH)
        for n in range(KT):
            act.activation(bh[:, n, :], qk[:, n, :], ACT.Copy).then_inc(db_hi, 1)
        evac_loop(W_ZB, 8, zb, ACT.Sigmoid)
        for n in range(KT):
            act.wait_ge(y_step, n + 1)
            act.activation(ah[:, n, :], gr[:, n, :], ACT.Copy).then_inc(y_hi, 1)
        norm(1, evacuated, W_O, split=1, shift=shift2)

        def gelu(w, bank, u, j, turn, first=False):
            if not first:
                act.wait_ge(act_stored[j], 16 * turn)
            evac(w, bank, act_out[:, j, :], ACT.Gelu)
            act.wait_ge(evacuated, w + 1)
            act.dma_start(item_of(act_table, u), act_out[:, j, :]).then_inc(act_stored[j], 16)

        for h in range(PH):
            for side in range(2):
                w = W_Q + (2 + UH) * h + side
                if h == 0 and side == 0:
                    act.wait_ge(evacuated, W_Q)
                if h >= 2:
                    act.wait_ge(ps_mm, 2 * (h - 2) + side + 1)
                evac(w, w % 4, pq[:, h % 2, side, :])
            for t in range(UH):
                u = UH * h + t
                gelu(W_Q + (2 + UH) * h + 2 + t, (2 + t) % 4, u, u % 4, u // 4, first=u < 4)
                if t == UH - 2:
                    act.wait_ge(sel, NSEL * h + SEL_SHIFTED)
                    act.activation(bexp[:, :, :], bexp[:, :, :], ACT.Exp).then_inc(sel_exp, 1)
        for u in range(PH * UH, PH * UH + 8):
            gelu(W_U + u - PH * UH, u % 4, u, u % 4, u // 4)

        U_TAB = PH * UH + 8

        def table(g, first):
            for b in range(8):
                gelu(W_TAB + 8 * g + b, b % 4, U_TAB + 8 * g + b, b % 4, U_TAB // 4 + 2 * g + b // 4)
                half = b // 4
                for q in (2 * b, 2 * b + 1):
                    act.wait_ge(table_mm, 16 * g + q + 1)
                    if q % 8 == 0 and not first:
                        act.wait_ge(table_stored[half], 16 * g)
                    act.activation(stage[:, half, :, 4 * (q % 8):4 * (q % 8) + 4].rearrange("p b t -> p t b"),
                                   aux[q % 4].rearrange("p (t b) -> p t b", t=4), ACT.Copy).then_inc(table_out, 1)
                if b % 4 == 3:
                    act.wait_ge(table_out, 16 * g + 2 * b + 2)
                    act.dma_start(item_of(gate_table, 2 * g + half),
                                  stage[:, half, :, :].rearrange("p b t -> p (b t)")).then_inc(table_stored[half], 16)
        table(0, True)
        with act.Fori(1, 8) as g:
            table(g, False)

        def load_chunk(half, c):
            act.dma_start(act_in[:, half, :, :], act_table[bass.ds(ET * c, ET)].rearrange("e p n -> p e n"))\
                .then_inc(chunk_here[half], 16)
            act.dma_start(gt[:, half, :, :],
                          gate_table.rearrange("g p (c n) -> c p g n", c=NCHUNK)[bass.ds(c, 1)]
                          .rearrange("a p g n -> p (a g) n")).then_inc(chunk_here[half], 16)

        for u in range(NK - 8, NK):
            if u == NK - 2:
                for half in range(2):
                    act.wait_ge(table_stored[half], 16 * 8)
                for j in range(4):
                    act.wait_ge(act_stored[j], 16 * (NK // 4 - 2))
                load_chunk(0, 0)
                load_chunk(1, 1)
            gelu(W_V - NK + u, u % 4, u, u % 4, u // 4)

        def experts(g, first=False, last=False):
            for half in range(2):
                for e in range(ET * half, ET * half + ET):
                    i = 2 * ET * g + e
                    act.wait_ge(e_mul, i + 1)
                    act.wait_ge(tile_done, W_V + i - 3)
                    act.activation(eh[:, e % 4, :], act_m[:, e % 2, :], ACT.Copy).then_inc(e_hi, 1)
                if first and half == 0:
                    for j in range(4):
                        act.wait_ge(act_stored[j], 16 * NK // 4)
                if not last:
                    load_chunk(half, 2 * g + 2 + half)
        experts(0, first=True)
        with act.Fori(1, NCHUNK // 2 - 1) as g:
            experts(g)
        experts(NCHUNK // 2 - 1, last=True)
        norm(2, evacuated, W_V, per=NK // KT)
        norm(3, nout_done, 0, split=2)

        for half in range(2):
            w = W_POOL + 32 * half
            act.wait_ge(evacuated, w)
            for n in range(8):
                i = 8 * half + n
                act.wait_ge(const_dve, 3)
                if i >= 2:
                    act.wait_ge(pl_step, PL_END[i - 2])
                evac(w + n, n % 4, ub[:, n % 2, 16:16 + S])
                act.wait_ge(pl_step, PL_END[i])
                act.activation(ch[:, n, :], um[:, n % 2, :], ACT.Copy).then_inc(pl_hi, 1)
            evac_loop(w + 8, 8, zs, ACT.Silu)
            for n in range(8):
                act.wait_ge(evacuated, w + 17 + n)
                act.activation(dh[:, n, :], um[:, n % 2, :], ACT.Copy).then_inc(pw_hi, 1)
        norm(4, evacuated, W_SB - 8, split=3)

        for half in range(2):
            w = W_SB + 32 * half
            act.wait_ge(evacuated, w)
            evac_loop(w, 4, sqk, scale=0.125)
            evac_loop(w + 4, 4, sqk[:, 4:8, :])
            evac_tokens(w + 8, 2, sv)
            for hd in range(-1, 8):
                i = 8 * half + hd
                if hd < 7:
                    n = i + 1
                    act.wait_ge(SB["qk"], n + 1)
                    if n:
                        act.wait_ge(SB["lb"], n)
                    act.activation(st[:, :], aux3, ACT.Abs).then_inc(SB["abs"], 1)
                    act.wait_ge(SB["abs"], n + 1)
                    act.activation(st[:, :], st[:, :], ACT.Exp, scale=-1.0).then_inc(SB["exp"], 1)
                    act.wait_ge(SB["exp"], n + 1)
                    act.activation(st[:, :], st[:, :], ACT.Ln, bias=one[:, :]).then_inc(SB["ln"], 1)
                if hd >= 0:
                    act.wait_ge(SB["sum"], i + 1)
                    if i:
                        act.wait_ge(SB["o"], i)
                    act.activation(sa[:, :], slb[i % 2][:, :], ACT.Exp).then_inc(SB["a"], 1)
                    evac(w + 16 + hd, 0, zs[:, hd, :], ACT.Silu)
                if hd < 7:
                    act.wait_ge(SB["mask"], n + 1)
                    if n:
                        act.wait_ge(SB["cum"], n)
                    act.activation(slh[:, :], slo[:, :], ACT.Copy).then_inc(SB["hi"], 1)
                if hd >= 0:
                    act.wait_ge(SB["y"], i + 1)
                    act.activation(ch[:, hd, :], sy[:, :], ACT.Copy).then_inc(SB["yhi"], 1)
        norm(5, evacuated, W_END - 8)
        for k in range(KT):
            act.wait_ge(nout_done, KT + k + 1)
            act.dma_start(io["out"][:, k, :], outT[:, k, :]).then_inc(out_stored, 16)
        act.wait_ge(out_stored, 16 * KT)

    @block.vector
    def _(dve):
        def tt(out, a, b, op):
            return dve.tensor_tensor(out, a, b, op)

        def stt(out, a, s, b, op0, op1):
            return dve.scalar_tensor_tensor(out=out, in0=a, scalar=s, in1=b, op0=op0, op1=op1)

        def norm(o, gain, split=None, shift=None, dst=None, out=0):
            dve.wait_ge(nstd_done, o + 1)
            dve.reciprocal(nrs[:, :], nstd[:, :]).then_inc(ninv_done, 1)
            dve.wait_ge(ninv_done, o + 1)
            for k in range(KT + 1):
                if split is None:
                    if k < KT:
                        stt(dst[:, k, :], xT[:, k, :], gain[:, k:k + 1], nrs[:, :], ALU.mult, ALU.mult)\
                            .then_inc(nout_done, 1)
                    continue
                if k < KT:
                    if k >= 2:
                        dve.wait_ge(nlo_done, KT * split + k - 1)
                    stt(nxn[:, k % 2, :], xT[:, k, :], gain[:, k:k + 1], nrs[:, :], ALU.mult, ALU.mult)\
                        .then_inc(nxn_done, 1)
                if k:
                    dve.wait_ge(nhi_done, KT * split + k)
                    stt(al[:, k - 1, :], nxn[:, (k - 1) % 2, :], zero[:, 0:1] if shift is None else shift[:, k - 1:k],
                        ah[:, k - 1, :].bitcast(F32), ALU.add, ALU.subtract).then_inc(nlo_done, 1)

        dve.wait_ge(const_pool, NCONST)
        dve.wait_ge(small_here, NSMALL)
        dve.wait_ge(ada_used, NADA)
        tt(ada[:, :], psum[:, 7, 0:NADA], VEC["b_ada"], ALU.add).then_inc(ada_done, 1)
        dve.wait_ge(ada_done, 1)
        stt(gs[:, 0, :], scale1, 1.0, VEC["norm1_g"], ALU.add, ALU.mult).then_inc(const_vec, 1)
        stt(gs[:, 1, :], scale2, 1.0, VEC["norm2_g"], ALU.add, ALU.mult).then_inc(const_vec, 1)
        dve.wait_ge(const_vec, 2)
        for n, window in enumerate(WINDOWS):
            dve.tensor_scalar(inv_count[:, n, :], iota16[:, :], 1.0, float(window), ALU.add, ALU.min).then_inc(const_vec, 1)
        dve.wait_ge(const_vec, 6)
        dve.reciprocal(inv_count[:, :, :], inv_count[:, :, :]).then_inc(const_dve, 1)
        dve.wait_ge(const_dve, 1)
        norm(0, gs[:, 0, :], split=0, shift=shift1)


        top = [0]

        def chain(ins):
            top[0] += 1
            ins.then_inc(top_step, 1)
            dve.wait_ge(top_step, top[0])

        for item in SEQ_G:
            kind = item[0]
            if kind == "ckv":
                dve.wait_ge(CA.sem, CA.at(0, "std"))
                dve.reciprocal(nrs[:, :], nstd[:, :]).then_inc(CD.sem, 1)
                dve.wait_ge(CD.sem, CD.at(0, "rstd"))
                for k in range(2):
                    stt(ckv[:, k, :], ckv[:, k, :], VEC["dsa_kv_norm_g"][:, k:k + 1], nrs[:, :], ALU.mult, ALU.mult)\
                        .then_inc(CD.sem, 1)
                dve.wait_ge(CP.sem, CP.at(0, "iw"))
                dve.tensor_scalar(iwn[:, :, :], aux[3].rearrange("p (t n) -> p t n", t=TT)[:, :, 32:32 + IH],
                                  IH ** -0.5, None, ALU.mult).then_inc(CD.sem, 1)
                dve.wait_ge(CD.sem, CD.at(0, "c1"))
                dve.memset(gat[:, :, :], 0.0).then_inc(const_vec, 1)
                dve.wait_ge(const_vec, 7)
                dve.wait_ge(evacuated, W_G)
            elif kind == "prep":
                h = item[1]
                m = gt1[:, 1, :]
                dve.wait_ge(GP.sem, GP.at(h, "gate"))
                dve.wait_ge(GA.sem, GA.at(h, "abs"))
                dve.tensor_scalar(m, aux[0], VEC["gla_b_gate"][:, h:h + 1], 0.0, ALU.add, ALU.min).then_inc(GD.sem, 1)
                dve.wait_ge(GD.sem, GD.at(h, "min"))
                dve.wait_ge(GA.sem, GA.at(h, "ln"))
                tt(m, m, gt1[:, 0, :], ALU.subtract).then_inc(GD.sem, 1)
                dve.wait_ge(GD.sem, GD.at(h, "logalpha"))
                dve.tensor_tensor_scan(gb[:, :], chunk_start[:, :], m, 0.0, ALU.mult, ALU.add).then_inc(GD.sem, 1)
                dve.wait_ge(GD.sem, GD.at(h, "cumsum"))
                b3 = gb[:, :].rearrange("p (c t) -> p c t", t=CH)
                tt(gke[:, :].rearrange("p (c t) -> p c t", t=CH), b3[:, :, CH - 1:CH].broadcast_to([P, S // CH, CH]),
                   b3, ALU.subtract).then_inc(GD.sem, 1)
                dve.wait_ge(GA.sem, GA.at(h, "eb"))
                stt(gqd[:, :], qk[:, 2 * h, :], GDK ** -0.5, geb[:, :], ALU.mult, ALU.mult).then_inc(GD.sem, 1)
                dve.wait_ge(GA.sem, GA.at(h, "enb"))
                tt(gki[:, :], gki[:, :], qk[:, 2 * h + 1, :], ALU.mult).then_inc(GD.sem, 1)
                dve.wait_ge(GA.sem, GA.at(h, "ekd"))
                tt(gke[:, :], gke[:, :], qk[:, 2 * h + 1, :], ALU.mult).then_inc(GD.sem, 1)
            elif kind == "attn":
                h = item[1]
                dve.wait_ge(GP.sem, GP.at(h, "attn"))
                dve.copy_predicated(gat[:, :, :], block_causal[:, :].bitcast(U32).unsqueeze(1).broadcast_to([P, TT, P]),
                                    aux[1].rearrange("p (t n) -> p t n", t=TT)).then_inc(GD.sem, 1)
            elif kind == "kv":
                h, t = item[1:]
                dve.wait_ge(GP.sem, GP.at(h, f"kv{t}"))
                for c in range(2 * t, min(2 * t + 2, 7)):
                    new = aux[2 - c % 2][:, 0:GDV]
                    if c == 0:
                        dve.tensor_copy(gst[:, 0, :], new).then_inc(GD.sem, 1)
                    else:
                        dve.wait_ge(GD.sem, GD.at(h, f"s{c}"))
                        stt(gst[:, c, :], gst[:, c - 1, :], geb[:, CH * c + CH - 1:CH * c + CH], new,
                            ALU.mult, ALU.add).then_inc(GD.sem, 1)
            elif kind == "o":
                h = item[1]
                dve.wait_ge(GA.sem, GA.at(h, "std"))
                dve.reciprocal(gke[:, :], gke[:, :]).then_inc(GD.sem, 1)
                dve.wait_ge(GD.sem, GD.at(h, "rstd"))
                dve.wait_ge(evacuated, W_G + 4 * h + 2)
                for v in range(2):
                    stt(gt1[:, v, :], aux[1 - v], VEC["gla_norm_g"][:, 2 * h + v:2 * h + v + 1], gke[:, :],
                        ALU.mult, ALU.mult).then_inc(GD.sem, 1)
                for v in range(2):
                    dve.wait_ge(GD.sem, GD.at(h, f"og{v}"))
                    tt(gr[:, 2 * h + v, :], gr[:, 2 * h + v, :], gt1[:, v, :], ALU.mult).then_inc(GD.sem, 1)
            elif kind == "idx":
                t, h = item[1:]
                i = (t - 1) * IH + h
                n = P * (t + 1)
                dve.wait_ge(idx_relu, i + 1)
                dve.wait_ge(CD.sem, CD.at(0, "iw"))
                if h == 0:
                    dve.tensor_scalar(score[:, 0:n], rel[:, i % 2, 0:n], iwn[:, t, h:h + 1], None, ALU.mult)\
                        .then_inc(idx_acc, 1)
                else:
                    dve.wait_ge(idx_acc, i)
                    stt(score[:, 0:n], rel[:, i % 2, 0:n], iwn[:, t, h:h + 1], score[:, 0:n], ALU.mult, ALU.add)\
                        .then_inc(idx_acc, 1)
            elif kind == "fill":
                t = item[1]
                dve.wait_ge(idx_acc, t * IH)
                chain(dve.copy_predicated(score[:, P * t:P * t + P], strict[:, :].bitcast(U32), neg[:, :]))
            elif kind == "top":
                n = P * (item[1] + 1)
                chain(dve.max(m8[:, :], score[:, 0:n]))
                chain(dve.match_replace(score[:, 0:n], m8[:, :], score[:, 0:n], TAKEN))
            elif kind == "mask":
                t = item[1]
                n = P * (t + 1)
                if t == 0:
                    chain(dve.memset(maskneg[:, 0, 0:P], 0.0))
                else:
                    chain(dve.tensor_scalar(maskneg[:, t, 0:n], score[:, 0:n], -1e38, NEG, ALU.is_ge, ALU.mult))
                chain(dve.copy_predicated(maskneg[:, t, P * t:P * t + P], strict[:, :].bitcast(U32), neg[:, :]))

        for item in SEQ_D:
            kind = item[0]
            if kind == "ga":
                n = item[1]
                dve.wait_ge(ga_hi, n + 1)
                tt(bl[:, n, :], gr[:, n, :], bh[:, n, :].bitcast(F32), ALU.subtract).then_inc(ga_lo, 1)
            elif kind == "lin":
                w = item[1]
                if w >= W_A:
                    n = w - W_A
                    if n == 0:
                        dve.wait_ge(evacuated, W_A)
                    dve.wait_ge(tile_done, w + 1)
                    tt(gr[:, n, :], acc[w % 4], gr[:, n, :], ALU.mult).then_inc(evacuated, 1)
            elif kind == "score":
                i = item[1]
                h, t = divmod(i, TT)
                n = P * (t + 1)
                if i:
                    dve.wait_ge(DD.sem, DD.at(i - 1, "logit"))
                stt(tneg[:, 0:n], relpos[:, 384 - P * t:384 - P * t + n], 2.0 ** -(h + 1), maskneg[:, t, 0:n],
                    ALU.mult, ALU.add).then_inc(DD.sem, 1)
                dve.wait_ge(DD.sem, DD.at(i, "bias"))
                dve.wait_ge(DP_s, i + 1)
                if i >= 2:
                    dve.wait_ge(DP_t, i - 1)
                stt(prob[:, i % 2, 0:n], aux[0][:, 0:n], P ** -0.5, tneg[:, 0:n], ALU.mult, ALU.add)\
                    .then_inc(DD.sem, 1)
                dve.wait_ge(DD.sem, DD.at(i, "logit"))
                dve.tensor_reduce(rowstat[:, 0, i:i + 1], prob[:, i % 2, 0:n], AX.X, ALU.max, negate=True)\
                    .then_inc(DD.sem, 1)
                dve.wait_ge(DA_e, i + 1)
                dve.reciprocal(rowstat[:, 2, i:i + 1], rowstat[:, 1, i:i + 1]).then_inc(DD.sem, 1)
            elif kind == "pt":
                i = item[1]
                t = i % TT
                dve.wait_ge(DP_t, i + 1)
                if i >= TT and t == 0:
                    dve.wait_ge(DP_o, i // TT)
                dve.tensor_copy(pT[:, 0:t + 1, P * t:P * t + P],
                                aux[1][:, 0:P * (t + 1)].rearrange("p (b n) -> p b n", n=P)).then_inc(pT_out, 1)

        for n in range(KT):
            dve.wait_ge(db_hi, n + 1)
            tt(bl[:, n, :], qk[:, n, :], bh[:, n, :].bitcast(F32), ALU.subtract).then_inc(db_lo, 1)
        dve.wait_ge(evacuated, W_B)
        for n in range(KT + 1):
            if n < KT:
                w = W_B + n
                dve.wait_ge(tile_done, w + 1)
                tt(zb[:, n, :], acc[w % 4], zb[:, n, :], ALU.mult).then_inc(evacuated, 1)
                dve.wait_ge(evacuated, w + 1)
                tt(gr[:, n, :], gr[:, n, :], zb[:, n, :], ALU.add).then_inc(y_step, 1)
            if n:
                dve.wait_ge(y_hi, n)
                tt(al[:, n - 1, :], gr[:, n - 1, :], ah[:, n - 1, :].bitcast(F32), ALU.subtract).then_inc(y_lo, 1)
        for n in range(KT):
            w = W_O + n
            dve.wait_ge(tile_done, w + 1)
            stt(xT[:, n, :], acc[w % 4], gate1[:, n:n + 1], xT[:, n, :], ALU.mult, ALU.add).then_inc(evacuated, 1)
        norm(1, gs[:, 1, :], split=1, shift=shift2)

        for h in range(PH):
            n = [NSEL * h]

            def step(ins):
                n[0] += 1
                return ins.then_inc(sel, 1)

            def settle():
                dve.wait_ge(sel, n[0])

            pairs = [(side, t) for side in range(2) for t in range(TT)]
            scores = [psum[:, 4 + 2 * (h % 2) + side, :] for side in range(2)]
            dve.wait_ge(ps_mm, 2 * h + 2)
            for side, t in pairs:
                step(dve.max(topv[:, side, t, 0:8], scores[side][:, P * t:P * t + P]))
            settle()
            for side, t in pairs:
                step(dve.max_index(topi[:, side, t, 0:8], topv[:, side, t, 0:8], scores[side][:, P * t:P * t + P]))
            for side, t in pairs:
                step(dve.match_replace(swork[:, side, t, :], topv[:, side, t, 0:8], scores[side][:, P * t:P * t + P],
                                       TAKEN))
            settle()
            for side, t in pairs:
                step(dve.max(topv[:, side, t, 8:16], swork[:, side, t, :]))
            settle()
            for side, t in pairs:
                step(dve.max_index(topi[:, side, t, 8:16], topv[:, side, t, 8:16], swork[:, side, t, :]))
            grid = [P, TT, PK, PK]
            step(tt(cand[:, :, :].rearrange("p t (a b) -> p t a b", a=PK), topv[:, 0, :, :].unsqueeze(3).broadcast_to(grid),
                    topv[:, 1, :, :].unsqueeze(2).broadcast_to(grid), ALU.add))
            settle()
            step(dve.tensor_copy(topf[:, :, :, :].rearrange("p s t k -> p (s t k)"),
                                 topi[:, :, :, :].rearrange("p s t k -> p (s t k)")))
            for t in range(TT):
                step(dve.max(best[:, t, 0:8], cand[:, t, :]))
            settle()
            for t in range(TT):
                step(dve.max_index(besti[:, t, 0:8], best[:, t, 0:8], cand[:, t, :]))
            settle()
            for t in range(TT):
                step(dve.match_replace(cand[:, t, :], best[:, t, 0:8], cand[:, t, :], TAKEN))
            settle()
            for t in range(TT):
                step(dve.max(best[:, t, 8:16], cand[:, t, :]))
            settle()
            for t in range(TT):
                step(dve.max_index(besti[:, t, 8:16], best[:, t, 8:16], cand[:, t, :]))
            step(tt(bexp[:, :, :], best[:, :, :], best[:, :, 0:1].broadcast_to([P, TT, PK]), ALU.subtract))
            assert n[0] == NSEL * h + SEL_SHIFTED
            settle()
            step(dve.tensor_scalar(bestij[:, 0, :, :], besti[:, :, :], 4, None, ALU.logical_shift_right))
            step(dve.tensor_scalar(bestij[:, 1, :, :], besti[:, :, :], 15, None, ALU.bitwise_and))
            settle()
            step(dve.tensor_copy(bestf[:, :, :, :].rearrange("p s t k -> p (s t k)"),
                                 bestij[:, :, :, :].rearrange("p s t k -> p (s t k)")))
            settle()
            for side in range(2):
                step(tt(onehot[:, :, :], bestf[:, side, :, :].rearrange("p t k -> p (t k)").unsqueeze(2)
                        .broadcast_to([P, TT * PK, PK]), iota16[:, :].unsqueeze(1).broadcast_to([P, TT * PK, PK]),
                        ALU.is_equal))
                settle()
                hot4 = onehot[:, :, :].rearrange("p (t k) j -> p t k j", t=TT)
                step(tt(hot4, hot4, topf[:, side, :, :].unsqueeze(2).broadcast_to(grid), ALU.mult))
                settle()
                step(dve.tensor_reduce(slots[:, side, :, PK * h:PK * h + PK], hot4, AX.X, ALU.add))
                settle()
            dve.wait_ge(sel_exp, h + 1)
            step(dve.tensor_reduce(bsum[:, :], bexp[:, :, :], AX.X, ALU.add))
            settle()
            step(dve.reciprocal(binv[:, :], bsum[:, :]))
            settle()
            step(tt(slots[:, 2, :, PK * h:PK * h + PK], bexp[:, :, :], binv[:, :].unsqueeze(2).broadcast_to([P, TT, PK]),
                    ALU.mult))
            assert n[0] == NSEL * (h + 1)

        for part in range(2):
            dve.wait_ge(sT_mm, part + 1)
            dve.tensor_copy(slotT[:, part, :], aux[part]).then_inc(sT_step, 1)
        dve.wait_ge(sT_mm, 3)
        dve.tensor_copy(gpart[:, 0, :], aux[2]).then_inc(sT_step, 1)
        for part in range(2):
            dve.wait_ge(sT_step, 3 + 2 * part)
            dve.tensor_copy(gp16[:, part, :], gpart[:, part, :]).then_inc(sT_step, 1)
            dve.wait_ge(sT_step, 4 + 2 * part)
            tt(gpart[:, part + 1, :], gpart[:, part, :], gp16[:, part, :], ALU.subtract).then_inc(sT_step, 1)
        dve.wait_ge(sT_step, 7)
        dve.tensor_copy(gp16[:, 2, :], gpart[:, 2, :]).then_inc(sT_step, 1)
        dve.wait_ge(sT_step, 8)

        def one_hots(g, first):
            iota8 = iota_row[:, :].unsqueeze(1).broadcast_to([P, 8, P])
            for b in range(8):
                tok = bass.ds(64 * g + 8 * b, 8)
                if not (first and b < 2):
                    dve.wait_ge(table_mm, 16 * g + 2 * b - 2)
                if not (first and b == 0):
                    dve.wait_ge(HOT.sem, HOT.at(8 * g + b - 1, "gates"))
                tt(hot[:, b % 2, 0, :, :], iota8, slotT[:, 0, tok].unsqueeze(2).broadcast_to([P, 8, P]), ALU.is_equal)\
                    .then_inc(HOT.sem, 1)
                tt(hotb[:, :, :], iota8, slotT[:, 1, tok].unsqueeze(2).broadcast_to([P, 8, P]), ALU.is_equal)\
                    .then_inc(HOT.sem, 1)
                dve.wait_ge(HOT.sem, HOT.at(8 * g + b, "key2"))
                tt(hot[:, b % 2, 1:4, :, :], hotb[:, :, :].unsqueeze(1).broadcast_to([P, 3, 8, P]),
                   gp16[:, :, tok].unsqueeze(3).broadcast_to([P, 3, 8, P]), ALU.mult).then_inc(HOT.sem, 1)
        one_hots(0, True)
        with dve.Fori(1, 8) as g:
            one_hots(g, False)

        with dve.Fori(0, NCHUNK // 2) as g:
            for half in range(2):
                for e in range(ET):
                    i = 2 * ET * g + ET * half + e
                    if e == 0:
                        dve.wait_ge(chunk_here[half], 32 * g + 32)
                    tt(act_m[:, e % 2, :].rearrange("p (g t) -> p g t", t=TG),
                       act_in[:, half, e, :].rearrange("p (g t) -> p g t", t=TG), gt[:, half, :, TG * e:TG * e + TG],
                       ALU.mult).then_inc(e_mul, 1)
                    dve.wait_ge(e_hi, i + 1)
                    dve.wait_ge(tile_done, W_V + i - 3)
                    tt(el[:, e % 4, :], act_m[:, e % 2, :], eh[:, e % 4, :].bitcast(F32), ALU.subtract)\
                        .then_inc(e_lo, 1)
        dve.wait_ge(tile_done, W_POOL)
        for n in range(KT):
            stt(xT[:, n, :], psum[:, (n + 4) % 8, :], gate2[:, n:n + 1], xT[:, n, :], ALU.mult, ALU.add)\
                .then_inc(evacuated, NK // KT)
        dve.wait_ge(evacuated, W_POOL)
        norm(2, VEC["final_norm_g"], dst=xT)
        dve.wait_ge(nout_done, KT)
        norm(3, VEC["norm_g0"], split=2)

        dve.wait_ge(nlo_done, 3 * KT)
        dve.memset(ub[:, :, 0:16], 0.0).then_inc(const_dve, 1)
        dve.memset(us[:, :, 0:16], 0.0).then_inc(const_dve, 1)
        dve.wait_ge(const_dve, 3)
        n_step = 0
        for half in range(2):
            w = W_POOL + 32 * half
            for n in range(8):
                i = 8 * half + n
                which = 2 * half + n // 4
                window = WINDOWS[which]
                u, src, m = ub[:, n % 2, :], ub[:, n % 2, :], um[:, n % 2, :]
                dve.wait_ge(evacuated, w + n + 1)
                for level in range(which + 1):
                    dst = us[:, level % 2, :]
                    tt(dst[:, 16:16 + S], src[:, 16:16 + S], src[:, 16 - 2 ** level:16 + S - 2 ** level], ALU.add)\
                        .then_inc(pl_step, 1)
                    n_step += 1
                    dve.wait_ge(pl_step, n_step)
                    src = dst
                stt(m[:, 16:S], src[:, 32:16 + S], 1.0 / window, u[:, 32:16 + S], ALU.mult, ALU.subtract)\
                    .then_inc(pl_step, 1)
                tt(m[:, 0:16], src[:, 16:32], inv_count[:, which, :], ALU.mult).then_inc(pl_step, 1)
                n_step += 2
                dve.wait_ge(pl_step, n_step)
                tt(m[:, 0:16], m[:, 0:16], u[:, 16:32], ALU.subtract).then_inc(pl_step, 1)
                n_step += 1
                assert n_step == PL_END[i]
                dve.wait_ge(pl_hi, i + 1)
                tt(cl[:, n, :], m, ch[:, n, :].bitcast(F32), ALU.subtract).then_inc(pl_lo, 1)
            dve.wait_ge(evacuated, w + 16)
            for n in range(8):
                m = um[:, n % 2, :]
                dve.wait_ge(tile_done, w + 17 + n)
                stt(m, acc[n % 4], VEC["pool_scale"][:, 8 * half + n:8 * half + n + 1], zs[:, n, :], ALU.mult, ALU.mult)\
                    .then_inc(evacuated, 1)
                dve.wait_ge(pw_hi, 8 * half + n + 1)
                tt(dl[:, n, :], m, dh[:, n, :].bitcast(F32), ALU.subtract).then_inc(pw_lo, 1)
            for n in range(8):
                dve.wait_ge(tile_done, w + 25 + n)
                tt(xT[:, n, :], acc[n % 4], xT[:, n, :], ALU.add).then_inc(evacuated, 1)
        norm(4, VEC["norm_g1"], split=3)

        diag = strict[:, :].unsqueeze(1).broadcast_to([P, TT, P])
        for half in range(2):
            w = W_SB + 32 * half
            for hd in range(-1, 8):
                i = 8 * half + hd
                n = i + 1
                if hd < 7:
                    dve.wait_ge(SB["ln"], n + 1)
                    if n >= 2:
                        dve.wait_ge(SB["a"], n - 1)
                    stt(slb[n % 2][:, :], aux3, 0.0, st[:, :], ALU.min, ALU.subtract).then_inc(SB["lb"], 1)
                if hd >= 0:
                    dve.wait_ge(SB["cum"], i + 1)
                    tt(slb[i % 2][:, :], acc3, slb[i % 2][:, :], ALU.add).then_inc(SB["sum"], 1)
                if hd < 7:
                    dve.wait_ge(SB["lb"], n + 1)
                    if n:
                        dve.wait_ge(SB["losplit"], n)
                    tt(slo[:, :], slb[n % 2][:, :], aux3, ALU.subtract).then_inc(SB["lo"], 1)
                if hd >= 0:
                    dve.wait_ge(SB["a"], i + 1)
                    square = sa[:, 0:S].rearrange("p (b n) -> p b n", n=P)
                    tt(square, square, diag, ALU.mult).then_inc(SB["amask"], 1)
                if hd < 7:
                    dve.wait_ge(SB["lo"], n + 1)
                    square = slo[:, 0:S].rearrange("p (b n) -> p b n", n=P)
                    tt(square, square, diag, ALU.mult).then_inc(SB["mask"], 1)
                    dve.wait_ge(SB["hi"], n + 1)
                    tt(sll[:, :], slo[:, :], slh[:, :].bitcast(F32), ALU.subtract).then_inc(SB["losplit"], 1)
                if hd >= 0:
                    dve.wait_ge(SB["o"], i + 1)
                    dve.wait_ge(evacuated, w + 16 + hd + 1)
                    tt(sy[:, :], aux[3], zs[:, hd, :], ALU.mult).then_inc(SB["y"], 1)
                    dve.wait_ge(SB["yhi"], i + 1)
                    tt(cl[:, hd, :], sy[:, :], ch[:, hd, :].bitcast(F32), ALU.subtract).then_inc(SB["ylo"], 1)
            for n in range(8):
                dve.wait_ge(tile_done, w + 25 + n)
                tt(xT[:, n, :], acc[n % 4], xT[:, n, :], ALU.add).then_inc(evacuated, 1)
        norm(5, VEC["norm_f"], dst=outT)

    block_cm.__exit__(None, None, None)


def _tiles(w):
    k, n = w.shape[0] // 128, w.shape[1] // 128
    return w.reshape(k, 128, n, 128).transpose(2, 1, 0, 3).reshape(n, 128, k * 128)


def _token_tiles(w):
    n = w.shape[1] // 512
    return w.reshape(4, 2, 128, n, 512).transpose(3, 0, 2, 1, 4).reshape(4 * n, 128, 1024)


def _columns(v):
    return v.reshape(-1, 128).T


def _layout(i):
    import numpy as np

    cut = np.cumsum((512, 512, 1024, 1024, 16, 1024, 256, 512, 64, 8, 1024))
    gq, gk, gv, gr, glow, dq, dkv, iq, ik, iw, za, zb = np.split(i["w_in"][0], cut, axis=1)
    cat = np.concatenate
    head = lambda w, h, n=128: w[:, n * h:n * h + n]
    w_in = cat([
        _tiles(cat([glow, glow] + [iw] * 12, axis=1)), _tiles(cat([ik, ik], axis=1)), _tiles(dkv),
        _tiles(cat([head(w, h) for h in range(4) for w in (gq, gk)], axis=1)),
        _token_tiles(gv), _tiles(iq),
        *[_tiles(cat([head(gr, h, 256), head(dq, h, 256)], axis=1)) for h in range(4)],
        _tiles(za), _tiles(zb),
    ])
    vec = cat([_columns(v) for v in (
        i["b_ada"][0], i["norm1_g"][0], i["norm2_g"][0], i["final_norm_g"], i["gla_b_gate"][0], i["gla_norm_g"][0],
        i["dsa_kv_norm_g"][0], i["norm_g_2"][0], i["norm_g_2"][1], i["norm_f_2"], i["pool_scale_2"][0])], axis=1)
    xb, z = np.split(i["pool_w_in_2"][0], 2, axis=1)
    pool_in = cat([_tiles(w[:, 1024 * h:1024 * h + 1024]) for h in range(2) for w in (xb, z)])
    pool_w = cat([_tiles(w) for w in i["pool_w_2"][0]])
    halves = lambda w: cat([_tiles(w[1024 * h:1024 * h + 1024]) for h in range(2)])
    q, k, v, z = np.split(i["sb_w_in_2"][0], (1024, 2048, 4096), axis=1)
    sb_in = cat([t for h in range(2) for t in (
        _tiles(q[:, 512 * h:512 * h + 512]), _tiles(k[:, 512 * h:512 * h + 512]),
        _token_tiles(v[:, 1024 * h:1024 * h + 1024]), _tiles(z[:, 1024 * h:1024 * h + 1024]))])
    u = i["peer_u"][0].reshape(128, 128, 8, 128).transpose(1, 3, 2, 0).reshape(128, 128, 1024)
    v = i["peer_v"][0].reshape(128, 128, 1024).transpose(1, 0, 2)
    return {
        "x": i["x"][0].T.reshape(8, 128, 512).transpose(1, 0, 2),
        "c": _columns(i["c"][0]),
        "vec": vec,
        "w_ada": _tiles(i["w_ada"][0]),
        "w_in": w_in,
        "gla_w_gate_up": i["gla_w_gate_up"][0],
        "dsa_w_uk": i["dsa_w_uk"][0],
        "dsa_w_uv": i["dsa_w_uv"][0].reshape(8, 2, 128, 128).transpose(0, 2, 1, 3),
        "w_branch_a": _tiles(i["w_branch_a"][0]),
        "w_branch_b": _tiles(i["w_branch_b"][0]),
        "w_out": _tiles(i["w_out"][0]),
        "peer_w_q": _tiles(i["peer_w_q"][0]),
        "peer_sub_keys": np.stack([i["peer_sub_keys_1"][0].T, i["peer_sub_keys_2"][0].T], axis=1),
        "peer_u": u,
        "peer_v": v,
        "pool_w_in": pool_in,
        "pool_w": pool_w,
        "pool_w_out": halves(i["pool_w_out_2"][0]),
        "sb_w_in": sb_in,
        "sb_w_out": halves(i["sb_w_out_2"][0]),
    }


def kernel(**inputs):
    import numpy as _np
    import concourse.bacc as _bacc
    from concourse.bass_utils import run_bass_kernel_spmd as _run

    nc = _bacc.Bacc("TRN2", target_bir_lowering=False, num_devices=1)
    arrays, io = {}, {}
    for name, a in _layout({k: _np.asarray(v) for k, v in inputs.items()}).items():
        a = _np.ascontiguousarray(a)
        arrays[f"in_{name}"] = a
        io[name] = nc.dram_tensor(f"in_{name}", a.shape, mybir.dt.from_np(a.dtype), kind="ExternalInput").ap()
    io["out"] = nc.dram_tensor("out", (128, 8, 512), F32, kind="ExternalOutput").ap()
    build(nc, io)
    r = _run(nc, [arrays], core_ids=[0])
    out = r.results[0]["out"]
    return _np.ascontiguousarray(out.transpose(1, 0, 2).reshape(1024, 512).T)[None]
```

```python
import concourse.bass as bass
from concourse import mybir

P = 128
F32 = mybir.dt.float32
F32R = mybir.dt.float32r
BF16 = mybir.dt.bfloat16
U32 = mybir.dt.uint32
ACT = mybir.ActivationFunctionType
ALU = mybir.AluOpType
AX = mybir.AxisListType

S = 512
TT = S // P
D = 1024
KT = D // P
EPS = 1e-6

GH, GDK, GDV, CH = 4, 128, 256, 64
TAU = 16.0
DH, LAT, IH, IDD, TOPK = 8, 256, 8, 64, 128
PH, NK, PK = 8, 128, 16
ET = 8
NCHUNK = NK // ET
UH = 6
VEC_PARTS = (("b_ada", 48), ("norm1_g", 8), ("norm2_g", 8), ("final_norm_g", 8), ("gla_b_gate", 4),
             ("gla_norm_g", 8), ("dsa_kv_norm_g", 2), ("norm_g0", 8), ("norm_g1", 8), ("norm_f", 8),
             ("pool_scale", 16))
TG = 32
WINDOWS = (2, 4, 8, 16)
NEG = -1e30
TAKEN = -3e38

NADA = 6 * KT
W_L1, W_G, W_ZA, W_A, W_ZB, W_B, W_O = 0, 24, 40, 48, 56, 64, 72
W_Q = 80
W_U = W_Q + PH * (2 + UH)
W_TAB = W_U + 8
W_V = W_Q + 2 * PH + NK
W_POOL = W_V + NK
W_SB = W_POOL + 64
W_END = W_SB + 64
RAW, SPLIT = 4, 2
PARTS = 4
NCONST = 20
NSMALL = 16 * 3
NSEL = 75
SEL_SHIFTED = 63
SB_REGIONS = [[(0, 0, 128), (512, 128, 384)], [(128, 128, 128), (1024, 256, 256)],
              [(256, 256, 128), (896, 384, 128)], [(384, 384, 128)]]


class Steps:

    def __init__(self, sem, *names):
        self.sem, self.names = sem, names

    def at(self, turn, name):
        return len(self.names) * turn + self.names.index(name) + 1


def lin_parts(first, count):
    return [("lin", w, part) for w in range(first, first + count) for part in range(PARTS)]


def schedule_gla():
    main = []
    for h in range(GH):
        fill = iter(lin_parts(W_G + 4 * h, 4))
        for item, parts in ((("prep", h), 5), (("attn", h), 2), (("kv", h, 0), 1), (("kv", h, 1), 1), (("kv", h, 2), 1),
                            (("kv", h, 3), 1), (("o", h), 2), (("ms", h), 3)):
            main += [item] + [next(fill) for _ in range(parts)]
    side = [("mask", 0)]
    for tt in range(1, TT):
        side += [("idx", tt, h) for h in range(IH)] + [("fill", tt)]
        side += [("top", tt, r) for r in range(TOPK // 8)] + [("mask", tt)]
    share = [2 if item[0] == "idx" else 1 for item in side]
    out, done = [("ckv",)], 0
    for n, item in enumerate(main):
        out.append(item)
        while done < len(side) and sum(share[:done + 1]) * len(main) <= sum(share) * (n + 1):
            out.append(side[done])
            done += 1
    return out


def schedule_dsa():
    fill = lin_parts(W_ZA, 2 * KT)
    out = [("ga", n) for n in range(KT)] + fill[:PARTS] + [("qlat", 0)]
    fill = fill[PARTS:]
    for i in range(DH * TT + 1):
        if i < DH * TT:
            out.append(("score", i))
        if i % TT == TT - 1 and i // TT + 1 < DH:
            out.append(("qlat", i // TT + 1))
        out += fill[:1]
        if i >= 1:
            out.append(("pt", i - 1))
        if i >= 1 and i % TT == 0:
            out.append(("out", i // TT - 1))
        out += fill[1:2]
        fill = fill[2:]
        if i >= 1 and i % TT == 0:
            out.append(("oval", i // TT - 1))
    return out + fill


def build(nc, io):
    base = 16512

    def sb(name, shape, dt, kb):
        return nc.alloc_sbuf_tensor_at(name, shape, dt, offset=base + int(kb * 1024))

    xT = sb("xT", [P, KT, S], F32, 0)
    ah = sb("ah", [P, KT, S], F32R, 16)
    al = sb("al", [P, KT, S], F32R, 32)
    raw = [sb(f"raw{i}", [P, D], F32, 48 + 4 * i) for i in range(RAW)]
    wh = [sb(f"wh{i}", [P, D], F32R, 64 + 4 * i) for i in range(SPLIT)]
    wl = [sb(f"wl{i}", [P, D], F32R, 72 + 4 * i) for i in range(SPLIT)]
    cpos = [80.0]

    def const(name, shape, dt=F32):
        n = 1
        for d in shape[1:]:
            n *= d
        size = n * (2 if dt == BF16 else 4)
        t = sb(name, shape, dt, cpos[0])
        cpos[0] += (size + 31) // 32 * 32 / 1024
        return t

    ident = const("ident", [P, P])
    ones = const("ones", [P, P])
    onesr = const("onesr", [P, P], F32R)
    strict = const("strict", [P, P])
    block_causal = const("block_causal", [P, P])
    trilr = const("trilr", [P, P], F32R)
    neg = const("neg", [P, P])
    chunk_start = const("chunk_start", [P, S])
    iota_row = const("iota_row", [P, P], BF16)
    iota16 = const("iota16", [P, PK])
    zero = const("zero", [P, 8])
    eps = const("eps", [P, 1])
    one = const("one", [P, 1])
    ada = const("ada", [P, NADA])
    vec = const("vec", [P, io["vec"].shape[1]])
    ada_sum = const("ada_sum", [P, NADA])
    gs = const("gs", [P, 2, KT])
    inv_count = const("inv_count", [P, 4, 16])
    assert cpos[0] <= 89, cpos[0]
    VEC, at = {}, 0
    for name, n in VEC_PARTS:
        VEC[name] = vec[:, at:at + n]
        at += n
    ada_part = [ada[:, KT * i:KT * i + KT] for i in range(6)]
    shift1, scale1, gate1, shift2, scale2, gate2 = ada_part

    nsq = sb("nsq", [P, 2, S], F32, 169)
    nxn = sb("nxn", [P, 2, S], F32, 173)
    nlog = sb("nlog", [P, S], F32, 177)
    nrs = sb("nrs", [P, S], F32, 179)

    cb = sb("cb", [P, D], F32, 165)
    ada_first = sb("ada_first", [P, 8, 2, D], F32, 89)
    ada_rest = sb("ada_rest", [P, 3, 2, D], F32, 105)

    qk = sb("qk", [P, 2 * GH, S], F32, 89)
    gr = sb("gr", [P, KT, S], F32, 105)
    maskneg = sb("maskneg", [P, TT, S], F32, 121)
    ckv = sb("ckv", [P, 2, S], F32, 129)
    ckvn = sb("ckvn", [P, TT, LAT], F32, 133)
    gv = sb("gv", [P, TT, D], F32, 137)
    iq = sb("iq", [P, 4, S], F32, 153)
    ik = sb("ik", [P, S], F32, 161)
    misc = sb("misc", [P, S], F32, 163)
    gt1 = sb("gt1", [P, 2, S], F32, 165)
    gb = sb("gb", [P, S], F32, 169)
    geb = sb("geb", [P, S], F32, 171)
    gki = sb("gki", [P, S], F32, 173)
    gke = sb("gke", [P, S], F32, 175)
    gqd = sb("gqd", [P, S], F32, 177)
    gat = sb("gat", [P, TT, P], F32, 179)
    gket = sb("gket", [P, TT, P], F32, 181)
    gst = sb("gst", [P, 7, GDV], F32, 183)
    score = sb("score", [P, S], F32, 190)
    rel = sb("rel", [P, 2, S], F32, 192)
    iwn = sb("iwn", [P, TT, IH], F32, 196)
    m8 = sb("m8", [P, 8], F32, 197)
    relpos = sb("relpos", [P, 896], F32, 198)
    gwu = sb("gwu", [16, GH * GDK], F32, 202)
    bh = sb("bh", [P, KT, S], F32R, 137)
    bl = sb("bl", [P, KT, S], F32R, 153)
    qlat = sb("qlat", [P, 2, S], F32, 169)
    uk = sb("uk", [P, 2, LAT], F32, 173)
    uv = sb("uv", [P, 2, 2, P], F32, 175)
    prob = sb("prob", [P, 2, S], F32, 177)
    tneg = sb("tneg", [P, S], F32, 181)
    pT = sb("pT", [P, TT, S], F32, 183)
    olat = sb("olat", [P, 2, S], F32, 191)
    rowstat = sb("rowstat", [P, 3, DH * TT], F32, 196.5)
    zb = sb("zb", [P, KT, S], F32, 169)
    pq = sb("pq", [P, 2, 2, S], F32, 89)
    keys = sb("keys", [P, 2, P], F32, 204)
    topv = sb("topv", [P, 2, TT, PK], F32, 98)
    topi = sb("topi", [P, 2, TT, PK], U32, 98.5)
    topf = sb("topf", [P, 2, TT, PK], F32, 99)
    swork = sb("swork", [P, 2, TT, P], F32, 100)
    cand = sb("cand", [P, TT, PK * PK], F32, 104)
    best = sb("best", [P, TT, PK], F32, 108)
    besti = sb("besti", [P, TT, PK], U32, 108.25)
    bestij = sb("bestij", [P, 2, TT, PK], U32, 108.5)
    bestf = sb("bestf", [P, 2, TT, PK], F32, 109)
    bexp = sb("bexp", [P, TT, PK], F32, 109.5)
    bsum = sb("bsum", [P, TT], F32, 109.75)
    binv = sb("binv", [P, TT], F32, 109.875)
    onehot = sb("onehot", [P, TT * PK, PK], F32, 110)
    slots = sb("slots", [P, 3, TT, PH * PK], F32, 114)
    slotT = sb("slotT", [P, 2, S], F32, 202)
    gp16 = sb("gp16", [P, 3, S], BF16, 124)
    gpart = sb("gpart", [P, 3, S], F32, 127)
    hot = sb("hot", [P, 2, 4, 8, P], BF16, 133)
    hotb = sb("hotb", [P, 8, P], BF16, 149)
    stage = sb("stage", [P, 2, NK, TG], F32, 151)
    act_out = sb("act_out", [P, 4, S], F32, 183)
    act_in = sb("act_in", [P, 2, ET, S], F32, 89)
    act_m = sb("act_m", [P, 2, S], F32, 121)
    eh = sb("eh", [P, 4, S], F32R, 125)
    el = sb("el", [P, 4, S], F32R, 133)
    gt = sb("gt", [P, 2, S // TG, ET * TG], F32, 141)
    ch = sb("ch", [P, KT, S], F32R, 89)
    cl = sb("cl", [P, KT, S], F32R, 105)
    dh = sb("dh", [P, KT, S], F32R, 121)
    dl = sb("dl", [P, KT, S], F32R, 137)
    zs = sb("zs", [P, KT, S], F32, 153)
    ub = sb("ub", [P, 2, 16 + S], F32, 169)
    us = sb("us", [P, 2, 16 + S], F32, 174)
    um = sb("um", [P, 2, S], F32, 179)
    sqk = sb("sqk", [P, KT, S], F32, 121)
    sv = sb("sv", [P, TT, D], F32, 137)
    SW = 1280
    st = sb("st", [P, SW], F32, 169)
    slb0 = sb("slb0", [P, SW], F32, 174)
    slo = sb("slo", [P, SW], F32, 179)
    slh = sb("slh", [P, SW], F32R, 184)
    sll = sb("sll", [P, SW], F32R, 189)
    sy = sb("sy", [P, S], F32, 194)
    sa = sb("sa", [P, SW], F32, 196)
    slb1 = sb("slb1", [P, SW], F32, 201)
    slb = [slb0, slb1]
    outT = sb("outT", [P, KT, S], F32, 121)

    psum = nc.alloc_psum_tensor("psum", [P, 8, S], F32)
    acc = [psum[:, i, :] for i in range(4)]
    aux = [psum[:, 4 + i, :] for i in range(4)]
    aux3 = psum[:, 4:7, :].rearrange("p a n -> p (a n)")[:, 0:SW]
    acc3 = psum[:, 1:4, :].rearrange("p a n -> p (a n)")[:, 0:SW]

    gate_table = nc.dram_tensor("gate_table", (S // TG, P, NK * TG), F32, kind="Internal").ap()
    act_table = nc.dram_tensor("act_table", (NK, P, S), F32, kind="Internal").ap()

    sem = nc.alloc_semaphore
    raw_here = [sem(f"raw_here{i}") for i in range(RAW)]
    c_here = sem("c_here")
    ada_first_here = [sem(f"ada_first_here{i}") for i in range(8)]
    ada_rest_here = [sem(f"ada_rest_here{i}") for i in range(3)]
    ada_used = sem("ada_used")
    weights_split = sem("weights_split")
    split_step = sem("split_step")
    tile_done = sem("tile_done")
    evacuated = sem("evacuated")
    small_here = sem("small_here")
    xin_here = sem("xin_here")
    const_pool = sem("const_pool")
    const_vec = sem("const_vec")
    const_dve = sem("const_dve")
    csil_done = sem("csil_done")
    ada_done = sem("ada_done")
    nsq_done, nmm_done, nln_done, ninv_done = sem("nsq_done"), sem("nmm_done"), sem("nln_done"), sem("ninv_done")
    nxn_done, nhi_done, nlo_done, nout_done = sem("nxn_done"), sem("nhi_done"), sem("nlo_done"), sem("nout_done")
    out_stored = sem("out_stored")

    GLA_PE = Steps(sem("gla_pe"), "gate", "attn", "ket", "kv0", "kv1", "kv2", "kv3", "o", "ms")
    GLA_ACT = Steps(sem("gla_act"), "abs", "exp", "ln", "eb", "enb", "ekd", "ket", "sq0", "sq1", "lnms", "rstd")
    GLA_DVE = Steps(sem("gla_dve"), "min", "logalpha", "cumsum", "dif", "qd", "ki", "ke", "attn",
               *[f"s{c}" for c in range(1, 8)], "og0", "og1", "y0", "y1")
    CKV_PE = Steps(sem("ckv_pe"), "ms", "iw", "ckvn")
    CKV_ACT = Steps(sem("ckv_act"), "sq0", "sq1", "ln", "rstd", "n0", "n1")
    CKV_DVE = Steps(sem("ckv_dve"), "c0", "c1", "iw")
    idx_mm, idx_relu, idx_acc = sem("idx_mm"), sem("idx_relu"), sem("idx_acc")
    top_step = sem("top_step")
    ga_hi, ga_lo = sem("ga_hi"), sem("ga_lo")
    uk_here = [sem("uk_here0"), sem("uk_here1")]
    qlat_mm, logit_mm, probT_mm, olat_mm, oval_mm = sem("qlat_mm"), sem("logit_mm"), sem("probT_mm"), sem("olat_mm"), sem("oval_mm")
    qlat_out, prob_exp, prob_norm, olat_out, oval_out = sem("qlat_out"), sem("prob_exp"), sem("prob_norm"), sem("olat_out"), sem("oval_out")
    DSA_DVE = Steps(sem("dsa_dve"), "bias", "logit", "max", "inv")
    pT_out = sem("probT_out")
    y_step, y_hi, y_lo = sem("y_step"), sem("y_hi"), sem("y_lo")
    db_hi, db_lo = sem("dsaout_hi"), sem("dsaout_lo")
    ps_mm = sem("ps_mm")
    sel = sem("sel_step")
    sel_exp = sem("sel_exp")
    sT_mm, sT_step = sem("slotT_mm"), sem("slotT_step")
    HOT = Steps(sem("hot_step"), "key1", "key2", "gates")
    table_mm, table_out = sem("table_mm"), sem("table_out")
    table_stored = [sem("table_stored0"), sem("table_stored1")]
    act_stored = [sem(f"act_stored{j}") for j in range(4)]
    chunk_here = [sem("chunk_here0"), sem("chunk_here1")]
    e_mul, e_hi, e_lo = sem("e_mul"), sem("e_hi"), sem("e_lo")
    pl_step, pl_hi, pl_lo = sem("pool_step"), sem("pool_hi"), sem("pool_lo")
    pw_hi, pw_lo = sem("pooly_hi"), sem("pooly_lo")
    SB = {name: sem("sb_" + name) for name in ("qk", "cum", "o",
                                               "abs", "exp", "ln", "hi", "a", "yhi", "zabs", "zexp", "zln", "zsig",
                                               "lb", "lo", "mask", "losplit", "sum", "amask", "zlog", "silu", "y", "ylo")}

    def groups(eng, count, body):
        if count == 1:
            body(0)
        else:
            with eng.Fori(0, count) as g:
                body(g)

    def item_of(table, index):
        return table[bass.ds(index, 1), :, :].rearrange("a p n -> p (a n)")


    PL_END, n = [], 0
    for half in range(2):
        for t in range(8):
            n += 2 * half + t // 4 + 1 + 3
            PL_END.append(n)
    SEQ_G, SEQ_D = schedule_gla(), schedule_dsa()
    block_cm = nc.Block()
    block = block_cm.__enter__()
    lin_segments = [("w_in", 0, W_L1, W_A), ("w_branch_a", 0, W_A, W_ZB), ("w_in", W_A, W_ZB, W_B),
                    ("w_branch_b", 0, W_B, W_O), ("w_out", 0, W_O, W_Q)]

    @block.sync
    def _(sp):
        def load(table, first, count, w, width=D):
            def four(g):
                for j in range(RAW):
                    sp.wait_ge(weights_split, w + 4 * g + j - RAW + 1)
                    sp.dma_start(raw[j][:, 0:width], item_of(table, first + 4 * g + j)).then_inc(raw_here[j], 16)
            groups(sp, count // RAW, four)

        sp.dma_start(cb[:, :], io["c"].broadcast_to([P, D])).then_inc(c_here, 16)
        for i in range(8):
            sp.dma_start(ada_first[:, i, :, :], io["w_ada"][2 * i:2 * i + 2].rearrange("t p n -> p t n"))\
                .then_inc(ada_first_here[i], 16)
        for j in range(RAW):
            sp.dma_start(raw[j][:, :], item_of(io["w_in"], j)).then_inc(raw_here[j], 16)
        load(io["w_in"], RAW, W_A - RAW, RAW)
        for name, first, w, end in lin_segments[1:]:
            load(io[name], first, end - w, w)

        with sp.Fori(0, PH) as h:
            for t in range(2 + UH):
                table, at = (io["peer_w_q"], 2 * h + t) if t < 2 else (io["peer_u"], UH * h + t - 2)
                sp.wait_ge(weights_split, W_Q + (2 + UH) * h + t - RAW + 1)
                sp.dma_start(raw[t % RAW][:, :], item_of(table, at)).then_inc(raw_here[t % RAW], 16)
        load(io["peer_u"], PH * UH, NK - PH * UH, W_U)
        load(io["peer_v"], 0, NK, W_V)

        for half in range(2):
            w = W_POOL + 32 * half
            load(io["pool_w_in"], 16 * half, 16, w)
            load(io["pool_w"], 8 * half, 8, w + 16, width=D // 2)
            load(io["pool_w_out"], 8 * half, 8, w + 24)
        for half in range(2):
            w = W_SB + 32 * half
            load(io["sb_w_in"], 24 * half, 24, w)
            load(io["sb_w_out"], 8 * half, 8, w + 24)

    @block.gpsimd
    def _(pool):
        steps = [
            pool.memset(ident[:, :], 0.0), pool.memset(ones[:, :], 1.0), pool.memset(strict[:, :], 1.0),
            pool.memset(block_causal[:, :], 1.0), pool.memset(neg[:, :], NEG),
            pool.memset(chunk_start[:, :], 1.0), pool.memset(zero[:, :], 0.0), pool.memset(eps[:, :], EPS),
            pool.memset(one[:, :], 1.0),
            pool.iota(iota_row[:, :], pattern=[[1, P]], base=0, channel_multiplier=0,
                      allow_small_or_imprecise_dtypes=True),
            pool.iota(iota16[:, :], pattern=[[1, PK]], base=0, channel_multiplier=0,
                      allow_small_or_imprecise_dtypes=True),
            pool.iota(relpos[:, :], pattern=[[1, 896]], base=-384, channel_multiplier=-1,
                      allow_small_or_imprecise_dtypes=True),
        ]
        for ins in steps:
            ins.then_inc(const_pool, 1)
        n = len(steps)
        pool.wait_ge(const_pool, n)
        for ins in (
            pool.affine_select(out=ident[:, :], in_=ident[:, :], compare_op=ALU.not_equal, fill=1.0, base=0,
                               pattern=[[-1, P]], channel_multiplier=1),
            pool.affine_select(out=strict[:, :], in_=strict[:, :], compare_op=ALU.is_gt, fill=0.0, base=0,
                               pattern=[[1, P]], channel_multiplier=-1),
            pool.affine_select(out=block_causal[:, :], in_=block_causal[:, :], compare_op=ALU.is_ge, fill=0.0,
                               base=0, pattern=[[1, P]], channel_multiplier=-1),
            pool.memset(chunk_start[:, :].rearrange("p (c t) -> p c t", t=CH)[:, :, 0:1], 0.0),
        ):
            ins.then_inc(const_pool, 1)
        pool.wait_ge(const_pool, n + 4)
        pool.memset(block_causal[0:CH, CH:P], 0.0).then_inc(const_pool, 1)
        pool.tensor_tensor(trilr[:, :], ones[:, :], strict[:, :], ALU.subtract).then_inc(const_pool, 1)
        pool.wait_ge(const_pool, n + 6)
        pool.tensor_tensor(trilr[:, :], trilr[:, :].bitcast(F32), ident[:, :], ALU.subtract).then_inc(const_pool, 1)
        pool.tensor_tensor(onesr[:, :], ones[:, :], zero[:, 0:1].broadcast_to([P, P]), ALU.add)\
            .then_inc(const_pool, 1)
        assert n + 8 == NCONST

        def split(w, j, g, width, first=False):
            s = j % SPLIT
            pool.wait_ge(raw_here[j], 16 * (g + 1))
            if not first:
                pool.wait_ge(tile_done, w - SPLIT + 1)
            pool.tensor_tensor(wh[s][:, 0:width], raw[j][:, 0:width], zero[:, 0:1].broadcast_to([P, width]),
                               ALU.add).then_inc(split_step, 1)
            pool.wait_ge(split_step, w + 1)
            pool.tensor_tensor(wl[s][:, 0:width], raw[j][:, 0:width], wh[s][:, 0:width].bitcast(F32),
                               ALU.subtract).then_inc(weights_split, 1)

        for j in range(RAW):
            split(j, j, 0, D, first=j < SPLIT)
        for w, count, width in [(RAW, W_POOL + 16 - RAW, D), (W_POOL + 16, 8, D // 2), (W_POOL + 24, 24, D),
                                (W_POOL + 48, 8, D // 2), (W_POOL + 56, W_END - W_POOL - 56, D)]:
            with pool.Fori(0, count // RAW) as g:
                for j in range(RAW):
                    split(w + 4 * g + j, j, w // 4 + g, width)

    @block.tensor
    def _(pe):
        def products(out, whi, wlo, ahi, alo, start, stop):
            pe.matmul(out, whi, ahi, start=start, stop=False, skip_group_check=True)
            pe.matmul(out, whi, alo, start=False, stop=False, skip_group_check=True)
            return pe.matmul(out, wlo, ahi, start=False, stop=stop, skip_group_check=True)

        def lin(w, j, hi, lo, k0=0, kt=KT, free=True, part=None, ready=None):
            if not part:
                pe.wait_ge(weights_split, w + 1)
                if free:
                    pe.wait_ge(evacuated, w - 3)
            s = j % SPLIT
            ks = range(kt) if part is None else range(kt // PARTS * part, kt // PARTS * (part + 1))
            for k in ks:
                if ready is not None:
                    pe.wait_ge(ready[0], ready[1] + k + 1)
                cols = slice(P * k, P * k + P)
                mm = products(acc[j], wh[s][:, cols], wl[s][:, cols], hi[:, k0 + k, :], lo[:, k0 + k, :],
                              k == 0, k == kt - 1)
            if part in (None, PARTS - 1):
                mm.then_inc(tile_done, 1)

        def lin_start(w, hi, lo, sem, base, free=True):
            for j in range(4):
                lin(w + j, j, hi, lo, free=free, ready=(sem, base) if j == 0 else None)

        def lin_loop(w, count, hi, lo):
            def four(g):
                for j in range(4):
                    lin(w + 4 * g + j, j, hi, lo)
            groups(pe, count // 4, four)

        def lin_tokens(w, turns, hi, lo):
            def turn(g):
                for j in range(4):
                    pe.wait_ge(weights_split, w + 4 * g + j + 1)
                    s = j % SPLIT
                    for kk in range(2):
                        k = 2 * j + kk
                        cols = slice(S * kk, S * kk + S)
                        for t in range(TT):
                            tok = slice(P * t, P * t + P)
                            first, last = k == 0, k == KT - 1
                            if first:
                                pe.wait_ge(evacuated, w + 4 * g - 3 + t)
                            pe.matmul(acc[t], hi[:, k, tok], wh[s][:, cols], start=first, stop=False,
                                      skip_group_check=True)
                            pe.matmul(acc[t], lo[:, k, tok], wh[s][:, cols], start=False, stop=False,
                                      skip_group_check=True)
                            mm = pe.matmul(acc[t], hi[:, k, tok], wl[s][:, cols], start=False, stop=last,
                                           skip_group_check=True)
                    mm.then_inc(tile_done, 1)
            groups(pe, turns, turn)

        def norm(o):
            for k in range(KT):
                pe.wait_ge(nsq_done, KT * o + k + 1)
                pe.matmul(aux[0], ones[:, :], nsq[:, k % 2, :], start=k == 0, stop=k == KT - 1)\
                    .then_inc(nmm_done, 1)

        pe.wait_ge(const_pool, NCONST)
        norm(0)
        lin_start(0, ah, al, nlo_done, 0, free=False)
        lin_loop(4, 8, ah, al)
        lin_tokens(12, 2, ah, al)
        lin_loop(20, 4, ah, al)

        pe.wait_ge(small_here, NSMALL)
        for item in SEQ_G:
            kind = item[0]
            if kind == "ckv":
                for k in range(2):
                    pe.wait_ge(CKV_ACT.sem, CKV_ACT.at(0, f"sq{k}"))
                    mm = pe.matmul(aux[0], ones[:, :], gt1[:, k, :], start=k == 0, stop=k == 1)
                mm.then_inc(CKV_PE.sem, 1)
                for t in range(TT):
                    mm = pe.transpose(aux[3][:, P * t:P * t + P], misc[:, P * t:P * t + P], ident[:, :])
                mm.then_inc(CKV_PE.sem, 1)
                pe.wait_ge(CKV_DVE.sem, CKV_DVE.at(0, "c1"))
                for t in range(TT):
                    for c in range(2):
                        mm = pe.transpose(psum[:, 5 + t // 2, LAT * (t % 2) + P * c:LAT * (t % 2) + P * c + P],
                                          ckv[:, c, P * t:P * t + P], ident[:, :])
                mm.then_inc(CKV_PE.sem, 1)
            elif kind == "lin":
                w, part = item[1:]
                lin(w, w % 4, ah, al, part=part)
            elif kind == "prep":
                h = item[1]
                if h:
                    pe.wait_ge(GLA_DVE.sem, GLA_DVE.at(h - 1, "og1"))
                else:
                    pe.wait_ge(CKV_ACT.sem, CKV_ACT.at(0, "rstd"))
                pe.matmul(aux[0], gwu[:, GDK * h:GDK * h + GDK], misc[0:16, :], start=True, stop=True)\
                    .then_inc(GLA_PE.sem, 1)
            elif kind == "attn":
                h = item[1]
                if h == 0:
                    pe.wait_ge(CKV_ACT.sem, CKV_ACT.at(0, "n1"))
                pe.wait_ge(GLA_DVE.sem, GLA_DVE.at(h, "ki"))
                for t in range(TT):
                    tok = slice(P * t, P * t + P)
                    mm = pe.matmul(aux[1][:, tok], gki[:, tok], gqd[:, tok], start=True, stop=True)
                mm.then_inc(GLA_PE.sem, 1)
                pe.wait_ge(GLA_DVE.sem, GLA_DVE.at(h, "ke"))
                for t in range(TT):
                    tok = slice(P * t, P * t + P)
                    mm = pe.transpose(aux[0][:, tok], gke[:, tok], ident[:, :])
                mm.then_inc(GLA_PE.sem, 1)
            elif kind == "kv":
                h, t = item[1:]
                if t == 0:
                    pe.wait_ge(GLA_ACT.sem, GLA_ACT.at(h, "ket"))
                    pe.wait_ge(GLA_DVE.sem, GLA_DVE.at(h, "attn"))
                    if h:
                        pe.wait_ge(GLA_ACT.sem, GLA_ACT.at(h - 1, "rstd"))
                else:
                    pe.wait_ge(GLA_DVE.sem, GLA_DVE.at(h, f"s{2 * t}"))
                for c in range(2 if t < 3 else 1):
                    rows = slice(CH * c, CH * c + CH)
                    mm = pe.matmul(aux[2 - c][:, 0:GDV], gket[rows, t, :],
                                   gv[rows, t, GDV * h:GDV * h + GDV], start=True, stop=True)
                mm.then_inc(GLA_PE.sem, 1)
            elif kind == "o":
                h = item[1]
                pe.wait_ge(GLA_DVE.sem, GLA_DVE.at(h, "s7"))
                for v in range(2):
                    out = aux[1 - v]
                    val = slice(GDV * h + P * v, GDV * h + P * v + P)
                    for t in range(TT):
                        tok = slice(P * t, P * t + P)
                        mm = pe.matmul(out[:, tok], gv[:, t, val], gat[:, t, :], start=t == 0, stop=False,
                                       skip_group_check=True)
                    for c in range(1, 8):
                        tok = slice(CH * c, CH * c + CH)
                        mm = pe.matmul(out[:, tok], gst[:, c - 1, P * v:P * v + P], gqd[:, tok], start=False,
                                       stop=c == 7, skip_group_check=True)
                mm.then_inc(GLA_PE.sem, 1)
            elif kind == "ms":
                h = item[1]
                for v in range(2):
                    pe.wait_ge(GLA_ACT.sem, GLA_ACT.at(h, f"sq{v}"))
                    mm = pe.matmul(aux[2], ones[:, :], gt1[:, v, :], start=v == 0, stop=v == 1)
                mm.then_inc(GLA_PE.sem, 1)
            elif kind == "idx":
                tt, h = item[1:]
                i = (tt - 1) * IH + h
                if i:
                    pe.wait_ge(idx_relu, i)
                else:
                    pe.wait_ge(evacuated, W_G)
                    pe.wait_ge(CKV_DVE.sem, CKV_DVE.at(0, "iw"))
                rows = slice(IDD * (h % 2), IDD * (h % 2) + IDD)
                pe.matmul(aux[3][:, 0:P * (tt + 1)], iq[rows, h // 2, P * tt:P * tt + P],
                          ik[rows, 0:P * (tt + 1)], start=True, stop=True).then_inc(idx_mm, 1)

        for item in SEQ_D:
            kind = item[0]
            if kind == "lin":
                w, part = item[1:]
                if w == W_A:
                    pe.wait_ge(ga_lo, KT)
                if w < W_A:
                    lin(w, w % 4, ah, al, part=part)
                else:
                    lin(w, w % 4, bh, bl, part=part)
            elif kind == "qlat":
                h = item[1]
                pe.wait_ge(uk_here[h % 2], 32 * (h // 2 + 1))
                if h >= 2:
                    pe.wait_ge(oval_out, h - 1)
                elif h == 0:
                    pe.wait_ge(GLA_ACT.sem, GLA_ACT.at(GH - 1, "rstd"))
                    pe.wait_ge(idx_relu, 3 * IH)
                    pe.wait_ge(evacuated, W_ZA)
                for c in range(2):
                    mm = pe.matmul(aux[2 + c], uk[:, h % 2, P * c:P * c + P], qk[:, h, :], start=True, stop=True)
                mm.then_inc(qlat_mm, 1)
            elif kind == "score":
                h, t = divmod(item[1], TT)
                i = item[1]
                n = P * (t + 1)
                pe.wait_ge(qlat_out, h + 1)
                if i:
                    pe.wait_ge(DSA_DVE.sem, DSA_DVE.at(i - 1, "logit"))
                else:
                    pe.wait_ge(GLA_DVE.sem, GLA_DVE.at(GH - 1, "og1"))
                for c in range(2):
                    mm = pe.matmul(aux[0][:, 0:n], qlat[:, c, P * t:P * t + P], ckv[:, c, 0:n],
                                   start=c == 0, stop=c == 1)
                mm.then_inc(logit_mm, 1)
            elif kind == "pt":
                i = item[1]
                t = i % TT
                pe.wait_ge(prob_norm, i + 1)
                if i:
                    pe.wait_ge(pT_out, i)
                for b in range(t + 1):
                    mm = pe.transpose(aux[1][:, P * b:P * b + P], prob[:, i % 2, P * b:P * b + P], ident[:, :])
                mm.then_inc(probT_mm, 1)
            elif kind == "out":
                h = item[1]
                pe.wait_ge(pT_out, TT * (h + 1))
                if h + 1 < DH:
                    pe.wait_ge(qlat_out, h + 2)
                for c in range(2):
                    for b in range(TT):
                        mm = pe.matmul(aux[2 + c][:, P * b:S], ckvn[:, b, P * c:P * c + P], pT[:, b, P * b:S],
                                       start=b == 0, stop=b == TT - 1, skip_group_check=True)
                mm.then_inc(olat_mm, 1)
            elif kind == "oval":
                h = item[1]
                pe.wait_ge(olat_out, h + 1)
                for c in range(2):
                    mm = pe.matmul(aux[2], uv[:, h % 2, c, :], olat[:, c, :], start=c == 0, stop=c == 1)
                mm.then_inc(oval_mm, 1)

        lin_loop(W_ZB, 8, ah, al)
        lin_start(W_B, bh, bl, db_lo, 0)
        lin_loop(W_B + 4, 4, bh, bl)
        lin_start(W_O, ah, al, y_lo, 0)
        lin_loop(W_O + 4, 4, ah, al)
        norm(1)

        for h in range(PH):
            w = W_Q + (2 + UH) * h
            for t in range(3):
                lin(w + t, t, ah, al, ready=(nlo_done, KT) if h == t == 0 else None)
            for side in range(2):
                pe.wait_ge(evacuated, w + side + 1)
                if h >= 2:
                    pe.wait_ge(sel, NSEL * (h - 2) + 24)
                for t in range(TT):
                    mm = pe.matmul(aux[2 * (h % 2) + side][:, P * t:P * t + P], pq[:, h % 2, side, P * t:P * t + P],
                                   keys[:, side, :], start=True, stop=True)
                mm.then_inc(ps_mm, 1)
            for t in range(3, 2 + UH):
                lin(w + t, t % 4, ah, al)
        lin_loop(W_U, 4, ah, al)
        pe.wait_ge(sel, NSEL * PH)
        for part in range(3):
            for t in range(TT):
                mm = pe.transpose(aux[part][:, P * t:P * t + P], slots[:, part, t, :], ident[:, :])
            mm.then_inc(sT_mm, 1)
        lin_loop(W_U + 4, 4, ah, al)
        pe.wait_ge(sT_step, 8)
        def table(g, first):
            for b in range(8):
                lin(W_TAB + 8 * g + b, b % 4, ah, al)
                pe.wait_ge(HOT.sem, HOT.at(8 * g + b, "gates"))
                for q in (2 * b, 2 * b + 1):
                    if not (first and q < 4):
                        pe.wait_ge(table_out, 16 * g + q - 3)
                    for t in range(4):
                        u = 4 * (q % 2) + t
                        for part in range(3):
                            mm = pe.matmul(aux[q % 4][:, P * t:P * t + P], hot[:, b % 2, 0, u, :],
                                           hot[:, b % 2, 1 + part, u, :], start=part == 0, stop=part == 2)
                    mm.then_inc(table_mm, 1)
        table(0, True)
        with pe.Fori(1, 8) as g:
            table(g, False)
        lin_loop(W_V - 8, 8, ah, al)

        def experts(g, first=False, last=False):
            for e in range(2 * ET):
                v = W_V + 2 * ET * g + e
                pe.wait_ge(weights_split, v + 1)
                if first and e == 0:
                    pe.wait_ge(evacuated, W_V)
                    pe.wait_ge(table_out, S // 4)
                pe.wait_ge(e_lo, 2 * ET * g + e + 1)
                for d in range(KT):
                    cols = slice(P * d, P * d + P)
                    mm = products(psum[:, (d + 4) % 8, :], wh[e % 2][:, cols], wl[e % 2][:, cols], eh[:, e % 4, :],
                                  el[:, e % 4, :], first and e == 0, last and e == 2 * ET - 1)
                mm.then_inc(tile_done, 1)
        experts(0, first=True)
        with pe.Fori(1, NCHUNK // 2 - 1) as g:
            experts(g)
        experts(NCHUNK // 2 - 1, last=True)
        norm(2)
        norm(3)

        for half in range(2):
            w = W_POOL + 32 * half
            lin_start(w, ah, al, nlo_done, 2 * KT)
            lin_loop(w + 4, 12, ah, al)
            for n in range(8):
                if n % 4 == 0:
                    pe.wait_ge(pl_lo, 8 * half + n + 4)
                lin(w + 16 + n, n % 4, ch, cl, k0=n // 4 * 4, kt=4)
            lin_start(w + 24, dh, dl, pw_lo, 8 * half)
            lin_loop(w + 28, 4, dh, dl)
        norm(4)

        def scores(i):
            hd = i % 8
            rows = slice(64 * (hd % 2), 64 * (hd % 2) + 64)
            q, k = sqk[rows, hd // 2, :], sqk[rows, 4 + hd // 2, :]
            if i:
                pe.wait_ge(SB["lo"], i)
            for b in range(TT):
                for at, c0, n in SB_REGIONS[b]:
                    mm = pe.matmul(aux3[:, at:at + n], k[:, P * b:P * b + P], q[:, c0:c0 + n],
                                   start=True, stop=True, skip_group_check=True)
            mm.then_inc(SB["qk"], 1)

        for half in range(2):
            w = W_SB + 32 * half
            lin_start(w, ah, al, nlo_done, 3 * KT)
            lin_loop(w + 4, 4, ah, al)
            pe.wait_ge(evacuated, w + 8)
            scores(8 * half)
            lin_tokens(w + 8, 2, ah, al)
            pe.wait_ge(evacuated, w + 16)
            for hd in range(8):
                i = 8 * half + hd
                if hd < 7:
                    scores(i + 1)
                pe.wait_ge(SB["losplit"], i + 1)
                if i:
                    pe.wait_ge(SB["sum"], i)
                plan = [(trilr, b, b) for b in range(TT)] + [(onesr, b, c) for b in range(TT) for c in range(b + 1, TT)]
                sums = []
                for mat, b, c in plan:
                    for at, c0, n in SB_REGIONS[c]:
                        for to, d0, m in SB_REGIONS[b]:
                            a, z = max(c0, d0), min(c0 + n, d0 + m)
                            if a < z:
                                sums += [(mat, src[:, at + a - c0:at + z - c0], to + a - d0, z - a)
                                         for src in (slh, sll)]
                banks = [to // S for _, _, to, _ in sums]
                for n, (mat, src, to, m) in enumerate(sums):
                    mm = pe.matmul(acc3[:, to:to + m], mat[:, :], src, start=banks[n] not in banks[:n],
                                   stop=banks[n] not in banks[n + 1:], skip_group_check=True)
                mm.then_inc(SB["cum"], 1)
                pe.wait_ge(weights_split, w + 16 + hd + 1)
                pe.wait_ge(evacuated, w + 16 + hd)
                s = hd % SPLIT
                for kk in range(KT):
                    cols = slice(P * kk, P * kk + P)
                    mm = products(acc[0], wh[s][:, cols], wl[s][:, cols], ah[:, kk, :], al[:, kk, :],
                                  kk == 0, kk == KT - 1)
                mm.then_inc(tile_done, 1)
                pe.wait_ge(SB["amask"], i + 1)
                if i:
                    pe.wait_ge(SB["y"], i)
                for b in range(TT):
                    for at, c0, n in SB_REGIONS[b]:
                        mm = pe.matmul(aux[3][:, c0:c0 + n], sv[:, b, P * hd:P * hd + P], sa[:, at:at + n],
                                       start=at == 0, stop=b == TT - 1, skip_group_check=True)
                mm.then_inc(SB["o"], 1)
            pe.wait_ge(evacuated, w + 24)
            pe.wait_ge(SB["sum"], 8 * half + 8)
            lin_start(w + 24, ch, cl, SB["ylo"], 8 * half)
            lin_loop(w + 28, 4, ch, cl)
        norm(5)

    @block.scalar
    def _(act):
        def evac(w, j, dst, func=ACT.Copy, done=None, scale=1.0):
            act.wait_ge(tile_done, w + 1 if done is None else done)
            act.activation(dst, acc[j], func, scale=scale).then_inc(evacuated, 1)

        def evac_loop(w, count, dst, func=ACT.Copy, scale=1.0):
            def four(g):
                for j in range(4):
                    evac(w + 4 * g + j, j, dst[:, bass.ds(4 * g + j, 1), :].rearrange("p a n -> p (a n)"), func,
                         scale=scale)
            if count == 4:
                for j in range(4):
                    evac(w + j, j, dst[:, j, :], func, scale=scale)
            else:
                groups(act, count // 4, four)

        def evac_tokens(w, turns, dst):
            for g in range(turns):
                for j in range(4):
                    evac(w, j, dst[:, j, S * g:S * g + S], done=w + 4 * g + 4)

        def log_exp():
            act.preload_act_table_set("natural_log_exp_and_others")

        def inverse_root(log, out, total, count, log_done, turn, done):
            act.activation(log, total, ACT.Ln, scale=1.0 / count, bias=eps[:, :]).then_inc(log_done, 1)
            act.wait_ge(log_done, turn)
            act.activation(out, log, ACT.Exp, scale=-0.5).then_inc(done, 1)

        def norm(o, ready, base, split=None, shift=None, per=1):
            for k in range(KT):
                act.wait_ge(ready, base if ready is xin_here else base + per * (k + 1))
                if k >= 2 or o:
                    act.wait_ge(nmm_done, KT * o + k - 1)
                act.activation(nsq[:, k % 2, :], xT[:, k, :], ACT.Square).then_inc(nsq_done, 1)
            act.wait_ge(nmm_done, KT * o + KT)
            inverse_root(nlog[:, :], nrs[:, :], aux[0], D, nln_done, o + 1, ninv_done)
            if shift is not None:
                act.wait_ge(ada_done, split + 1)
            if split is not None:
                for k in range(KT):
                    act.wait_ge(nxn_done, KT * split + k + 1)
                    act.activation(ah[:, k, :], nxn[:, k % 2, :], ACT.Identity,
                                   bias=zero[:, 0:1] if shift is None else shift[:, k:k + 1]).then_inc(nhi_done, 1)

        act.dma_start(xT[:, :, :], io["x"]).then_inc(xin_here, 16)
        for dst, name in ((vec, "vec"), (gwu, "gla_w_gate_up"), (keys, "peer_sub_keys")):
            src = io[name].rearrange("p a n -> p (a n)") if name == "peer_sub_keys" else io[name]
            d = dst[:, :, :].rearrange("p a n -> p (a n)") if name == "peer_sub_keys" else dst[:, :]
            act.dma_start(d, src).then_inc(small_here, 16)
        act.wait_ge(c_here, 16)
        act.activation(cb[:, :], cb[:, :], ACT.Silu).then_inc(csil_done, 1)
        act.wait_ge(const_pool, NCONST)
        log_exp()
        norm(0, xin_here, 16, split=0, shift=shift1)

        outs = [misc[:, :], ik[:, :], ckv[:, 0, :], ckv[:, 1, :]] + [qk[:, n, :] for n in range(8)]
        outs += [gv[:, j, S * n:S * n + S] for n in range(2) for j in range(4)] + [iq[:, n, :] for n in range(4)]
        for w, dst in enumerate(outs):
            evac(w, w % 4, dst, done=w // 4 * 4 + 4 if 12 <= w < 20 else None)
            if w < 16:
                act.wait_ge(ada_used, 16 + 2 * max(w - 2, 0))
                act.dma_start(ada_rest[:, w % 3, :, :], io["w_ada"][16 + 2 * w:18 + 2 * w].rearrange("t p n -> p t n"))\
                    .then_inc(ada_rest_here[w % 3], 16)
        act.wait_ge(ada_used, NADA)

        for item in SEQ_G:
            kind = item[0]
            if kind == "ckv":
                act.wait_ge(evacuated, 4)
                for k in range(2):
                    act.activation(gt1[:, k, :], ckv[:, k, :], ACT.Square).then_inc(CKV_ACT.sem, 1)
                act.wait_ge(CKV_PE.sem, CKV_PE.at(0, "ms"))
                inverse_root(nlog[:, :], nrs[:, :], aux[0], LAT, CKV_ACT.sem, CKV_ACT.at(0, "ln"), CKV_ACT.sem)
                act.wait_ge(CKV_PE.sem, CKV_PE.at(0, "ckvn"))
                for b in range(2):
                    act.activation(ckvn[:, 2 * b:2 * b + 2, :].rearrange("p a n -> p (a n)"), psum[:, 5 + b, :],
                                   ACT.Copy).then_inc(CKV_ACT.sem, 1)
            elif kind == "lin":
                w, part = item[1:]
                h, r = divmod(w - W_G, 4)
                if part < PARTS - 1:
                    continue
                if r == 1:
                    for n in range(2):
                        evac(w - 1 + n, (w - 1 + n) % 4, gr[:, 2 * h + n, :], ACT.Silu)
                    log_exp()
                elif r > 1:
                    act.wait_ge(GLA_DVE.sem, GLA_DVE.at(h, "ke"))
                    evac(w, w % 4, qk[:, 2 * h + r - 2, :])
            elif kind == "prep":
                h = item[1]
                act.wait_ge(GLA_PE.sem, GLA_PE.at(h, "gate"))
                if h:
                    act.wait_ge(GLA_DVE.sem, GLA_DVE.at(h - 1, "y1"))
                act.activation(gt1[:, 0, :], aux[0], ACT.Abs, bias=VEC["gla_b_gate"][:, h:h + 1])\
                    .then_inc(GLA_ACT.sem, 1)
                act.wait_ge(GLA_ACT.sem, GLA_ACT.at(h, "abs"))
                act.activation(gt1[:, 0, :], gt1[:, 0, :], ACT.Exp, scale=-1.0).then_inc(GLA_ACT.sem, 1)
                act.wait_ge(GLA_ACT.sem, GLA_ACT.at(h, "exp"))
                act.activation(gt1[:, 0, :], gt1[:, 0, :], ACT.Ln, bias=one[:, :]).then_inc(GLA_ACT.sem, 1)
                act.wait_ge(GLA_DVE.sem, GLA_DVE.at(h, "cumsum"))
                act.activation(geb[:, :], gb[:, :], ACT.Exp, scale=1.0 / TAU).then_inc(GLA_ACT.sem, 1)
                act.activation(gki[:, :], gb[:, :], ACT.Exp, scale=-1.0 / TAU).then_inc(GLA_ACT.sem, 1)
                act.wait_ge(GLA_DVE.sem, GLA_DVE.at(h, "dif"))
                act.activation(gke[:, :], gke[:, :], ACT.Exp, scale=1.0 / TAU).then_inc(GLA_ACT.sem, 1)
            elif kind == "attn":
                h = item[1]
                act.wait_ge(GLA_PE.sem, GLA_PE.at(h, "ket"))
                act.activation(gket[:, :, :].rearrange("p a n -> p (a n)"), aux[0], ACT.Copy).then_inc(GLA_ACT.sem, 1)
            elif kind == "o":
                h = item[1]
                act.wait_ge(GLA_PE.sem, GLA_PE.at(h, "o"))
                for v in range(2):
                    act.activation(gt1[:, v, :], aux[1 - v], ACT.Square).then_inc(GLA_ACT.sem, 1)
            elif kind == "ms":
                h = item[1]
                act.wait_ge(GLA_PE.sem, GLA_PE.at(h, "ms"))
                inverse_root(gki[:, :], gke[:, :], aux[2], GDV, GLA_ACT.sem, GLA_ACT.at(h, "lnms"), GLA_ACT.sem)
            elif kind == "idx":
                tt, h = item[1:]
                i = (tt - 1) * IH + h
                n = P * (tt + 1)
                act.wait_ge(idx_mm, i + 1)
                if i >= 2:
                    act.wait_ge(idx_acc, i - 1)
                act.activation(rel[:, i % 2, 0:n], aux[3][:, 0:n], ACT.Relu, scale=IDD ** -0.5).then_inc(idx_relu, 1)

        def load_head(h):
            act.dma_start(uk[:, h % 2, :], io["dsa_w_uk"][h]).then_inc(uk_here[h % 2], 16)
            act.dma_start(uv[:, h % 2, :, :], io["dsa_w_uv"][h]).then_inc(uk_here[h % 2], 16)

        act.wait_ge(GLA_DVE.sem, GLA_DVE.at(GH - 1, "y1"))
        load_head(0)
        load_head(1)
        for item in SEQ_D:
            kind = item[0]
            if kind == "ga":
                n = item[1]
                act.activation(bh[:, n, :], gr[:, n, :], ACT.Copy).then_inc(ga_hi, 1)
            elif kind == "lin":
                w, part = item[1:]
                if w < W_A and part == PARTS - 1 and w % 2:
                    act.wait_ge(ga_lo, w - W_ZA + 1)
                    for n in (w - 1, w):
                        evac(n, n % 4, gr[:, n - W_ZA, :], ACT.Sigmoid)
                    log_exp()
            elif kind == "qlat":
                h = item[1]
                act.wait_ge(qlat_mm, h + 1)
                for c in range(2):
                    ins = act.activation(qlat[:, c, :], aux[2 + c], ACT.Copy)
                ins.then_inc(qlat_out, 1)
            elif kind == "score":
                i = item[1]
                n = P * (i % TT + 1)
                act.wait_ge(DSA_DVE.sem, DSA_DVE.at(i, "max"))
                act.activation(prob[:, i % 2, 0:n], prob[:, i % 2, 0:n], ACT.Exp, bias=rowstat[:, 0, i:i + 1],
                               accum_out=rowstat[:, 1, i:i + 1]).then_inc(prob_exp, 1)
                act.wait_ge(DSA_DVE.sem, DSA_DVE.at(i, "inv"))
                act.activation(prob[:, i % 2, 0:n], prob[:, i % 2, 0:n], ACT.Copy, scale=rowstat[:, 2, i:i + 1])\
                    .then_inc(prob_norm, 1)
            elif kind == "out":
                h = item[1]
                act.wait_ge(olat_mm, h + 1)
                for c in range(2):
                    ins = act.activation(olat[:, c, :], aux[2 + c], ACT.Copy)
                ins.then_inc(olat_out, 1)
            elif kind == "oval":
                h = item[1]
                act.wait_ge(oval_mm, h + 1)
                act.activation(qk[:, h, :], aux[2], ACT.Copy).then_inc(oval_out, 1)
                if h + 2 < DH:
                    load_head(h + 2)

        act.wait_ge(evacuated, W_ZB)
        act.wait_ge(oval_out, DH)
        for n in range(KT):
            act.activation(bh[:, n, :], qk[:, n, :], ACT.Copy).then_inc(db_hi, 1)
        evac_loop(W_ZB, 8, zb, ACT.Sigmoid)
        for n in range(KT):
            act.wait_ge(y_step, n + 1)
            act.activation(ah[:, n, :], gr[:, n, :], ACT.Copy).then_inc(y_hi, 1)
        log_exp()
        norm(1, evacuated, W_O, split=1, shift=shift2)

        def gelu(w, bank, u, j, turn, first=False):
            if not first:
                act.wait_ge(act_stored[j], 16 * turn)
            evac(w, bank, act_out[:, j, :], ACT.Gelu)
            act.wait_ge(evacuated, w + 1)
            act.dma_start(item_of(act_table, u), act_out[:, j, :]).then_inc(act_stored[j], 16)

        for h in range(PH):
            for side in range(2):
                w = W_Q + (2 + UH) * h + side
                if h == 0 and side == 0:
                    act.wait_ge(evacuated, W_Q)
                if h >= 2:
                    act.wait_ge(ps_mm, 2 * (h - 2) + side + 1)
                evac(w, w % 4, pq[:, h % 2, side, :])
            for t in range(UH):
                u = UH * h + t
                gelu(W_Q + (2 + UH) * h + 2 + t, (2 + t) % 4, u, u % 4, u // 4, first=u < 4)
                if t == UH - 2:
                    act.wait_ge(sel, NSEL * h + SEL_SHIFTED)
                    act.activation(bexp[:, :, :], bexp[:, :, :], ACT.Exp).then_inc(sel_exp, 1)
        for u in range(PH * UH, PH * UH + 8):
            gelu(W_U + u - PH * UH, u % 4, u, u % 4, u // 4)

        U_TAB = PH * UH + 8

        def load_acts(half, c):
            act.dma_start(act_in[:, half, :, :], act_table[bass.ds(ET * c, ET)].rearrange("e p n -> p e n"))\
                .then_inc(chunk_here[half], 16)

        def load_gates(half, c):
            act.dma_start(gt[:, half, :, :],
                          gate_table.rearrange("g p (c n) -> c p g n", c=NCHUNK)[bass.ds(c, 1)]
                          .rearrange("a p g n -> p (a g) n")).then_inc(chunk_here[half], 16)

        act.wait_ge(sT_mm, 3)
        for j in range(4):
            act.wait_ge(act_stored[j], 16 * 4)
        load_acts(0, 0)
        load_acts(1, 1)

        def table(g, first):
            for b in range(8):
                gelu(W_TAB + 8 * g + b, b % 4, U_TAB + 8 * g + b, b % 4, U_TAB // 4 + 2 * g + b // 4)
                half = b // 4
                for q in (2 * b, 2 * b + 1):
                    act.wait_ge(table_mm, 16 * g + q + 1)
                    if q % 8 == 0 and not first:
                        act.wait_ge(table_stored[half], 16 * g)
                    act.activation(stage[:, half, :, 4 * (q % 8):4 * (q % 8) + 4].rearrange("p b t -> p t b"),
                                   aux[q % 4].rearrange("p (t b) -> p t b", t=4), ACT.Copy).then_inc(table_out, 1)
                if b % 4 == 3:
                    act.wait_ge(table_out, 16 * g + 2 * b + 2)
                    act.dma_start(item_of(gate_table, 2 * g + half),
                                  stage[:, half, :, :].rearrange("p b t -> p (b t)")).then_inc(table_stored[half], 16)
        table(0, True)
        with act.Fori(1, 8) as g:
            table(g, False)

        for u in range(NK - 8, NK):
            if u == NK - 4:
                for half in range(2):
                    act.wait_ge(table_stored[half], 16 * 8)
                load_gates(0, 0)
                load_gates(1, 1)
            gelu(W_V - NK + u, u % 4, u, u % 4, u // 4)

        def experts(g, first=False, last=False):
            for half in range(2):
                for e in range(ET * half, ET * half + ET):
                    i = 2 * ET * g + e
                    act.wait_ge(e_mul, i + 1)
                    act.wait_ge(tile_done, W_V + i - 3)
                    act.activation(eh[:, e % 4, :], act_m[:, e % 2, :], ACT.Copy).then_inc(e_hi, 1)
                if first and half == 0:
                    for j in range(4):
                        act.wait_ge(act_stored[j], 16 * NK // 4)
                if not last:
                    load_acts(half, 2 * g + 2 + half)
                    load_gates(half, 2 * g + 2 + half)
        experts(0, first=True)
        with act.Fori(1, NCHUNK // 2 - 1) as g:
            experts(g)
        experts(NCHUNK // 2 - 1, last=True)
        log_exp()
        norm(2, evacuated, W_V, per=NK // KT)
        norm(3, nout_done, 0, split=2)

        for half in range(2):
            w = W_POOL + 32 * half
            act.wait_ge(evacuated, w)
            for n in range(8):
                i = 8 * half + n
                act.wait_ge(const_dve, 3)
                if i >= 2:
                    act.wait_ge(pl_step, PL_END[i - 2])
                evac(w + n, n % 4, ub[:, n % 2, 16:16 + S])
                act.wait_ge(pl_step, PL_END[i])
                act.activation(ch[:, n, :], um[:, n % 2, :], ACT.Copy).then_inc(pl_hi, 1)
            evac_loop(w + 8, 8, zs, ACT.Silu)
            for n in range(8):
                act.wait_ge(evacuated, w + 17 + n)
                act.activation(dh[:, n, :], um[:, n % 2, :], ACT.Copy).then_inc(pw_hi, 1)
        log_exp()
        norm(4, evacuated, W_SB - 8, split=3)

        def y_high(i):
            act.wait_ge(SB["y"], i + 1)
            act.activation(ch[:, i % 8, :], sy[:, :], ACT.Copy).then_inc(SB["yhi"], 1)

        for half in range(2):
            w = W_SB + 32 * half
            act.wait_ge(evacuated, w)
            evac_loop(w, 4, sqk, scale=0.125)
            evac_loop(w + 4, 4, sqk[:, 4:8, :])
            for hd in range(-1, 8):
                i = 8 * half + hd
                if hd == 0:
                    evac_tokens(w + 8, 2, sv)
                if hd < 7:
                    n = i + 1
                    act.wait_ge(SB["qk"], n + 1)
                    if n:
                        act.wait_ge(SB["lb"], n)
                    act.activation(st[:, :], aux3, ACT.Abs).then_inc(SB["abs"], 1)
                    act.wait_ge(SB["abs"], n + 1)
                    act.activation(st[:, :], st[:, :], ACT.Exp, scale=-1.0).then_inc(SB["exp"], 1)
                    act.wait_ge(SB["exp"], n + 1)
                    act.activation(st[:, :], st[:, :], ACT.Ln, bias=one[:, :]).then_inc(SB["ln"], 1)
                if hd >= 1:
                    y_high(i - 1)
                if hd >= 0:
                    act.wait_ge(SB["sum"], i + 1)
                    if i:
                        act.wait_ge(SB["o"], i)
                    act.activation(sa[:, :], slb[i % 2][:, :], ACT.Exp).then_inc(SB["a"], 1)
                if hd < 7:
                    act.wait_ge(SB["mask"], n + 1)
                    if n:
                        act.wait_ge(SB["cum"], n)
                    act.activation(slh[:, :], slo[:, :], ACT.Copy).then_inc(SB["hi"], 1)
                if hd >= 0:
                    z, sig = zs[:, 0, :], zs[:, 1, :]
                    evac(w + 16 + hd, 0, z)
                    act.wait_ge(evacuated, w + 16 + hd + 1)
                    act.activation(sig, z, ACT.Abs).then_inc(SB["zabs"], 1)
                    act.wait_ge(SB["zabs"], i + 1)
                    act.activation(sig, sig, ACT.Exp, scale=-1.0).then_inc(SB["zexp"], 1)
                    act.wait_ge(SB["zexp"], i + 1)
                    act.activation(sig, sig, ACT.Ln, bias=one[:, :]).then_inc(SB["zln"], 1)
                    act.wait_ge(SB["zlog"], i + 1)
                    act.activation(sig, sig, ACT.Exp).then_inc(SB["zsig"], 1)
            y_high(8 * half + 7)
        norm(5, evacuated, W_END - 8)
        for k in range(KT):
            act.wait_ge(nout_done, KT + k + 1)
            act.dma_start(io["out"][:, k, :], outT[:, k, :]).then_inc(out_stored, 16)
        act.wait_ge(out_stored, 16 * KT)

    @block.vector
    def _(dve):
        def tt(out, a, b, op):
            return dve.tensor_tensor(out, a, b, op)

        def stt(out, a, s, b, op0, op1):
            return dve.scalar_tensor_tensor(out=out, in0=a, scalar=s, in1=b, op0=op0, op1=op1)

        def norm(o, gain, split=None, shift=None, dst=None, out=0):
            dve.wait_ge(ninv_done, o + 1)
            for k in range(KT + 1):
                if split is None:
                    if k < KT:
                        stt(dst[:, k, :], xT[:, k, :], gain[:, k:k + 1], nrs[:, :], ALU.mult, ALU.mult)\
                            .then_inc(nout_done, 1)
                    continue
                if k < KT:
                    if k >= 2:
                        dve.wait_ge(nlo_done, KT * split + k - 1)
                    stt(nxn[:, k % 2, :], xT[:, k, :], gain[:, k:k + 1], nrs[:, :], ALU.mult, ALU.mult)\
                        .then_inc(nxn_done, 1)
                if k:
                    dve.wait_ge(nhi_done, KT * split + k)
                    stt(al[:, k - 1, :], nxn[:, (k - 1) % 2, :], zero[:, 0:1] if shift is None else shift[:, k - 1:k],
                        ah[:, k - 1, :].bitcast(F32), ALU.add, ALU.subtract).then_inc(nlo_done, 1)

        dve.wait_ge(csil_done, 1)

        def modulate(tile, n):
            dve.tensor_tensor_reduce(out=tile, in0=tile, in1=cb[:, :], scale=1.0, scalar=0.0, op0=ALU.mult,
                                     op1=ALU.add, accum_out=ada_sum[:, n:n + 1]).then_inc(ada_used, 1)

        def modulation(a, z, turn):
            dve.wait_ge(ada_used, z)
            tt(ada[:, a:z], ada_sum[:, a:z], VEC["b_ada"][:, a:z], ALU.add).then_inc(ada_done, 1)
            dve.wait_ge(ada_done, turn)

        for n in range(16):
            if n % 2 == 0:
                dve.wait_ge(ada_first_here[n // 2], 16)
            modulate(ada_first[:, n // 2, n % 2, :], n)
        dve.wait_ge(const_pool, NCONST)
        dve.wait_ge(small_here, NSMALL)
        modulation(0, 16, 1)
        stt(gs[:, 0, :], scale1, 1.0, VEC["norm1_g"], ALU.add, ALU.mult).then_inc(const_vec, 1)
        dve.wait_ge(const_vec, 1)
        norm(0, gs[:, 0, :], split=0, shift=shift1)
        for n, window in enumerate(WINDOWS):
            dve.tensor_scalar(inv_count[:, n, :], iota16[:, :], 1.0, float(window), ALU.add, ALU.min).then_inc(const_vec, 1)
        dve.wait_ge(const_vec, 5)
        dve.reciprocal(inv_count[:, :, :], inv_count[:, :, :]).then_inc(const_dve, 1)
        dve.wait_ge(const_dve, 1)

        for n in range(16, NADA):
            k = (n - 16) // 2
            if n % 2 == 0:
                dve.wait_ge(ada_rest_here[k % 3], 16 * (k // 3 + 1))
            modulate(ada_rest[:, k % 3, n % 2, :], n)
        modulation(16, NADA, 2)
        stt(gs[:, 1, :], scale2, 1.0, VEC["norm2_g"], ALU.add, ALU.mult).then_inc(const_vec, 1)

        top = [0]

        def chain(ins):
            top[0] += 1
            ins.then_inc(top_step, 1)
            dve.wait_ge(top_step, top[0])

        for item in SEQ_G:
            kind = item[0]
            if kind == "ckv":
                dve.wait_ge(CKV_ACT.sem, CKV_ACT.at(0, "rstd"))
                for k in range(2):
                    stt(ckv[:, k, :], ckv[:, k, :], VEC["dsa_kv_norm_g"][:, k:k + 1], nrs[:, :], ALU.mult, ALU.mult)\
                        .then_inc(CKV_DVE.sem, 1)
                dve.wait_ge(CKV_PE.sem, CKV_PE.at(0, "iw"))
                dve.tensor_scalar(iwn[:, :, :], aux[3].rearrange("p (t n) -> p t n", t=TT)[:, :, 32:32 + IH],
                                  IH ** -0.5, None, ALU.mult).then_inc(CKV_DVE.sem, 1)
                dve.wait_ge(CKV_DVE.sem, CKV_DVE.at(0, "c1"))
                dve.memset(gat[:, :, :], 0.0).then_inc(const_vec, 1)
                dve.wait_ge(const_vec, 7)
                dve.wait_ge(evacuated, W_G)
            elif kind == "prep":
                h = item[1]
                m = gt1[:, 1, :]
                dve.wait_ge(GLA_PE.sem, GLA_PE.at(h, "gate"))
                dve.wait_ge(GLA_ACT.sem, GLA_ACT.at(h, "abs"))
                dve.tensor_scalar(m, aux[0], VEC["gla_b_gate"][:, h:h + 1], 0.0, ALU.add, ALU.min).then_inc(GLA_DVE.sem, 1)
                dve.wait_ge(GLA_DVE.sem, GLA_DVE.at(h, "min"))
                dve.wait_ge(GLA_ACT.sem, GLA_ACT.at(h, "ln"))
                tt(m, m, gt1[:, 0, :], ALU.subtract).then_inc(GLA_DVE.sem, 1)
                dve.wait_ge(GLA_DVE.sem, GLA_DVE.at(h, "logalpha"))
                dve.tensor_tensor_scan(gb[:, :], chunk_start[:, :], m, 0.0, ALU.mult, ALU.add).then_inc(GLA_DVE.sem, 1)
                dve.wait_ge(GLA_DVE.sem, GLA_DVE.at(h, "cumsum"))
                b3 = gb[:, :].rearrange("p (c t) -> p c t", t=CH)
                tt(gke[:, :].rearrange("p (c t) -> p c t", t=CH), b3[:, :, CH - 1:CH].broadcast_to([P, S // CH, CH]),
                   b3, ALU.subtract).then_inc(GLA_DVE.sem, 1)
                dve.wait_ge(GLA_ACT.sem, GLA_ACT.at(h, "eb"))
                stt(gqd[:, :], qk[:, 2 * h, :], GDK ** -0.5, geb[:, :], ALU.mult, ALU.mult).then_inc(GLA_DVE.sem, 1)
                dve.wait_ge(GLA_ACT.sem, GLA_ACT.at(h, "enb"))
                tt(gki[:, :], gki[:, :], qk[:, 2 * h + 1, :], ALU.mult).then_inc(GLA_DVE.sem, 1)
                dve.wait_ge(GLA_ACT.sem, GLA_ACT.at(h, "ekd"))
                tt(gke[:, :], gke[:, :], qk[:, 2 * h + 1, :], ALU.mult).then_inc(GLA_DVE.sem, 1)
            elif kind == "attn":
                h = item[1]
                dve.wait_ge(GLA_PE.sem, GLA_PE.at(h, "attn"))
                dve.copy_predicated(gat[:, :, :], block_causal[:, :].bitcast(U32).unsqueeze(1).broadcast_to([P, TT, P]),
                                    aux[1].rearrange("p (t n) -> p t n", t=TT)).then_inc(GLA_DVE.sem, 1)
            elif kind == "kv":
                h, t = item[1:]
                dve.wait_ge(GLA_PE.sem, GLA_PE.at(h, f"kv{t}"))
                for c in range(2 * t, min(2 * t + 2, 7)):
                    new = aux[2 - c % 2][:, 0:GDV]
                    if c == 0:
                        dve.tensor_copy(gst[:, 0, :], new).then_inc(GLA_DVE.sem, 1)
                    else:
                        dve.wait_ge(GLA_DVE.sem, GLA_DVE.at(h, f"s{c}"))
                        stt(gst[:, c, :], gst[:, c - 1, :], geb[:, CH * c + CH - 1:CH * c + CH], new,
                            ALU.mult, ALU.add).then_inc(GLA_DVE.sem, 1)
            elif kind == "ms":
                h = item[1]
                dve.wait_ge(GLA_ACT.sem, GLA_ACT.at(h, "rstd"))
                dve.wait_ge(evacuated, W_G + 4 * h + 2)
                for v in range(2):
                    stt(gt1[:, v, :], aux[1 - v], VEC["gla_norm_g"][:, 2 * h + v:2 * h + v + 1], gke[:, :],
                        ALU.mult, ALU.mult).then_inc(GLA_DVE.sem, 1)
                for v in range(2):
                    dve.wait_ge(GLA_DVE.sem, GLA_DVE.at(h, f"og{v}"))
                    tt(gr[:, 2 * h + v, :], gr[:, 2 * h + v, :], gt1[:, v, :], ALU.mult).then_inc(GLA_DVE.sem, 1)
            elif kind == "idx":
                t, h = item[1:]
                i = (t - 1) * IH + h
                n = P * (t + 1)
                dve.wait_ge(idx_relu, i + 1)
                dve.wait_ge(CKV_DVE.sem, CKV_DVE.at(0, "iw"))
                if h == 0:
                    dve.tensor_scalar(score[:, 0:n], rel[:, i % 2, 0:n], iwn[:, t, h:h + 1], None, ALU.mult)\
                        .then_inc(idx_acc, 1)
                else:
                    dve.wait_ge(idx_acc, i)
                    stt(score[:, 0:n], rel[:, i % 2, 0:n], iwn[:, t, h:h + 1], score[:, 0:n], ALU.mult, ALU.add)\
                        .then_inc(idx_acc, 1)
            elif kind == "fill":
                t = item[1]
                dve.wait_ge(idx_acc, t * IH)
                chain(dve.copy_predicated(score[:, P * t:P * t + P], strict[:, :].bitcast(U32), neg[:, :]))
            elif kind == "top":
                n = P * (item[1] + 1)
                chain(dve.max(m8[:, :], score[:, 0:n]))
                chain(dve.match_replace(score[:, 0:n], m8[:, :], score[:, 0:n], TAKEN))
            elif kind == "mask":
                t = item[1]
                n = P * (t + 1)
                if t == 0:
                    chain(dve.memset(maskneg[:, 0, 0:P], 0.0))
                else:
                    chain(dve.tensor_scalar(maskneg[:, t, 0:n], score[:, 0:n], -1e38, NEG, ALU.is_ge, ALU.mult))
                chain(dve.copy_predicated(maskneg[:, t, P * t:P * t + P], strict[:, :].bitcast(U32), neg[:, :]))

        for item in SEQ_D:
            kind = item[0]
            if kind == "ga":
                n = item[1]
                dve.wait_ge(ga_hi, n + 1)
                tt(bl[:, n, :], gr[:, n, :], bh[:, n, :].bitcast(F32), ALU.subtract).then_inc(ga_lo, 1)
            elif kind == "lin":
                w, part = item[1:]
                if w >= W_A and part == PARTS - 1:
                    n = w - W_A
                    if n == 0:
                        dve.wait_ge(evacuated, W_A)
                    dve.wait_ge(tile_done, w + 1)
                    tt(gr[:, n, :], acc[w % 4], gr[:, n, :], ALU.mult).then_inc(evacuated, 1)
            elif kind == "score":
                i = item[1]
                h, t = divmod(i, TT)
                n = P * (t + 1)
                if i:
                    dve.wait_ge(DSA_DVE.sem, DSA_DVE.at(i - 1, "logit"))
                stt(tneg[:, 0:n], relpos[:, 384 - P * t:384 - P * t + n], 2.0 ** -(h + 1), maskneg[:, t, 0:n],
                    ALU.mult, ALU.add).then_inc(DSA_DVE.sem, 1)
                dve.wait_ge(DSA_DVE.sem, DSA_DVE.at(i, "bias"))
                dve.wait_ge(logit_mm, i + 1)
                if i >= 2:
                    dve.wait_ge(probT_mm, i - 1)
                stt(prob[:, i % 2, 0:n], aux[0][:, 0:n], P ** -0.5, tneg[:, 0:n], ALU.mult, ALU.add)\
                    .then_inc(DSA_DVE.sem, 1)
                dve.wait_ge(DSA_DVE.sem, DSA_DVE.at(i, "logit"))
                dve.tensor_reduce(rowstat[:, 0, i:i + 1], prob[:, i % 2, 0:n], AX.X, ALU.max, negate=True)\
                    .then_inc(DSA_DVE.sem, 1)
                dve.wait_ge(prob_exp, i + 1)
                dve.reciprocal(rowstat[:, 2, i:i + 1], rowstat[:, 1, i:i + 1]).then_inc(DSA_DVE.sem, 1)
            elif kind == "pt":
                i = item[1]
                t = i % TT
                dve.wait_ge(probT_mm, i + 1)
                if i >= TT and t == 0:
                    dve.wait_ge(olat_mm, i // TT)
                dve.tensor_copy(pT[:, 0:t + 1, P * t:P * t + P],
                                aux[1][:, 0:P * (t + 1)].rearrange("p (b n) -> p b n", n=P)).then_inc(pT_out, 1)

        for n in range(KT):
            dve.wait_ge(db_hi, n + 1)
            tt(bl[:, n, :], qk[:, n, :], bh[:, n, :].bitcast(F32), ALU.subtract).then_inc(db_lo, 1)
        dve.wait_ge(evacuated, W_B)
        for n in range(KT + 1):
            if n < KT:
                w = W_B + n
                dve.wait_ge(tile_done, w + 1)
                tt(zb[:, n, :], acc[w % 4], zb[:, n, :], ALU.mult).then_inc(evacuated, 1)
                dve.wait_ge(evacuated, w + 1)
                tt(gr[:, n, :], gr[:, n, :], zb[:, n, :], ALU.add).then_inc(y_step, 1)
            if n:
                dve.wait_ge(y_hi, n)
                tt(al[:, n - 1, :], gr[:, n - 1, :], ah[:, n - 1, :].bitcast(F32), ALU.subtract).then_inc(y_lo, 1)
        for n in range(KT):
            w = W_O + n
            dve.wait_ge(tile_done, w + 1)
            stt(xT[:, n, :], acc[w % 4], gate1[:, n:n + 1], xT[:, n, :], ALU.mult, ALU.add).then_inc(evacuated, 1)
        norm(1, gs[:, 1, :], split=1, shift=shift2)

        for h in range(PH):
            n = [NSEL * h]

            def step(ins):
                n[0] += 1
                return ins.then_inc(sel, 1)

            def settle():
                dve.wait_ge(sel, n[0])

            pairs = [(side, t) for side in range(2) for t in range(TT)]
            scores = [psum[:, 4 + 2 * (h % 2) + side, :] for side in range(2)]
            dve.wait_ge(ps_mm, 2 * h + 2)
            for side, t in pairs:
                step(dve.max(topv[:, side, t, 0:8], scores[side][:, P * t:P * t + P]))
            settle()
            for side, t in pairs:
                step(dve.max_index(topi[:, side, t, 0:8], topv[:, side, t, 0:8], scores[side][:, P * t:P * t + P]))
            for side, t in pairs:
                step(dve.match_replace(swork[:, side, t, :], topv[:, side, t, 0:8], scores[side][:, P * t:P * t + P],
                                       TAKEN))
            settle()
            for side, t in pairs:
                step(dve.max(topv[:, side, t, 8:16], swork[:, side, t, :]))
            settle()
            for side, t in pairs:
                step(dve.max_index(topi[:, side, t, 8:16], topv[:, side, t, 8:16], swork[:, side, t, :]))
            grid = [P, TT, PK, PK]
            step(tt(cand[:, :, :].rearrange("p t (a b) -> p t a b", a=PK), topv[:, 0, :, :].unsqueeze(3).broadcast_to(grid),
                    topv[:, 1, :, :].unsqueeze(2).broadcast_to(grid), ALU.add))
            settle()
            step(dve.tensor_copy(topf[:, :, :, :].rearrange("p s t k -> p (s t k)"),
                                 topi[:, :, :, :].rearrange("p s t k -> p (s t k)")))
            for t in range(TT):
                step(dve.max(best[:, t, 0:8], cand[:, t, :]))
            settle()
            for t in range(TT):
                step(dve.max_index(besti[:, t, 0:8], best[:, t, 0:8], cand[:, t, :]))
            settle()
            for t in range(TT):
                step(dve.match_replace(cand[:, t, :], best[:, t, 0:8], cand[:, t, :], TAKEN))
            settle()
            for t in range(TT):
                step(dve.max(best[:, t, 8:16], cand[:, t, :]))
            settle()
            for t in range(TT):
                step(dve.max_index(besti[:, t, 8:16], best[:, t, 8:16], cand[:, t, :]))
            step(tt(bexp[:, :, :], best[:, :, :], best[:, :, 0:1].broadcast_to([P, TT, PK]), ALU.subtract))
            assert n[0] == NSEL * h + SEL_SHIFTED
            settle()
            step(dve.tensor_scalar(bestij[:, 0, :, :], besti[:, :, :], 4, None, ALU.logical_shift_right))
            step(dve.tensor_scalar(bestij[:, 1, :, :], besti[:, :, :], 15, None, ALU.bitwise_and))
            settle()
            step(dve.tensor_copy(bestf[:, :, :, :].rearrange("p s t k -> p (s t k)"),
                                 bestij[:, :, :, :].rearrange("p s t k -> p (s t k)")))
            settle()
            for side in range(2):
                step(tt(onehot[:, :, :], bestf[:, side, :, :].rearrange("p t k -> p (t k)").unsqueeze(2)
                        .broadcast_to([P, TT * PK, PK]), iota16[:, :].unsqueeze(1).broadcast_to([P, TT * PK, PK]),
                        ALU.is_equal))
                settle()
                hot4 = onehot[:, :, :].rearrange("p (t k) j -> p t k j", t=TT)
                step(tt(hot4, hot4, topf[:, side, :, :].unsqueeze(2).broadcast_to(grid), ALU.mult))
                settle()
                step(dve.tensor_reduce(slots[:, side, :, PK * h:PK * h + PK], hot4, AX.X, ALU.add))
                settle()
            dve.wait_ge(sel_exp, h + 1)
            step(dve.tensor_reduce(bsum[:, :], bexp[:, :, :], AX.X, ALU.add))
            settle()
            step(dve.reciprocal(binv[:, :], bsum[:, :]))
            settle()
            step(tt(slots[:, 2, :, PK * h:PK * h + PK], bexp[:, :, :], binv[:, :].unsqueeze(2).broadcast_to([P, TT, PK]),
                    ALU.mult))
            assert n[0] == NSEL * (h + 1)

        for part in range(2):
            dve.wait_ge(sT_mm, part + 1)
            dve.tensor_copy(slotT[:, part, :], aux[part]).then_inc(sT_step, 1)
        dve.wait_ge(sT_mm, 3)
        dve.tensor_copy(gpart[:, 0, :], aux[2]).then_inc(sT_step, 1)
        for part in range(2):
            dve.wait_ge(sT_step, 3 + 2 * part)
            dve.tensor_copy(gp16[:, part, :], gpart[:, part, :]).then_inc(sT_step, 1)
            dve.wait_ge(sT_step, 4 + 2 * part)
            tt(gpart[:, part + 1, :], gpart[:, part, :], gp16[:, part, :], ALU.subtract).then_inc(sT_step, 1)
        dve.wait_ge(sT_step, 7)
        dve.tensor_copy(gp16[:, 2, :], gpart[:, 2, :]).then_inc(sT_step, 1)
        dve.wait_ge(sT_step, 8)

        def one_hots(g, first):
            iota8 = iota_row[:, :].unsqueeze(1).broadcast_to([P, 8, P])
            for b in range(8):
                tok = bass.ds(64 * g + 8 * b, 8)
                if not (first and b < 2):
                    dve.wait_ge(table_mm, 16 * g + 2 * b - 2)
                if not (first and b == 0):
                    dve.wait_ge(HOT.sem, HOT.at(8 * g + b - 1, "gates"))
                tt(hot[:, b % 2, 0, :, :], iota8, slotT[:, 0, tok].unsqueeze(2).broadcast_to([P, 8, P]), ALU.is_equal)\
                    .then_inc(HOT.sem, 1)
                tt(hotb[:, :, :], iota8, slotT[:, 1, tok].unsqueeze(2).broadcast_to([P, 8, P]), ALU.is_equal)\
                    .then_inc(HOT.sem, 1)
                dve.wait_ge(HOT.sem, HOT.at(8 * g + b, "key2"))
                tt(hot[:, b % 2, 1:4, :, :], hotb[:, :, :].unsqueeze(1).broadcast_to([P, 3, 8, P]),
                   gp16[:, :, tok].unsqueeze(3).broadcast_to([P, 3, 8, P]), ALU.mult).then_inc(HOT.sem, 1)
        one_hots(0, True)
        with dve.Fori(1, 8) as g:
            one_hots(g, False)

        with dve.Fori(0, NCHUNK // 2) as g:
            for half in range(2):
                for e in range(ET):
                    i = 2 * ET * g + ET * half + e
                    if e == 0:
                        dve.wait_ge(chunk_here[half], 32 * g + 32)
                    tt(act_m[:, e % 2, :].rearrange("p (g t) -> p g t", t=TG),
                       act_in[:, half, e, :].rearrange("p (g t) -> p g t", t=TG), gt[:, half, :, TG * e:TG * e + TG],
                       ALU.mult).then_inc(e_mul, 1)
                    dve.wait_ge(e_hi, i + 1)
                    dve.wait_ge(tile_done, W_V + i - 3)
                    tt(el[:, e % 4, :], act_m[:, e % 2, :], eh[:, e % 4, :].bitcast(F32), ALU.subtract)\
                        .then_inc(e_lo, 1)
        dve.wait_ge(tile_done, W_POOL)
        for n in range(KT):
            stt(xT[:, n, :], psum[:, (n + 4) % 8, :], gate2[:, n:n + 1], xT[:, n, :], ALU.mult, ALU.add)\
                .then_inc(evacuated, NK // KT)
        dve.wait_ge(evacuated, W_POOL)
        norm(2, VEC["final_norm_g"], dst=xT)
        dve.wait_ge(nout_done, KT)
        norm(3, VEC["norm_g0"], split=2)

        dve.wait_ge(nlo_done, 3 * KT)
        dve.memset(ub[:, :, 0:16], 0.0).then_inc(const_dve, 1)
        dve.memset(us[:, :, 0:16], 0.0).then_inc(const_dve, 1)
        dve.wait_ge(const_dve, 3)
        n_step = 0
        for half in range(2):
            w = W_POOL + 32 * half
            for n in range(8):
                i = 8 * half + n
                which = 2 * half + n // 4
                window = WINDOWS[which]
                u, src, m = ub[:, n % 2, :], ub[:, n % 2, :], um[:, n % 2, :]
                dve.wait_ge(evacuated, w + n + 1)
                for level in range(which + 1):
                    dst = us[:, level % 2, :]
                    tt(dst[:, 16:16 + S], src[:, 16:16 + S], src[:, 16 - 2 ** level:16 + S - 2 ** level], ALU.add)\
                        .then_inc(pl_step, 1)
                    n_step += 1
                    dve.wait_ge(pl_step, n_step)
                    src = dst
                stt(m[:, 16:S], src[:, 32:16 + S], 1.0 / window, u[:, 32:16 + S], ALU.mult, ALU.subtract)\
                    .then_inc(pl_step, 1)
                tt(m[:, 0:16], src[:, 16:32], inv_count[:, which, :], ALU.mult).then_inc(pl_step, 1)
                n_step += 2
                dve.wait_ge(pl_step, n_step)
                tt(m[:, 0:16], m[:, 0:16], u[:, 16:32], ALU.subtract).then_inc(pl_step, 1)
                n_step += 1
                assert n_step == PL_END[i]
                dve.wait_ge(pl_hi, i + 1)
                tt(cl[:, n, :], m, ch[:, n, :].bitcast(F32), ALU.subtract).then_inc(pl_lo, 1)
            dve.wait_ge(evacuated, w + 16)
            for n in range(8):
                m = um[:, n % 2, :]
                dve.wait_ge(tile_done, w + 17 + n)
                stt(m, acc[n % 4], VEC["pool_scale"][:, 8 * half + n:8 * half + n + 1], zs[:, n, :], ALU.mult, ALU.mult)\
                    .then_inc(evacuated, 1)
                dve.wait_ge(pw_hi, 8 * half + n + 1)
                tt(dl[:, n, :], m, dh[:, n, :].bitcast(F32), ALU.subtract).then_inc(pw_lo, 1)
            for n in range(8):
                dve.wait_ge(tile_done, w + 25 + n)
                tt(xT[:, n, :], acc[n % 4], xT[:, n, :], ALU.add).then_inc(evacuated, 1)
        norm(4, VEC["norm_g1"], split=3)

        def y_low(i):
            dve.wait_ge(SB["yhi"], i + 1)
            tt(cl[:, i % 8, :], sy[:, :], ch[:, i % 8, :].bitcast(F32), ALU.subtract).then_inc(SB["ylo"], 1)

        diag = strict[:, :].unsqueeze(1).broadcast_to([P, TT, P])
        for half in range(2):
            w = W_SB + 32 * half
            for hd in range(-1, 8):
                i = 8 * half + hd
                n = i + 1
                if hd >= 0:
                    dve.wait_ge(SB["cum"], i + 1)
                    tt(slb[i % 2][:, :], acc3, slb[i % 2][:, :], ALU.add).then_inc(SB["sum"], 1)
                if hd < 7:
                    dve.wait_ge(SB["ln"], n + 1)
                    if n >= 2:
                        dve.wait_ge(SB["a"], n - 1)
                    stt(slb[n % 2][:, :], aux3, 0.0, st[:, :], ALU.min, ALU.subtract).then_inc(SB["lb"], 1)
                if hd >= 1:
                    y_low(i - 1)
                if hd >= 0:
                    dve.wait_ge(SB["a"], i + 1)
                    square = sa[:, 0:S].rearrange("p (b n) -> p b n", n=P)
                    tt(square, square, diag, ALU.mult).then_inc(SB["amask"], 1)
                if hd < 7:
                    dve.wait_ge(SB["lb"], n + 1)
                    if n:
                        dve.wait_ge(SB["losplit"], n)
                    tt(slo[:, :], slb[n % 2][:, :], aux3, ALU.subtract).then_inc(SB["lo"], 1)
                if hd < 7:
                    dve.wait_ge(SB["lo"], n + 1)
                    square = slo[:, 0:S].rearrange("p (b n) -> p b n", n=P)
                    tt(square, square, diag, ALU.mult).then_inc(SB["mask"], 1)
                    dve.wait_ge(SB["hi"], n + 1)
                    tt(sll[:, :], slo[:, :], slh[:, :].bitcast(F32), ALU.subtract).then_inc(SB["losplit"], 1)
                if hd >= 0:
                    dve.wait_ge(SB["zln"], i + 1)
                    stt(zs[:, 1, :], zs[:, 0, :], 0.0, zs[:, 1, :], ALU.min, ALU.subtract).then_inc(SB["zlog"], 1)
                    dve.wait_ge(SB["zsig"], i + 1)
                    tt(zs[:, 1, :], zs[:, 0, :], zs[:, 1, :], ALU.mult).then_inc(SB["silu"], 1)
                    dve.wait_ge(SB["o"], i + 1)
                    dve.wait_ge(SB["silu"], i + 1)
                    if i:
                        dve.wait_ge(SB["ylo"], i)
                    tt(sy[:, :], aux[3], zs[:, 1, :], ALU.mult).then_inc(SB["y"], 1)
            y_low(8 * half + 7)
            for n in range(8):
                dve.wait_ge(tile_done, w + 25 + n)
                tt(xT[:, n, :], acc[n % 4], xT[:, n, :], ALU.add).then_inc(evacuated, 1)
        norm(5, VEC["norm_f"], dst=outT)

    block_cm.__exit__(None, None, None)


def _tiles(w):
    k, n = w.shape[0] // 128, w.shape[1] // 128
    return w.reshape(k, 128, n, 128).transpose(2, 1, 0, 3).reshape(n, 128, k * 128)


def _token_tiles(w):
    n = w.shape[1] // 512
    return w.reshape(4, 2, 128, n, 512).transpose(3, 0, 2, 1, 4).reshape(4 * n, 128, 1024)


def _columns(v):
    return v.reshape(-1, 128).T


def _layout(i):
    import numpy as np

    cut = np.cumsum((512, 512, 1024, 1024, 16, 1024, 256, 512, 64, 8, 1024))
    gq, gk, gv, gr, glow, dq, dkv, iq, ik, iw, za, zb = np.split(i["w_in"][0], cut, axis=1)
    cat = np.concatenate
    head = lambda w, h, n=128: w[:, n * h:n * h + n]
    w_in = cat([
        _tiles(cat([glow, glow] + [iw] * 12, axis=1)), _tiles(cat([ik, ik], axis=1)), _tiles(dkv),
        _tiles(cat([head(w, h) for h in range(4) for w in (gq, gk)], axis=1)),
        _token_tiles(gv), _tiles(iq),
        *[_tiles(cat([head(gr, h, 256), head(dq, h, 256)], axis=1)) for h in range(4)],
        _tiles(za), _tiles(zb),
    ])
    vec = cat([_columns(v) for v in (
        i["b_ada"][0], i["norm1_g"][0], i["norm2_g"][0], i["final_norm_g"], i["gla_b_gate"][0], i["gla_norm_g"][0],
        i["dsa_kv_norm_g"][0], i["norm_g_2"][0], i["norm_g_2"][1], i["norm_f_2"], i["pool_scale_2"][0])], axis=1)
    xb, z = np.split(i["pool_w_in_2"][0], 2, axis=1)
    pool_in = cat([_tiles(w[:, 1024 * h:1024 * h + 1024]) for h in range(2) for w in (xb, z)])
    pool_w = cat([_tiles(w) for w in i["pool_w_2"][0]])
    halves = lambda w: cat([_tiles(w[1024 * h:1024 * h + 1024]) for h in range(2)])
    q, k, v, z = np.split(i["sb_w_in_2"][0], (1024, 2048, 4096), axis=1)
    sb_in = cat([t for h in range(2) for t in (
        _tiles(q[:, 512 * h:512 * h + 512]), _tiles(k[:, 512 * h:512 * h + 512]),
        _token_tiles(v[:, 1024 * h:1024 * h + 1024]), _tiles(z[:, 1024 * h:1024 * h + 1024]))])
    u = i["peer_u"][0].reshape(128, 128, 8, 128).transpose(1, 3, 2, 0).reshape(128, 128, 1024)
    v = i["peer_v"][0].reshape(128, 128, 1024).transpose(1, 0, 2)
    return {
        "x": i["x"][0].T.reshape(8, 128, 512).transpose(1, 0, 2),
        "c": i["c"],
        "vec": vec,
        "w_ada": i["w_ada"][0].T.reshape(48, 128, 1024),
        "w_in": w_in,
        "gla_w_gate_up": i["gla_w_gate_up"][0],
        "dsa_w_uk": i["dsa_w_uk"][0],
        "dsa_w_uv": i["dsa_w_uv"][0].reshape(8, 2, 128, 128).transpose(0, 2, 1, 3),
        "w_branch_a": _tiles(i["w_branch_a"][0]),
        "w_branch_b": _tiles(i["w_branch_b"][0]),
        "w_out": _tiles(i["w_out"][0]),
        "peer_w_q": _tiles(i["peer_w_q"][0]),
        "peer_sub_keys": np.stack([i["peer_sub_keys_1"][0].T, i["peer_sub_keys_2"][0].T], axis=1),
        "peer_u": u,
        "peer_v": v,
        "pool_w_in": pool_in,
        "pool_w": pool_w,
        "pool_w_out": halves(i["pool_w_out_2"][0]),
        "sb_w_in": sb_in,
        "sb_w_out": halves(i["sb_w_out_2"][0]),
    }


def kernel(**inputs):
    import numpy as _np
    import concourse.bacc as _bacc
    from concourse.bass_utils import run_bass_kernel_spmd as _run

    nc = _bacc.Bacc("TRN2", target_bir_lowering=False, num_devices=1)
    arrays, io = {}, {}
    for name, a in _layout({k: _np.asarray(v) for k, v in inputs.items()}).items():
        a = _np.ascontiguousarray(a)
        arrays[f"in_{name}"] = a
        io[name] = nc.dram_tensor(f"in_{name}", a.shape, mybir.dt.from_np(a.dtype), kind="ExternalInput").ap()
    io["out"] = nc.dram_tensor("out", (128, 8, 512), F32, kind="ExternalOutput").ap()
    build(nc, io)
    r = _run(nc, [arrays], core_ids=[0])
    out = r.results[0]["out"]
    return _np.ascontiguousarray(out.transpose(1, 0, 2).reshape(1024, 512).T)[None]
```
